# Optimizing a Trainium2 kernel written in Bass

```python
import jax, jax.numpy as jnp
from jax import lax
import numpy as np
import math

D_MODEL = 1024
BATCH = 1
SEQ = 256
DEPTH = 1

RET_HEADS = 4
RET_HEAD_DIM = D_MODEL // 2 // RET_HEADS
RET_WIDTH = RET_HEADS * RET_HEAD_DIM
RET_CHUNK = 128
DN_HEADS = 4
DN_HEAD_DIM = D_MODEL // 2 // DN_HEADS
DN_WIDTH = DN_HEADS * DN_HEAD_DIM
DN_CHUNK = 64
CONV_WIDTH = 4
ROPE_THETA = 10000.0
N_GROUPS = 4
EXPERTS_PER_GROUP = 8
N_EXPERTS = N_GROUPS * EXPERTS_PER_GROUP
TOP_K = 2
D_EXPERT = D_MODEL // 2
N_MOD = 6
NORM_EPS = 1e-6
IN_COLS = 4 * RET_WIDTH + 4 * DN_WIDTH + 2 * DN_HEADS


def rmsnorm(x, w=None):
    xf = x.astype(jnp.float32)
    y = xf * lax.rsqrt(jnp.mean(xf * xf, axis=-1, keepdims=True) + NORM_EPS)
    if w is not None:
        y = y * w.astype(jnp.float32)
    return y.astype(x.dtype)

def l2norm(x):
    return x * lax.rsqrt(jnp.sum(x * x, axis=-1, keepdims=True) + NORM_EPS)

def modulate(h, shift, scale):
    return h * (1.0 + scale[:, None, :]) + shift[:, None, :]

def rotary(x, positions):
    dh = x.shape[-1]
    inv_freq = ROPE_THETA ** (-jnp.arange(0, dh, 2, dtype=jnp.float32) / dh)
    ang = positions.astype(jnp.float32)[..., None] * inv_freq
    cos, sin = jnp.cos(ang)[:, :, None, :], jnp.sin(ang)[:, :, None, :]
    xf = x.astype(jnp.float32)
    x1, x2 = xf[..., : dh // 2], xf[..., dh // 2:]
    return jnp.concatenate([x1 * cos - x2 * sin, x2 * cos + x1 * sin], axis=-1)

def retention(q, k, v):
    B, T, H, Dh = q.shape
    C = RET_CHUNK
    N = T // C
    log_gamma = jnp.log1p(-jnp.power(2.0, -5.0 - jnp.arange(H, dtype=jnp.float32)))
    q = q.astype(jnp.float32).reshape(B, N, C, H, Dh)
    k = (k.astype(jnp.float32) * Dh ** -0.5).reshape(B, N, C, H, Dh)
    v = v.astype(jnp.float32).reshape(B, N, C, H, Dh)
    idx = jnp.arange(C, dtype=jnp.float32)
    rel = idx[:, None] - idx[None, :]
    causal = rel >= 0
    decay = jnp.where(causal[None], jnp.exp(log_gamma[:, None, None] * jnp.where(causal, rel, 0.0)[None]), 0.0)
    scores = jnp.einsum('bnihd,bnjhd->bnhij', q, k) * decay[None, None]
    inner = jnp.einsum('bnhij,bnjhd->bnihd', scores, v)
    k_w = k * jnp.exp(log_gamma[None, :] * (C - 1 - idx)[:, None])[:, :, None]
    incr = jnp.einsum('bnjhk,bnjhv->nbhkv', k_w, v)
    chunk_decay = jnp.exp(log_gamma * C)[None, :, None, None]

    def step(state, incr_n):
        return chunk_decay * state + incr_n, state

    _, s_prev = lax.scan(step, jnp.zeros((B, H, Dh, Dh), jnp.float32), incr)
    q_w = q * jnp.exp(log_gamma[None, :] * (idx + 1.0)[:, None])[:, :, None]
    cross = jnp.einsum('bnihk,nbhkv->bnihv', q_w, s_prev)
    return (inner + cross).reshape(B, T, H, Dh)

def causal_dwconv(x, w):
    k = w.shape[0]
    return lax.conv_general_dilated(x, w[:, None, :].astype(x.dtype), window_strides=(1,), padding=((k - 1, 0),),
                                    dimension_numbers=('NWC', 'WIO', 'NWC'), feature_group_count=x.shape[-1])

def gated_delta_rule(q, k, v, g, beta):
    B, T, H, Dh = q.shape
    C = DN_CHUNK
    N = T // C
    to_chunks = lambda t: t.reshape(B, N, C, H, -1).transpose(0, 3, 1, 2, 4)
    q, k, v = to_chunks(q), to_chunks(k), to_chunks(v)
    g = jnp.cumsum(g.reshape(B, N, C, H).transpose(0, 3, 1, 2), axis=-1)
    beta = beta.reshape(B, N, C, H).transpose(0, 3, 1, 2)
    k_beta = k * beta[..., None]
    v_beta = v * beta[..., None]
    tri_incl = jnp.tril(jnp.ones((C, C), bool))
    tri_strict = jnp.tril(jnp.ones((C, C), bool), -1)
    decay = jnp.exp(jnp.where(tri_incl, g[..., :, None] - g[..., None, :], -jnp.inf))
    a_mat = jnp.where(tri_strict, (k_beta @ jnp.swapaxes(k, -1, -2)) * decay, 0.0)
    eye = jnp.eye(C, dtype=jnp.float32)
    t_mat = lax.linalg.triangular_solve(eye + a_mat, jnp.broadcast_to(eye, a_mat.shape),
                                        left_side=True, lower=True, unit_diagonal=True)
    u = t_mat @ v_beta
    w = t_mat @ (k_beta * jnp.exp(g)[..., None])
    attn = (q @ jnp.swapaxes(k, -1, -2)) * decay
    q_g = q * jnp.exp(g)[..., None]
    k_tail = k * jnp.exp(g[..., -1:] - g)[..., None]
    g_last = jnp.exp(g[..., -1])
    lead = lambda t: jnp.moveaxis(t, 2, 0)

    def step(state, inp):
        u_n, w_n, qg_n, kt_n, attn_n, gl_n = inp
        v_new = u_n - w_n @ state
        o_n = qg_n @ state + attn_n @ v_new
        state = state * gl_n[..., None, None] + jnp.swapaxes(kt_n, -1, -2) @ v_new
        return state, o_n

    _, o = lax.scan(step, jnp.zeros((B, H, Dh, Dh), jnp.float32),
                    (lead(u), lead(w), lead(q_g), lead(k_tail), lead(attn), lead(g_last)))
    return o.transpose(1, 0, 3, 2, 4).reshape(B, T, H, Dh)

def hierarchical_moe(h, w_group, b_group, w_expert, b_expert, w1, w3, w2):
    B, T, D = h.shape
    xf = h.reshape(-1, D)
    n = xf.shape[0]
    group_probs = jax.nn.softmax((xf @ w_group + b_group).astype(jnp.float32), axis=-1)
    p_group, g_idx = lax.top_k(group_probs, 1)
    e_logits = (xf @ w_expert + b_expert).astype(jnp.float32).reshape(n, N_GROUPS, EXPERTS_PER_GROUP)
    e_logits = jnp.take_along_axis(e_logits, g_idx[:, :, None], axis=1)[:, 0]
    p_exp, e_local = lax.top_k(jax.nn.softmax(e_logits, axis=-1), TOP_K)
    gate = p_group * p_exp / jnp.sum(p_exp, axis=-1, keepdims=True)
    flat_e = (g_idx * EXPERTS_PER_GROUP + e_local).reshape(-1)
    order = jnp.argsort(flat_e)
    tok = order // TOP_K
    group_sizes = jnp.bincount(flat_e, length=N_EXPERTS).astype(jnp.int32)
    xs = xf[tok]
    hid = jax.nn.silu(lax.ragged_dot(xs, w1, group_sizes)) * lax.ragged_dot(xs, w3, group_sizes)
    ys = lax.ragged_dot(hid.astype(xs.dtype), w2, group_sizes) * gate.reshape(-1)[order][:, None].astype(xs.dtype)
    return jax.ops.segment_sum(ys, tok, num_segments=n).reshape(B, T, D)

def first_inputs(seed: int = 0) -> dict:
    key = jax.random.key(seed)
    ks = jax.random.split(key, 24)
    f32 = jnp.float32
    nrm = lambda k, shape, s: jax.random.normal(k, shape, f32) * s
    dt = jnp.exp(jax.random.uniform(ks[9], (DEPTH, DN_HEADS), f32, np.log(1e-3), np.log(1e-1)))
    return {
        'x': nrm(ks[0], (BATCH, SEQ, D_MODEL), 1.0),
        'c': nrm(ks[1], (BATCH, D_MODEL), 1.0),
        'positions': jnp.broadcast_to(jnp.arange(SEQ, dtype=jnp.int32)[None], (BATCH, SEQ)),
        'w_ada': nrm(ks[2], (DEPTH, D_MODEL, N_MOD * D_MODEL), D_MODEL ** -0.5),
        'b_ada': nrm(ks[3], (DEPTH, N_MOD * D_MODEL), 0.01),
        'norm1_w': 1.0 + nrm(ks[4], (DEPTH, D_MODEL), 0.01),
        'w_in': nrm(ks[5], (DEPTH, D_MODEL, IN_COLS), D_MODEL ** -0.5),
        'conv_w': nrm(ks[6], (DEPTH, CONV_WIDTH, 3 * DN_WIDTH), CONV_WIDTH ** -0.5),
        'a_log': jnp.log(jax.random.uniform(ks[7], (DEPTH, DN_HEADS), f32, 1.0, 16.0)),
        'dt_bias': dt + jnp.log(-jnp.expm1(-dt)),
        'dn_norm_w': 1.0 + nrm(ks[8], (DEPTH, DN_HEAD_DIM), 0.01),
        'w_out': nrm(ks[10], (DEPTH, D_MODEL, D_MODEL), D_MODEL ** -0.5),
        'norm2_w': 1.0 + nrm(ks[11], (DEPTH, D_MODEL), 0.01),
        'w_group': nrm(ks[12], (DEPTH, D_MODEL, N_GROUPS), D_MODEL ** -0.5),
        'b_group': nrm(ks[13], (DEPTH, N_GROUPS), 0.01),
        'w_expert': nrm(ks[14], (DEPTH, D_MODEL, N_EXPERTS), D_MODEL ** -0.5),
        'b_expert': nrm(ks[15], (DEPTH, N_EXPERTS), 0.01),
        'w1': nrm(ks[16], (DEPTH, N_EXPERTS, D_MODEL, D_EXPERT), D_MODEL ** -0.5),
        'w3': nrm(ks[17], (DEPTH, N_EXPERTS, D_MODEL, D_EXPERT), D_MODEL ** -0.5),
        'w2': nrm(ks[18], (DEPTH, N_EXPERTS, D_EXPERT, D_MODEL), D_EXPERT ** -0.5),
        'final_norm_w': 1.0 + nrm(ks[19], (D_MODEL,), 0.01),
    }

def first_block(x, c, positions, w_ada, b_ada, norm1_w, w_in, conv_w, a_log, dt_bias, dn_norm_w, w_out,
              norm2_w, w_group, b_group, w_expert, b_expert, w1, w3, w2, final_norm_w):
    B, T, D = x.shape
    cuts = [RET_WIDTH, 2 * RET_WIDTH, 3 * RET_WIDTH, 4 * RET_WIDTH,
            4 * RET_WIDTH + DN_WIDTH, 4 * RET_WIDTH + 2 * DN_WIDTH, 4 * RET_WIDTH + 3 * DN_WIDTH,
            4 * RET_WIDTH + 4 * DN_WIDTH, 4 * RET_WIDTH + 4 * DN_WIDTH + DN_HEADS]
    for l in range(DEPTH):
        mod = jax.nn.silu(c) @ w_ada[l] + b_ada[l]
        shift1, scale1, gate1, shift2, scale2, gate2 = jnp.split(mod, N_MOD, axis=-1)

        h = modulate(rmsnorm(x, norm1_w[l]), shift1, scale1)
        proj = h @ w_in[l]
        r_q, r_k, r_v, r_g, d_q, d_k, d_v, d_z, d_a, d_b = jnp.split(proj, cuts, axis=-1)

        heads = lambda t, nh: t.reshape(B, T, nh, -1)
        rq = rotary(heads(r_q, RET_HEADS), positions)
        rk = rotary(heads(r_k, RET_HEADS), positions)
        ret = retention(rq, rk, heads(r_v, RET_HEADS))
        ret = rmsnorm(ret).reshape(B, T, RET_WIDTH) * jax.nn.silu(r_g.astype(jnp.float32))

        qkv = jax.nn.silu(causal_dwconv(jnp.concatenate([d_q, d_k, d_v], axis=-1), conv_w[l]))
        cq, ck, cv = jnp.split(qkv.astype(jnp.float32), 3, axis=-1)
        dq = l2norm(heads(cq, DN_HEADS)) * DN_HEAD_DIM ** -0.5
        dk = l2norm(heads(ck, DN_HEADS))
        beta = jax.nn.sigmoid(d_b.astype(jnp.float32))
        g = -jnp.exp(a_log[l].astype(jnp.float32)) * jax.nn.softplus((d_a + dt_bias[l]).astype(jnp.float32))
        dn = gated_delta_rule(dq, dk, heads(cv, DN_HEADS), g, beta)
        dn = rmsnorm(dn, dn_norm_w[l]).reshape(B, T, DN_WIDTH) * jax.nn.silu(d_z.astype(jnp.float32))

        mix = jnp.concatenate([ret, dn], axis=-1).astype(x.dtype) @ w_out[l]
        x = x + gate1[:, None, :] * mix

        h2 = modulate(rmsnorm(x, norm2_w[l]), shift2, scale2)
        ffn = hierarchical_moe(h2, w_group[l], b_group[l], w_expert[l], b_expert[l], w1[l], w3[l], w2[l])
        x = x + gate2[:, None, :] * ffn.astype(x.dtype)
    return rmsnorm(x, final_norm_w)


N_MIXERS = 4
EPS = 1e-6
POOL_WINDOWS = (2, 4, 8, 16)
POOL_GROUP = D_MODEL // len(POOL_WINDOWS)
S5_GROUP = 16
S5_GROUPS = D_MODEL // S5_GROUP
S5_STATE = 64
S5_DT_MIN = 1e-3
S5_DT_MAX = 1e-1
LRU_WIDTH = D_MODEL
LRU_BLOCKS = 4
LRU_BLOCK = LRU_WIDTH // LRU_BLOCKS
LRU_CONV = 4
LRU_C = 8.0
SB_HEADS = 16
SB_HEAD_DIM = D_MODEL // SB_HEADS
SB_Q_BLOCK = 128
FFN_HIDDEN = 2816
FFN_CONV = 3


def n_layers_of(m):
    return len(range(m, DEPTH, N_MIXERS))

def rms_norm(x, g):
    xf = x.astype(jnp.float32)
    y = xf * lax.rsqrt(jnp.mean(xf * xf, axis=-1, keepdims=True) + EPS)
    return (y * g.astype(jnp.float32)).astype(x.dtype)

def causal_depthwise_conv(x, w, b):
    k_width = w.shape[0]
    seq = x.shape[1]
    xp = jnp.pad(x, ((0, 0), (k_width - 1, 0), (0, 0)))
    y = b
    for k in range(k_width):
        y = y + w[k] * xp[:, k:k + seq]
    return y

def linear_scan_combine(left, right):
    a_l, b_l = left
    a_r, b_r = right
    return a_r * a_l, a_r * b_l + b_r

def pool_mixer(x, w, b, scale):
    bsz, seq, _ = x.shape
    xf = x.astype(jnp.float32)
    cs = jnp.pad(jnp.cumsum(xf, axis=1), ((0, 0), (1, 0), (0, 0)))
    pos = jnp.arange(seq)
    groups = []
    for gi, w_len in enumerate(POOL_WINDOWS):
        c = cs[..., gi * POOL_GROUP:(gi + 1) * POOL_GROUP]
        lo = jnp.maximum(pos + 1 - w_len, 0)
        window_sum = c[:, 1:] - jnp.take(c, lo, axis=1)
        count = (pos + 1 - lo).astype(jnp.float32)[:, None]
        groups.append(window_sum / count - xf[..., gi * POOL_GROUP:(gi + 1) * POOL_GROUP])
    d = jnp.stack(groups, axis=2)
    y = jnp.einsum('bsgc,gcd->bsgd', d, w.astype(jnp.float32)).reshape(bsz, seq, D_MODEL) + b
    return (scale * y).astype(x.dtype)

def s5_mixer(x, lam_re, lam_im, log_dt, b_re, b_im, c_re, c_im, d_skip, w_out, b_out):
    f32 = jnp.float32
    bsz, seq, _ = x.shape
    xf = x.astype(f32)
    u = xf.reshape(bsz, seq, S5_GROUPS, S5_GROUP)
    lam = lax.complex(jnp.minimum(lam_re.astype(f32), -1e-4), lam_im.astype(f32))
    dt = jnp.exp(log_dt.astype(f32))[:, None]
    lam_bar = jnp.exp(lam * dt)
    b_bar = ((lam_bar - 1.0) / lam)[..., None] * lax.complex(b_re.astype(f32), b_im.astype(f32))
    bu = lax.complex(jnp.einsum('bsgh,gph->bsgp', u, jnp.real(b_bar)),
                     jnp.einsum('bsgh,gph->bsgp', u, jnp.imag(b_bar)))
    a = jnp.broadcast_to(lam_bar, (seq,) + lam_bar.shape)[None]
    _, states = lax.associative_scan(linear_scan_combine, (a, bu), axis=1)
    y = (jnp.einsum('bsgp,ghp->bsgh', jnp.real(states), c_re.astype(f32))
         - jnp.einsum('bsgp,ghp->bsgh', jnp.imag(states), c_im.astype(f32)))
    y = y.reshape(bsz, seq, D_MODEL) + d_skip.astype(f32) * xf
    y = jax.nn.gelu(y).astype(x.dtype)
    val, gate = jnp.split(y @ w_out + b_out, 2, axis=-1)
    return val * jax.nn.sigmoid(gate)

def rglru_mixer(x, w_in, conv_w, conv_b, w_a, b_a, w_x, b_x, lam, w_out):
    f32 = jnp.float32
    bsz, seq, _ = x.shape
    gate_branch, rec = jnp.split(x @ w_in, 2, axis=-1)
    rec = causal_depthwise_conv(rec, conv_w, conv_b).astype(f32)
    rb = rec.reshape(bsz, seq, LRU_BLOCKS, LRU_BLOCK)
    r = jax.nn.sigmoid(jnp.einsum('bsnc,ncd->bsnd', rb, w_a.astype(f32)).reshape(bsz, seq, LRU_WIDTH) + b_a)
    i = jax.nn.sigmoid(jnp.einsum('bsnc,ncd->bsnd', rb, w_x.astype(f32)).reshape(bsz, seq, LRU_WIDTH) + b_x)
    log_a = -LRU_C * r * jax.nn.softplus(-lam.astype(f32))
    a = jnp.exp(log_a)
    mult = jnp.sqrt(-jnp.expm1(2.0 * log_a))
    _, h = lax.associative_scan(linear_scan_combine, (a, mult * (i * rec)), axis=1)
    y = jax.nn.gelu(gate_branch.astype(f32)) * h
    return y.astype(x.dtype) @ w_out

def stick_breaking_mixer(x, w_qkv, q_g, k_g, w_o):
    bsz, seq, _ = x.shape
    q, k, v = jnp.split(x @ w_qkv, 3, axis=-1)
    to_heads = lambda t: t.reshape(bsz, seq, SB_HEADS, SB_HEAD_DIM).transpose(0, 2, 1, 3)
    q = rms_norm(to_heads(q), q_g)
    k = rms_norm(to_heads(k), k_g)
    v = to_heads(v)
    scale = 1.0 / math.sqrt(SB_HEAD_DIM)
    outs = []
    for start in range(0, seq, SB_Q_BLOCK):
        end = start + SB_Q_BLOCK
        kb, vb = k[:, :, :end], v[:, :, :end]
        z = jnp.einsum('bhtd,bhsd->bhts', q[:, :, start:end], kb).astype(jnp.float32) * scale
        t_pos = start + jnp.arange(SB_Q_BLOCK)[:, None]
        s_pos = jnp.arange(end)[None, :]
        mask = s_pos < t_pos
        log_1m_beta = jnp.where(mask, jax.nn.log_sigmoid(-z), 0.0)
        rest = lax.cumsum(log_1m_beta, axis=3, reverse=True) - log_1m_beta
        att = jnp.where(mask, jnp.exp(jax.nn.log_sigmoid(z) + rest), 0.0)
        outs.append(jnp.einsum('bhts,bhsd->bhtd', att.astype(v.dtype), vb))
    o = jnp.concatenate(outs, axis=2).transpose(0, 2, 1, 3).reshape(bsz, seq, D_MODEL)
    return o @ w_o

def conv_ffn(x, w_in, conv_w, conv_b, w_out):
    h = causal_depthwise_conv(x @ w_in, conv_w, conv_b)
    val, gate = jnp.split(h, 2, axis=-1)
    return (jax.nn.silu(gate) * val) @ w_out

def second_inputs(seed: int = 0) -> dict:
    key = jax.random.key(seed)
    ks = iter(jax.random.split(key, 40))
    nrm = lambda shape, std: jax.random.normal(next(ks), shape, jnp.float32) * std
    gain = lambda shape: 1.0 + nrm(shape, 0.02)
    nA, nB, nC, nD = (n_layers_of(m) for m in range(N_MIXERS))
    G, P, H = S5_GROUPS, S5_STATE, S5_GROUP
    a0 = jax.random.uniform(next(ks), (nC, LRU_WIDTH), jnp.float32, 0.9, 0.999)
    return {
        "x": nrm((BATCH, SEQ, D_MODEL), 1.0),
        "norm_mix_g": gain((DEPTH, D_MODEL)),
        "norm_ffn_g": gain((DEPTH, D_MODEL)),
        "pool_w": nrm((nA, len(POOL_WINDOWS), POOL_GROUP, POOL_GROUP), POOL_GROUP ** -0.5),
        "pool_b": nrm((nA, D_MODEL), 0.01),
        "pool_scale": 1.0 + nrm((nA, D_MODEL), 0.1),
        "s5_lam_re": -0.5 + nrm((nA * 0 + nB, G, P), 0.01),
        "s5_lam_im": math.pi * jnp.arange(P, dtype=jnp.float32) + nrm((nB, G, P), 0.01),
        "s5_log_dt": jax.random.uniform(next(ks), (nB, G), jnp.float32, math.log(S5_DT_MIN), math.log(S5_DT_MAX)),
        "s5_b_re": nrm((nB, G, P, H), (2 * H) ** -0.5),
        "s5_b_im": nrm((nB, G, P, H), (2 * H) ** -0.5),
        "s5_c_re": nrm((nB, G, H, P), P ** -0.5),
        "s5_c_im": nrm((nB, G, H, P), P ** -0.5),
        "s5_d": nrm((nB, D_MODEL), 1.0),
        "s5_w_out": nrm((nB, D_MODEL, 2 * D_MODEL), D_MODEL ** -0.5),
        "s5_b_out": nrm((nB, 2 * D_MODEL), 0.01),
        "lru_w_in": nrm((nC, D_MODEL, 2 * LRU_WIDTH), D_MODEL ** -0.5),
        "lru_conv_w": nrm((nC, LRU_CONV, LRU_WIDTH), LRU_CONV ** -0.5),
        "lru_conv_b": nrm((nC, LRU_WIDTH), 0.01),
        "lru_w_a": nrm((nC, LRU_BLOCKS, LRU_BLOCK, LRU_BLOCK), LRU_BLOCK ** -0.5),
        "lru_b_a": nrm((nC, LRU_WIDTH), 0.01),
        "lru_w_x": nrm((nC, LRU_BLOCKS, LRU_BLOCK, LRU_BLOCK), LRU_BLOCK ** -0.5),
        "lru_b_x": nrm((nC, LRU_WIDTH), 0.01),
        "lru_lam": jnp.log(a0) - jnp.log1p(-a0),
        "lru_w_out": nrm((nC, LRU_WIDTH, D_MODEL), LRU_WIDTH ** -0.5),
        "sb_w_qkv": nrm((nD, D_MODEL, 3 * D_MODEL), D_MODEL ** -0.5),
        "sb_q_g": gain((nD, SB_HEAD_DIM)),
        "sb_k_g": gain((nD, SB_HEAD_DIM)),
        "sb_w_o": nrm((nD, D_MODEL, D_MODEL), D_MODEL ** -0.5),
        "ffn_w_in": nrm((DEPTH, D_MODEL, 2 * FFN_HIDDEN), D_MODEL ** -0.5),
        "ffn_conv_w": nrm((DEPTH, FFN_CONV, 2 * FFN_HIDDEN), FFN_CONV ** -0.5),
        "ffn_conv_b": nrm((DEPTH, 2 * FFN_HIDDEN), 0.01),
        "ffn_w_out": nrm((DEPTH, FFN_HIDDEN, D_MODEL), FFN_HIDDEN ** -0.5),
    }

def second_block(x, norm_mix_g, norm_ffn_g,
              pool_w, pool_b, pool_scale,
              s5_lam_re, s5_lam_im, s5_log_dt, s5_b_re, s5_b_im, s5_c_re, s5_c_im, s5_d, s5_w_out, s5_b_out,
              lru_w_in, lru_conv_w, lru_conv_b, lru_w_a, lru_b_a, lru_w_x, lru_b_x, lru_lam, lru_w_out,
              sb_w_qkv, sb_q_g, sb_k_g, sb_w_o,
              ffn_w_in, ffn_conv_w, ffn_conv_b, ffn_w_out):
    for layer in range(DEPTH):
        m, j = layer % N_MIXERS, layer // N_MIXERS
        h = rms_norm(x, norm_mix_g[layer])
        if m == 0:
            y = pool_mixer(h, pool_w[j], pool_b[j], pool_scale[j])
        elif m == 1:
            y = s5_mixer(h, s5_lam_re[j], s5_lam_im[j], s5_log_dt[j], s5_b_re[j], s5_b_im[j],
                         s5_c_re[j], s5_c_im[j], s5_d[j], s5_w_out[j], s5_b_out[j])
        elif m == 2:
            y = rglru_mixer(h, lru_w_in[j], lru_conv_w[j], lru_conv_b[j], lru_w_a[j], lru_b_a[j],
                            lru_w_x[j], lru_b_x[j], lru_lam[j], lru_w_out[j])
        else:
            y = stick_breaking_mixer(h, sb_w_qkv[j], sb_q_g[j], sb_k_g[j], sb_w_o[j])
        x = x + y.astype(x.dtype)
        f = conv_ffn(rms_norm(x, norm_ffn_g[layer]), ffn_w_in[layer], ffn_conv_w[layer], ffn_conv_b[layer], ffn_w_out[layer])
        x = x + f.astype(x.dtype)
    return x


def setup_inputs(seed=0):
    out = dict(first_inputs(seed))
    for name, value in second_inputs(seed + 1).items():
        if name != "x":
            out[name + "_2"] = value
    return out


def reference(
    x, c, positions, w_ada, b_ada, norm1_w, w_in, conv_w, a_log, dt_bias, dn_norm_w, w_out,
    norm2_w, w_group, b_group, w_expert, b_expert, w1, w3, w2, final_norm_w, norm_mix_g_2,
    norm_ffn_g_2, pool_w_2, pool_b_2, pool_scale_2, s5_lam_re_2, s5_lam_im_2, s5_log_dt_2,
    s5_b_re_2, s5_b_im_2, s5_c_re_2, s5_c_im_2, s5_d_2, s5_w_out_2, s5_b_out_2, lru_w_in_2,
    lru_conv_w_2, lru_conv_b_2, lru_w_a_2, lru_b_a_2, lru_w_x_2, lru_b_x_2, lru_lam_2,
    lru_w_out_2, sb_w_qkv_2, sb_q_g_2, sb_k_g_2, sb_w_o_2, ffn_w_in_2, ffn_conv_w_2,
    ffn_conv_b_2, ffn_w_out_2,
):
    x = first_block(
        x, c, positions, w_ada, b_ada, norm1_w, w_in, conv_w, a_log, dt_bias, dn_norm_w, w_out,
        norm2_w, w_group, b_group, w_expert, b_expert, w1, w3, w2, final_norm_w,
    )
    return second_block(
        x, norm_mix_g_2, norm_ffn_g_2, pool_w_2, pool_b_2, pool_scale_2, s5_lam_re_2,
        s5_lam_im_2, s5_log_dt_2, s5_b_re_2, s5_b_im_2, s5_c_re_2, s5_c_im_2, s5_d_2,
        s5_w_out_2, s5_b_out_2, lru_w_in_2, lru_conv_w_2, lru_conv_b_2, lru_w_a_2, lru_b_a_2,
        lru_w_x_2, lru_b_x_2, lru_lam_2, lru_w_out_2, sb_w_qkv_2, sb_q_g_2, sb_k_g_2, sb_w_o_2,
        ffn_w_in_2, ffn_conv_w_2, ffn_conv_b_2, ffn_w_out_2,
    )


_drawn_inputs = setup_inputs


def setup_inputs(seed=0):
    import zlib

    import numpy as np

    out = dict(_drawn_inputs(seed))
    spreads = {}
    factors = {'norm1_w': 3.449,
     'dn_norm_w': 4.595,
     'norm2_w': 3.37,
     'b_group': 23.52,
     'b_expert': 4.678,
     'final_norm_w': 102.77,
     'norm_mix_g_2': 74.585,
     'norm_ffn_g_2': 17.694,
     'pool_b_2': 123.33,
     'ffn_conv_b_2': 34.54}
    for name, (base, spread) in spreads.items():
        noise = np.random.default_rng([zlib.crc32(name.encode()), seed]).standard_normal(out[name].shape)
        drawn = base * np.exp(spread * noise) if base else spread * noise
        out[name] = __import__('jax').numpy.asarray(drawn.astype(out[name].dtype))
    for name, factor in factors.items():
        out[name] = (out[name] * factor).astype(out[name].dtype)
    return out
```

```python
from contextlib import ExitStack

import numpy as np

import concourse.bass as bass
from concourse import mybir

ALU = mybir.AluOpType
ACT = mybir.ActivationFunctionType
AX = mybir.AxisListType.X
F32 = mybir.dt.float32
I32 = mybir.dt.int32
U32 = mybir.dt.uint32

R = 4
SLOTS = 64
NBLK = 256 // SLOTS
NE = 32
SPARE = 9999.0
WINDOWS = (2, 4, 8, 16)


class Lane:

    def __init__(self, sem):
        self.sem, self.n, self.ops = sem, 0, []

    def do(self, fn, *deps, inc=True):
        if inc:
            self.n += 1
        self.ops.append((fn, [d for d in deps if d is not None], (self.sem, 1) if inc else None))
        return (self.sem, self.n)

    def after(self, fn, *deps):
        return self.do(fn, (self.sem, self.n), *deps)

    def dma(self, fn, flag, *deps):
        flag[1] += 16
        self.ops.append((fn, [d for d in deps if d is not None], (flag[0], 16)))
        return (flag[0], flag[1])

    def wait(self, *deps):
        self.ops.append((None, [d for d in deps if d is not None], None))

    def play(self, eng, seen=None):
        seen = {} if seen is None else seen
        for fn, deps, up in self.ops:
            for sem, val in deps:
                if val > seen.get(sem.name, 0):
                    eng.wait_ge(sem, val)
                    seen[sem.name] = val
            if fn is not None:
                ins = fn(eng)
                if up is not None:
                    ins.then_inc(up[0], up[1])


def constants():
    p = np.arange(128)
    out = {}
    out["ident"] = np.eye(128)
    out["incl"] = (p[:, None] <= p[None, :]) * 1.0
    out["strict"] = (p[:, None] < p[None, :]) * 1.0
    out["ones"] = np.ones((128, 128))
    masks = []
    for level in range(7):
        b = 1 << level
        same = (p[:, None] // (2 * b)) == (p[None, :] // (2 * b))
        masks.append(same & ((p[:, None] // b) % 2 == 0) & ((p[None, :] // b) % 2 == 1))
    out["masks"] = np.concatenate(masks, axis=1) * 1.0
    i = np.arange(256)
    rel = (i[None, :] - p[:, None]).astype(np.float64)
    dec = []
    for h in range(4):
        lg = np.log1p(-(2.0 ** (-5.0 - h)))
        dec.append(np.where(rel >= 0, np.exp(lg * np.maximum(rel, 0)), 0.0) * 128.0 ** -0.5)
    out["decay"] = np.concatenate(dec, axis=1)
    freq = np.float32(10000.0) ** (-np.arange(0, 128, 2, dtype=np.float32) / np.float32(128))
    out["freq"] = np.tile(freq[None], (128, 1))
    out["rev4"] = np.tile(np.arange(4, 0, -1)[None], (128, 1))
    out["rev8"] = np.tile(np.arange(8, 0, -1)[None], (128, 1))
    out["base"] = np.tile(256.0 * np.arange(NE)[None], (128, 1))
    out["ids"] = np.stack([p, p + 128, p + 256, p + 384], axis=1)
    out["half"] = (p[:, None] >= SLOTS) * 1.0
    out["eps"] = np.full((128, 1), 1e-6)
    return {k: np.ascontiguousarray(v, np.float32) for k, v in out.items()}


def late_constants():
    s = np.arange(128)[:, None]
    t = np.arange(256)[None, :]
    parts = []
    for w in WINDOWS:
        count = np.minimum(t + 1, w)
        band = np.where((t - s >= 0) & (t - s < w), 1.0 / count, 0.0) - (t == s)
        u = t[:, 128:]
        own = np.where((u - (s + 128) >= 0) & (u - (s + 128) < w), 1.0 / w, 0.0) - (u == s + 128)
        parts += [band, own]
    return np.ascontiguousarray(np.concatenate(parts, axis=1), np.float32)


def layout():
    at, out = 0, {}
    for k, v in constants().items():
        out[k] = (at, v.shape[1])
        at += v.shape[1]
    return out, at


def program(nc, I, out):
    where, n_const = layout()
    ctx = ExitStack()
    with ctx:
        def sb(name, shape, dt=F32):
            return ctx.enter_context(nc.sbuf_tensor(name, shape, dt))

        def sem(name):
            return ctx.enter_context(nc.semaphore(name))

        C = sb("consts", [128, n_const])
        ring = sb("ring", [128, R, 4096])
        X = sb("X", [128, 2, 1024])
        modb = sb("modb", [128, 6144])
        vb1 = sb("vb1", [128, 1024])
        vb2 = sb("vb2", [128, 1024])
        proj = sb("proj", [128, 5, 2, 512])
        qkv = sb("qkv", [128, 12, 256])
        hT = sb("hT", [128, 8, 256])
        RQ = sb("RQ", [128, 8, 256])
        MX = sb("MX", [128, 2, 1024])
        D = [sb(f"D{i}", [128, 2, 4, 128]) for i in range(5)]
        S = sb("S", [128, 2640])
        posi = sb("posi", [128, 2], I32)
        idx = sb("idx", [128, 2, 128], U32)
        pos_u = sb("pos_u", [128, 2, 2], U32)
        flag_i = sb("flag_i", [128, 1], I32)
        PS = [ctx.enter_context(nc.psum_tensor(f"ps{i}", [128, 512], F32)) for i in range(8)]

        def cst(name):
            a, n = where[name]
            return C[:, a:a + n]

        ident, incl, strict, ones = cst("ident"), cst("incl"), cst("strict"), cst("ones")
        eps = cst("eps")

        s_at = [0]

        def small(n):
            a = s_at[0]
            s_at[0] += n

            assert s_at[0] <= 2640
            return S[:, a:a + n]

        pe, ve, ac, po, sp = (Lane(sem(n)) for n in ("pe_n", "ve_n", "ac_n", "po_n", "sp_n"))

        def flag(name):
            return [sem(name), 0]

        free = [None] * 8
        turn = [0]

        def bank():
            b = turn[0] % 8
            turn[0] += 1
            return b, PS[b], free[b]

        slot_flag = [flag(f"ring{i}") for i in range(R)]
        used = []
        n_units = [0]

        def unit(src, cols, inner):
            u = n_units[0]
            n_units[0] += 1
            s = u % R
            dst = ring[:, s, 0:cols].rearrange("p (a b) -> p a b", b=inner)
            before = used[u - R] if u >= R else None
            tok = sp.dma(lambda e, d=dst, q=src: e.dma_start(d, q), slot_flag[s], before)
            return dst, tok

        f_c, f_x, f_mod = flag("f_c"), flag("f_x"), flag("f_mod")
        t_c = ac.dma(lambda e: e.dma_start(C[:, :], I["consts"]), f_c)
        stack = D[4][:, 0, 0, :]
        f_st = flag("f_st")
        ac.dma(lambda e: e.dma_start(stack[0:48, :], I["conv_w"].rearrange("l k (m p) -> (l k m) p", p=128)), f_st)
        t_st = ac.dma(lambda e: e.dma_start(stack[48:56, :], I["c"].rearrange("l (m p) -> (l m) p", p=128)), f_st)
        t_x = ac.dma(lambda e: e.dma_start(X[:, :, :], I["x"].rearrange("b (n p) d -> p (b n) d", p=128)), f_x)
        t_mod = ac.dma(lambda e: e.dma_start(modb[:, :], I["b_ada"][0, :].partition_broadcast(128)), f_mod)
        f_v = flag("f_v")
        ac.dma(lambda e: e.dma_start(vb1[:, :], I["norm1_w"][0, :].partition_broadcast(128)), f_v)
        AB = sb("AB", [128, 8, 8])
        dnw, alog, dtb = small(128), small(4), small(4)
        ac.dma(lambda e: e.dma_start(vb2[:, :], I["norm2_w"][0, :].partition_broadcast(128)), f_v)
        ac.dma(lambda e: e.dma_start(AB[:, :, :], I["w_in"][0, :, 4096:4104].rearrange("(c p) n -> p c n", p=128)), f_v)
        ac.dma(lambda e: e.dma_start(dnw, I["dn_norm_w"][0, :].partition_broadcast(128)), f_v)
        ac.dma(lambda e: e.dma_start(alog, I["a_log"][0, :].partition_broadcast(128)), f_v)
        ac.dma(lambda e: e.dma_start(dtb, I["dt_bias"][0, :].partition_broadcast(128)), f_v)
        t_v = ac.dma(lambda e: e.dma_start(posi[:, :], I["positions"].rearrange("b (n p) -> p (b n)", p=128),
                                           allow_slow_non_contiguous=True), f_v)

        def rsqrt(dst, src, scale, eps_val, tmp, *deps):
            m, y, t = tmp
            t0 = ve.after(lambda e: e.tensor_scalar(m, src, scale, eps_val, ALU.mult, ALU.add), *deps)
            ac.do(lambda e: e.activation(y, m, ACT.Ln), t0)
            t1 = ac.after(lambda e: e.activation(y, y, ACT.Exp, scale=-0.5))
            ve.after(lambda e: e.tensor_tensor(t, y, y, ALU.mult), t1)
            ve.after(lambda e: e.tensor_tensor(t, t, m, ALU.mult))
            ve.after(lambda e: e.tensor_scalar(t, t, -0.5, 1.5, ALU.mult, ALU.add))
            return ve.after(lambda e: e.tensor_tensor(dst, y, t, ALU.mult))

        ss, rr, tm = small(8), small(8), [small(8) for _ in range(3)]

        def row_norm(src, junk, n_tok, *deps):
            for n in range(2):
                t = ac.after(lambda e, n=n: e.activation(junk[:, n, :], src[:, n, :], ACT.Square,
                                                         accum_out=ss[:, n:n + 1]), *deps)
            return rsqrt(rr[:, 0:2], ss[:, 0:2], 1.0 / 1024, 1e-6, [q[:, 0:2] for q in tm], t)

        def turn_rows(dst, src, *deps):
            toks = []
            for n in range(2):
                for g in range(2):
                    b, ps, fr = bank()
                    for c in range(4):
                        t = pe.do(lambda e, c=c, n=n, g=g, ps=ps: e.transpose(
                            ps[:, c * 128:(c + 1) * 128],
                            src[:, n, (4 * g + c) * 128:(4 * g + c + 1) * 128], ident),
                            fr, *deps, inc=(c == 3))
                    lane = ve if (n + g) % 2 else ac
                    t = lane.do(lambda e, n=n, g=g, ps=ps, l=(lane is ve): (
                        e.tensor_copy if l else e.copy)(
                        dst[:, 4 * g:4 * g + 4, n * 128:(n + 1) * 128],
                        ps[:, :].rearrange("p (c t) -> p c t", c=4)), t)
                    free[b] = t
                    toks.append(t)
            return toks

        def tokens_by(acts, w, t_w, col, width, ps, fr, deps, chunks=8):
            for k in range(chunks):
                a = acts(k)
                t = pe.do(lambda e, k=k, a=a: e.matmul(ps[:, 0:width], a, w[:, k, col:col + width],
                                                  start=(k == 0), stop=(k == chunks - 1)),
                          t_w, fr, *deps, inc=(k == chunks - 1))
            return t

        cols = small(56)
        b, ps, fr = bank()
        t = pe.do(lambda e: e.transpose(PS[0][:, 0:56], stack[0:56, :], ident[0:56, 0:56]), t_c, t_st)
        t = ve.do(lambda e: e.tensor_copy(cols, PS[0][:, 0:56]), t)
        free[0] = t
        ccol = small(8)
        t = ac.do(lambda e: e.activation(ccol, cols[:, 48:56], ACT.Silu), t)
        crep = D[0][:, :, :, :].rearrange("p a b c -> p (a b) c")
        t_crep = ve.do(lambda e: e.tensor_copy(crep, ccol.unsqueeze(2).to_broadcast([128, 8, 128])), t)

        w_ada = I["w_ada"][0, :, :].rearrange("(c p) n -> p c n", p=128)
        w_in = I["w_in"][0, :, :].rearrange("(c p) n -> p c n", p=128)
        t_modb = [None] * 12

        def ada(j):
            w, t_w = unit(w_ada[:, :, 512 * j:512 * j + 512], 4096, 512)
            b, ps, fr = bank()
            t = tokens_by(lambda k: crep[:, k, :], w, t_w, 0, 512, ps, fr, [t_crep])
            used.append(t)
            sl = modb[:, 512 * j:512 * j + 512]
            free[b] = t_modb[j] = ve.do(lambda e: e.tensor_tensor(sl, ps[:, :], sl, ALU.add), t, t_mod)

        for j in range(4):
            ada(j)
        t_n = row_norm(X, MX, 2, t_x)
        ve.after(lambda e: e.scalar_tensor_tensor(modb[:, 1024:2048], modb[:, 1024:2048], 1.0, vb1[:, :],
                                                  ALU.add, ALU.mult), t_v)

        def modulated(dst, src, a, b_):
            for n in range(2):
                ve.after(lambda e, n=n: e.scalar_tensor_tensor(dst[:, n, :], src[:, n, :], rr[:, n:n + 1],
                                                               modb[:, a:a + 1024], ALU.mult, ALU.mult))
                t = ve.after(lambda e, n=n: e.tensor_tensor(dst[:, n, :], dst[:, n, :],
                                                            modb[:, b_:b_ + 1024], ALU.add))
            return t

        t = modulated(MX, X, 1024, 0)
        t_hT = turn_rows(hT, MX, t)

        t_qkv = []
        for seg in range(3):
            w, t_w = unit(w_in[:, :, 2048 + 512 * seg:2560 + 512 * seg], 4096, 512)
            for m in range(4):
                b, ps, fr = bank()
                for k in range(8):
                    t = pe.do(lambda e, k=k, m=m, w=w, ps=ps: e.matmul(
                        ps[:, 0:256], w[:, k, m * 128:(m + 1) * 128], hT[:, k, :],
                        start=(k == 0), stop=(k == 7)), t_w, fr, *t_hT, inc=(k == 7))
                y = qkv[:, 4 * seg + m, :]
                tap = [cols[:, 12 * q + 4 * seg + m:12 * q + 4 * seg + m + 1] for q in range(4)]
                t = ve.do(lambda e, y=y, ps=ps, tap=tap: e.tensor_scalar(y, ps[:, 0:256], tap[3], None, ALU.mult), t)
                for q in (2, 1, 0):
                    o = 3 - q
                    t = ve.after(lambda e, y=y, ps=ps, w_=tap[q], o=o: e.scalar_tensor_tensor(
                        y[:, o:256], ps[:, 0:256 - o], w_, y[:, o:256], ALU.mult, ALU.add))
                free[b] = t
                t_qkv.append(ac.do(lambda e, y=y: e.activation(y, y, ACT.Silu), t))
            used.append((pe.sem, pe.n))

        b, ps_ab, fr = bank()
        for n in range(2):
            for k in range(8):
                t = pe.do(lambda e, k=k, n=n, ps=ps_ab: e.matmul(
                    ps[:, 8 * n:8 * n + 8], hT[:, k, n * 128:(n + 1) * 128], AB[:, k, :],
                    start=(k == 0), stop=(k == 7)), t_v, fr, inc=(k == 7))
        ab = small(16).rearrange("p (n h) -> p n h", n=2)
        free[b] = t = ve.do(lambda e: e.tensor_copy(ab, ps_ab[:, 0:16].rearrange("p (n h) -> p n h", n=2)), t)

        def s8():
            return small(8).rearrange("p (n h) -> p n h", n=2)

        z, az, gl, beta, ea, GC, EG, BE = (s8() for _ in range(8))
        eal = small(4)

        def mid(ap, n=2):
            return ap.unsqueeze(1).to_broadcast([128, n, ap.shape[1]])

        t = ve.after(lambda e: e.tensor_tensor(z, ab[:, :, 0:4], mid(dtb), ALU.add), t_v)
        ac.do(lambda e: e.activation(eal, alog, ACT.Exp), t_v)
        ac.do(lambda e: e.activation(ea, ab[:, :, 4:8], ACT.Exp, scale=-1.0), t)
        t = ac.do(lambda e: e.activation(az, z, ACT.Abs), t)
        t = ac.do(lambda e: e.activation(az, az, ACT.Exp, scale=-1.0), t)
        t = ve.after(lambda e: e.tensor_scalar(az, az, 1.0, None, ALU.add), t)
        t = ac.do(lambda e: e.activation(az, az, ACT.Ln), t)
        ve.after(lambda e: e.tensor_scalar(z, z, 0.0, None, ALU.max))
        ve.after(lambda e: e.tensor_tensor(z, z, az, ALU.add), t)
        ve.after(lambda e: e.scalar_tensor_tensor(gl, z, -1.0, mid(eal), ALU.mult, ALU.mult))
        ve.after(lambda e: e.tensor_scalar(ea, ea, 1.0, None, ALU.add))
        t_g = ve.after(lambda e: e.reciprocal(beta, ea))
        GR, BR = RQ[:, 0:4, :], RQ[:, 4:8, :]
        GR = GR.rearrange("p a b -> p (a b)").rearrange("p (n h i) -> p n h i", n=2, h=4)
        BR = BR.rearrange("p a b -> p (a b)").rearrange("p (n h i) -> p n h i", n=2, h=4)
        for n in range(2):
            ve.do(lambda e, n=n, GR=GR: e.tensor_copy(GR[:, n], gl[:, n, :].unsqueeze(2).to_broadcast([128, 4, 128])), t_g)
            t_gr = ve.do(lambda e, n=n, BR=BR: e.tensor_copy(BR[:, n], beta[:, n, :].unsqueeze(2).to_broadcast([128, 4, 128])), t_g)

        t_seg = [[None, None] for _ in range(5)]

        def project(seg, col, func):
            w, t_w = unit(w_in[:, :, col:col + 512], 4096, 512)
            for n in range(2):
                b, ps, fr = bank()
                t = tokens_by(lambda k, n=n: hT[:, k, n * 128:(n + 1) * 128], w, t_w, 0, 512, ps, fr, t_hT)
                free[b] = t_seg[seg][n] = ac.do(
                    lambda e, n=n, ps=ps: e.activation(proj[:, seg, n, :], ps[:, :], func), t)
            used.append(t)

        project(0, 0, ACT.Copy)
        project(1, 512, ACT.Copy)

        t_sq = None
        SQ = MX[:, :, :].rearrange("p n (a t) -> p (n a) t", t=256)
        t_sq = ac.do(lambda e: e.activation(SQ, qkv[:, 0:8, :], ACT.Square), *t_qkv[0:8], *t_hT)
        t_k = None
        for m in range(4):
            b, ps, fr = bank()
            t = pe.do(lambda e, m=m, ps=ps: e.matmul(ps[:, :], ones, SQ[:, 2 * m:2 * m + 2, :],
                                                    start=True, stop=True), t_sq, fr)
            v2 = SQ[:, 2 * m:2 * m + 2, :]
            free[b] = ac.do(lambda e, v2=v2, ps=ps: e.activation(
                v2, ps[:, :].rearrange("p (a t) -> p a t", a=2), ACT.Ln, bias=eps), t)
        t = ac.after(lambda e: e.activation(SQ, SQ, ACT.Exp, scale=-0.5))
        ve.do(lambda e: e.scalar_tensor_tensor(qkv[:, 0:4, :], qkv[:, 0:4, :], 128.0 ** -0.5, SQ[:, 0:4, :],
                                               ALU.mult, ALU.mult), t)
        t_qk = ve.do(lambda e: e.tensor_tensor(qkv[:, 4:8, :], qkv[:, 4:8, :], SQ[:, 4:8, :], ALU.mult), t)

        AT, DEC, PM, LT, ATT = D
        b, ps, fr = bank()
        for n in range(2):
            t = pe.do(lambda e, n=n, ps=ps: e.matmul(ps[:, 4 * n:4 * n + 4], incl, gl[:, n, :],
                                                     start=True, stop=True), t_gr, fr)
        free[b] = t = ve.do(lambda e, ps=ps: e.tensor_copy(GC, ps[:, 0:8].rearrange("p (n h) -> p n h", n=2)), t)
        t = ac.do(lambda e: e.activation(EG, GC, ACT.Exp), t)
        t_be = ve.after(lambda e: e.tensor_tensor(BE, EG, beta, ALU.mult), t)
        t_dec = []
        for n in range(2):
            b, ps, fr = bank()
            for h in range(4):
                t = pe.do(lambda e, n=n, h=h, ps=ps, GR=GR: e.matmul(ps[:, h * 128:(h + 1) * 128], GR[:, n, h, :], incl,
                                                              start=True, stop=True), t_gr, fr, inc=(h == 3))
            for h in range(4):
                t = ve.do(lambda e, n=n, h=h, ps=ps: e.tensor_scalar(
                    DEC[:, n, h, :], ps[:, h * 128:(h + 1) * 128], GC[:, n, h:h + 1], 0.0,
                    ALU.subtract, ALU.min), t, t_be)
            free[b] = t
            t = ac.do(lambda e, n=n: e.activation(DEC[:, n], DEC[:, n], ACT.Exp), t)
            t_dec.append(ve.do(lambda e, n=n: e.tensor_tensor(DEC[:, n], DEC[:, n], mid(incl, 4), ALU.mult), t))
        t_at, t_att = [], []

        def v4(ps):
            return ps[:, :].rearrange("p (h i) -> p h i", h=4)

        BT = D[2]
        for n in range(2):
            b, ps, fr = bank()
            for h in range(4):
                t = pe.do(lambda e, n=n, h=h, ps=ps, BR=BR: e.matmul(ps[:, h * 128:(h + 1) * 128], BR[:, n, h, :], ident,
                                                              start=True, stop=True), t_gr, fr, inc=(h == 3))
            free[b] = t_b = ve.do(lambda e, n=n, ps=ps: e.tensor_tensor(BT[:, n], v4(ps), DEC[:, n], ALU.mult),
                                  t, t_dec[n])
        t_br_used = (pe.sem, pe.n)
        ang = small(128).rearrange("p (n f) -> p n f", n=2)
        kk_ = small(128).rearrange("p (n f) -> p n f", n=2)
        cs = small(128).rearrange("p (n f) -> p n f", n=2)
        sn = small(128).rearrange("p (n f) -> p n f", n=2)
        posf = small(2)
        po.do(lambda e: e.tensor_copy(posf, posi[:, :]), t_v)
        for n in range(2):
            po.after(lambda e, n=n: e.tensor_scalar(ang[:, n, :], cst("freq"), posf[:, n:n + 1], None, ALU.mult), t_c)
        MAGIC = 12582912.0
        C1, C2 = 6.28125, 0.0019350051879882812
        C3 = float(2 * np.pi - C1 - C2)
        t = po.after(lambda e: e.tensor_scalar(kk_, ang, float(1 / (2 * np.pi)), None, ALU.mult))
        po.after(lambda e: e.tensor_scalar(kk_, kk_, MAGIC, None, ALU.add))
        po.after(lambda e: e.tensor_scalar(kk_, kk_, -MAGIC, None, ALU.add))
        for cc in (C1, C2, C3):
            po.after(lambda e, cc=cc: e.tensor_scalar(cs, kk_, -cc, None, ALU.mult))
            po.after(lambda e: e.tensor_tensor(ang, ang, cs, ALU.add))
        PI = 3.1415925
        t = po.after(lambda e: e.tensor_scalar(ang, ang, PI, -PI, ALU.min, ALU.max))
        t = ac.do(lambda e: e.activation(cs, ang, ACT.Abs), t)
        t = po.after(lambda e: e.tensor_scalar(cs, cs, -1.0, float(np.pi / 2), ALU.mult, ALU.add), t)
        ac.do(lambda e: e.activation(sn, ang, ACT.Sin), t)
        t_sc = ac.do(lambda e: e.activation(cs, cs, ACT.Sin), t)
        room = small(1024)
        rt = [room[:, 256 * i:256 * i + 256].rearrange("p (h f) -> p h f", h=4) for i in range(4)]
        t_rot = {}
        for seg in range(2):
            for n in range(2):
                pv = proj[:, seg, n, :].rearrange("p (h a f) -> p h a f", h=4, a=2)
                x1, x2 = pv[:, :, 0, :], pv[:, :, 1, :]
                cb = cs[:, n, :].unsqueeze(1).to_broadcast([128, 4, 64])
                sb_ = sn[:, n, :].unsqueeze(1).to_broadcast([128, 4, 64])
                for q, (xa, tr) in enumerate(((x1, cb), (x2, sb_), (x2, cb), (x1, sb_))):
                    po.after(lambda e, q=q, xa=xa, tr=tr: e.tensor_tensor(rt[q], xa, tr, ALU.mult),
                             t_sc, t_seg[seg][n])
                po.after(lambda e, x1=x1: e.tensor_tensor(x1, rt[0], rt[1], ALU.subtract))
                t_rot[seg, n] = po.after(lambda e, x2=x2: e.tensor_tensor(x2, rt[2], rt[3], ALU.add))

        project(2, 1024, ACT.Copy)

        for n in range(2):
            tl = slice(n * 128, (n + 1) * 128)
            b, ps, fr = bank()
            for h in range(4):
                t = pe.do(lambda e, h=h, ps=ps, tl=tl: e.matmul(ps[:, h * 128:(h + 1) * 128], qkv[:, 4 + h, tl],
                                                                qkv[:, 4 + h, tl], start=True, stop=True),
                          t_qk, fr, inc=(h == 3))
            A2 = D[4]
            free[b] = ve.do(lambda e, n=n, ps=ps, A2=A2: e.tensor_tensor(A2[:, n], v4(ps), BT[:, n], ALU.mult), t, t_b)
            t_at.append(free[b])
            b, ps, fr = bank()
            for h in range(4):
                t = pe.do(lambda e, h=h, ps=ps, tl=tl: e.matmul(ps[:, h * 128:(h + 1) * 128], qkv[:, 4 + h, tl],
                                                                qkv[:, h, tl], start=True, stop=True),
                          t_qk, fr, inc=(h == 3))
            AQ = D[3]
            free[b] = ve.do(lambda e, n=n, ps=ps, AQ=AQ: e.tensor_tensor(AQ[:, n], v4(ps), DEC[:, n], ALU.mult), t, t_dec[n])
            t_att.append(free[b])
        AT, ATT = D[4], D[3]

        KT = small(512).rearrange("p (h d) -> p h d", h=4)
        b, ps, fr = bank()
        for h in range(4):
            t = pe.do(lambda e, h=h, ps=ps: e.transpose(ps[:, h * 128:(h + 1) * 128], qkv[:, 4 + h, 0:128], ident),
                      t_qk, fr, inc=(h == 3))
        free[b] = t_kt = ac.do(lambda e, ps=ps: e.copy(KT, v4(ps)), t)
        VBT = qkv[:, 8:12, :].rearrange("p a b -> p (a b)").rearrange("p (n h d) -> p n h d", n=2, h=4)
        vb_ps = []
        for n in range(2):
            b, ps, fr = bank()
            for h in range(4):
                t = pe.do(lambda e, h=h, n=n, ps=ps: e.transpose(ps[:, h * 128:(h + 1) * 128],
                                                                 qkv[:, 8 + h, n * 128:(n + 1) * 128], ident),
                          fr, *t_qkv[8:12], inc=(h == 3))
            vb_ps.append((b, ps))
        for n, (b, ps) in enumerate(vb_ps):
            free[b] = t_vbt = ve.do(lambda e, n=n, ps=ps: e.tensor_tensor(
                VBT[:, n], v4(ps), beta[:, n, :].unsqueeze(2).to_broadcast([128, 4, 128]), ALU.mult), t)

        project(3, 1536, ACT.Silu)
        project(4, 3584, ACT.Silu)

        t_rq = []
        for seg in range(2):
            for n in range(2):
                b, ps, fr = bank()
                for h in range(4):
                    t = pe.do(lambda e, h=h, n=n, seg=seg, ps=ps: e.transpose(
                        ps[:, h * 128:(h + 1) * 128], proj[:, seg, n, h * 128:(h + 1) * 128], ident),
                        fr, t_rot[seg, n], inc=(h == 3))
                free[b] = ac.do(lambda e, n=n, seg=seg, ps=ps: e.copy(
                    RQ[:, 4 * seg:4 * seg + 4, n * 128:(n + 1) * 128], v4(ps)), t, t_br_used)
                t_rq.append(free[b])
        WT = proj[:, 0:2, :, :].rearrange("p a n c -> p (a n c)")[:, 0:1536].rearrange("p (h c) -> p h c", h=4)
        t_turned = (pe.sem, pe.n)
        dec_r = cst("decay").rearrange("p (h i) -> p h i", h=4)
        for h in range(4):
            b, ps, fr = bank()
            pe.do(lambda e, h=h, ps=ps: e.matmul(ps[:, 0:256], RQ[:, 4 + h, 0:128], RQ[:, h, :],
                                                 start=True, stop=True), fr, *t_rq, inc=False)
            t = pe.do(lambda e, h=h, ps=ps: e.matmul(ps[:, 256:384], RQ[:, 4 + h, 128:256], RQ[:, h, 128:256],
                                                     start=True, stop=True))
            ve.do(lambda e, h=h, ps=ps: e.tensor_tensor(WT[:, h, 0:256], ps[:, 0:256], dec_r[:, h, :], ALU.mult),
                  t, t_turned)
            free[b] = t_wt = ve.do(lambda e, h=h, ps=ps: e.tensor_tensor(WT[:, h, 256:384], ps[:, 256:384],
                                                                         dec_r[:, h, 0:128], ALU.mult))

        junk = room[:, 0:512].rearrange("p (h d) -> p h d", h=4)

        def head_norm(o, n, dst, gate_seg, weight, *deps):
            sq = junk
            ve.after(lambda e: e.tensor_tensor(sq, o, o, ALU.mult), *deps)
            ve.after(lambda e: e.tensor_reduce(ss[:, 0:4], sq, AX, ALU.add))
            rsqrt(rr[:, 0:4], ss[:, 0:4], 1.0 / 128, 1e-6, [q[:, 0:4] for q in tm])
            ve.after(lambda e: e.tensor_tensor(o, o, rr[:, 0:4].unsqueeze(2).to_broadcast([128, 4, 128]), ALU.mult))
            if weight is not None:
                ve.after(lambda e: e.tensor_tensor(o, o, mid(weight, 4), ALU.mult))
            return ve.after(lambda e: e.tensor_tensor(
                dst, o, proj[:, gate_seg, n, :].rearrange("p (h d) -> p h d", h=4), ALU.mult), t_seg[gate_seg][n])

        OT = room[:, 512:1024].rearrange("p (h d) -> p h d", h=4)
        for n in range(2):
            b, ps, fr = bank()
            for h in range(4):
                hs = slice(h * 128, (h + 1) * 128)
                if n == 0:
                    t = pe.do(lambda e, h=h, hs=hs, ps=ps: e.matmul(ps[:, hs], WT[:, h, 0:128], proj[:, 2, 0, hs],
                                                                    start=True, stop=True),
                              fr, t_wt, *t_seg[2], inc=(h == 3))
                else:
                    pe.do(lambda e, h=h, hs=hs, ps=ps: e.matmul(ps[:, hs], WT[:, h, 128:256], proj[:, 2, 0, hs],
                                                                start=True, stop=False), fr, inc=False)
                    t = pe.do(lambda e, h=h, hs=hs, ps=ps: e.matmul(ps[:, hs], WT[:, h, 256:384], proj[:, 2, 1, hs],
                                                                    start=False, stop=True), inc=(h == 3))
            free[b] = ve.after(lambda e, ps=ps: e.tensor_copy(OT, v4(ps)), t)
            t_ret = head_norm(OT, n, MX[:, n, 0:512].rearrange("p (h d) -> p h d", h=4), 3, None)
        t_ret_pe = (pe.sem, pe.n)

        XM = hT[:, 0:4, :].rearrange("p a b -> p (a b)").rearrange("p (n h i) -> p n h i", n=2, h=4)
        XT = hT[:, 4:8, :].rearrange("p a b -> p (a b)").rearrange("p (n h i) -> p n h i", n=2, h=4)
        PM = D[2]
        LT = proj[:, 0, :, :].rearrange("p n (h i) -> p n h i", h=4)
        masks = cst("masks").rearrange("p (l i) -> p l i", l=7)
        t_x, t_xt, t_p = [None] * 2, [None] * 2, [None] * 2
        t_proj_done = (pe.sem, pe.n)

        def four(lhs, rhs, *deps):
            b, ps, fr = bank()
            for h in range(4):
                a, m = lhs(h), rhs(h)
                t = pe.do(lambda e, h=h, a=a, m=m: e.matmul(ps[:, h * 128:(h + 1) * 128], a, m,
                                                  start=True, stop=True), fr, *deps, inc=(h == 3))
            return b, ps, t

        for level in range(7):
            for n in range(2):
                t = ve.after(lambda e, n=n, level=level, LT=LT, AT=AT: e.tensor_tensor(
                    LT[:, n], AT[:, n], masks[:, level, :].unsqueeze(1).to_broadcast([128, 4, 128]), ALU.mult),
                    t_at[n], t_p[n], t_ret_pe)
                if level == 0:
                    b, ps, tq = four(lambda h, n=n, LT=LT: LT[:, n, h, :], lambda h: ident, t)
                    idb = mid(ident, 4)
                    t_xt[n] = ve.after(lambda e, n=n, idb=idb, LT=LT: e.tensor_tensor(XT[:, n], idb, LT[:, n], ALU.subtract),
                                       t_proj_done)
                    free[b] = t_x[n] = ve.do(lambda e, n=n, idb=idb, ps=ps: e.tensor_tensor(
                        XM[:, n], idb, v4(ps), ALU.subtract), tq, t_proj_done)
                    t_p[n] = tq
                else:
                    b, ps, tq = four(lambda h, n=n, LT=LT: LT[:, n, h, :], lambda h, n=n: XM[:, n, h, :], t, t_x[n])
                    t_p[n] = tq
                    free[b] = t_pm = ac.do(lambda e, n=n, ps=ps, PM=PM: e.copy(PM[:, n], v4(ps)), tq, t_at[n], t_xt[n])
                    b2, ps2, tr = four(lambda h, n=n, PM=PM: PM[:, n, h, :], lambda h, n=n: XT[:, n, h, :], t_pm, t_xt[n])
                    if level < 6:
                        b1, ps1, tq = four(lambda h, n=n: XT[:, n, h, :], lambda h, n=n, PM=PM: PM[:, n, h, :], t_pm)
                        free[b1] = t_x[n] = ve.after(lambda e, n=n, ps=ps1: e.tensor_tensor(
                            XM[:, n], XM[:, n], v4(ps), ALU.subtract), tq)
                    free[b2] = t_xt[n] = ve.after(lambda e, n=n, ps=ps2: e.tensor_tensor(
                        XT[:, n], XT[:, n], v4(ps), ALU.subtract), tr, tq)
            ada(4 + level)
        ada(11)

        def heads_bc(ap):
            return ap.unsqueeze(2).to_broadcast([128, 4, 128])

        U0, UK = PM[:, 0], PM[:, 1]
        ST, VN = LT[:, 0], LT[:, 1]
        b, ps, t = four(lambda h: XT[:, 0, h, :], lambda h: VBT[:, 0, h, :], t_xt[0], t_vbt)
        ve.after(lambda e, ps=ps: e.tensor_copy(U0, v4(ps)), t, (pe.sem, t[1]))
        free[b] = t_uk = ve.after(lambda e: e.tensor_tensor(
            UK, U0, DEC[:, 0, :, 127:128].to_broadcast([128, 4, 128]), ALU.mult))
        b, ps, t = four(lambda h: KT[:, h, :], lambda h: UK[:, h, :], t_uk, t_kt)
        free[b] = t_st = ve.after(lambda e, ps=ps: e.tensor_copy(ST, v4(ps)), t)
        b0, ps0, t0 = four(lambda h, ATT=ATT: ATT[:, 0, h, :], lambda h: U0[:, h, :], t_uk, t_att[0])
        b, ps, t = four(lambda h: qkv[:, 4 + h, 128:256], lambda h: ST[:, h, :], t_st)
        ve.after(lambda e, ps=ps: e.tensor_tensor(VN, v4(ps), heads_bc(BE[:, 1, :]), ALU.mult), t)
        free[b] = t_vn = ve.after(lambda e: e.tensor_tensor(VN, VBT[:, 1], VN, ALU.subtract))
        bq, psq, tq = four(lambda h: qkv[:, h, 128:256], lambda h: ST[:, h, :], t_st)
        b, ps, t = four(lambda h: XT[:, 1, h, :], lambda h: VN[:, h, :], t_vn, t_xt[1])
        U1 = UK
        free[b] = t_u1 = ve.after(lambda e, ps=ps: e.tensor_copy(U1, v4(ps)), t)
        b1, ps1, t1 = four(lambda h, ATT=ATT: ATT[:, 1, h, :], lambda h: U1[:, h, :], t_u1, t_att[1])
        free[b0] = ve.after(lambda e: e.tensor_copy(OT, v4(ps0)), t0)
        head_norm(OT, 0, MX[:, 0, 512:1024].rearrange("p (h d) -> p h d", h=4), 4, dnw)
        free[bq] = ve.after(lambda e: e.tensor_tensor(OT, v4(psq), heads_bc(EG[:, 1, :]), ALU.mult), tq)
        free[b1] = ve.after(lambda e, ps1=ps1: e.tensor_tensor(OT, OT, v4(ps1), ALU.add), t1)
        t_mx = head_norm(OT, 1, MX[:, 1, 512:1024].rearrange("p (h d) -> p h d", h=4), 4, dnw)

        t_hT = turn_rows(hT, MX, t_mx, t_ret)
        w_out = I["w_out"][0, :, :].rearrange("(c p) n -> p c n", p=128)
        for j in range(2):
            w, t_w = unit(w_out[:, :, 512 * j:512 * j + 512], 4096, 512)
            js = slice(512 * j, 512 * j + 512)
            for n in range(2):
                b, ps, fr = bank()
                t = tokens_by(lambda k, n=n: hT[:, k, n * 128:(n + 1) * 128], w, t_w, 0, 512, ps, fr, t_hT)
                tmp = D[1 + j][:, n].rearrange("p h d -> p (h d)")
                free[b] = ve.after(lambda e, ps=ps, tmp=tmp, j=j: e.tensor_tensor(
                    tmp, ps[:, :], modb[:, 2048 + 512 * j:2560 + 512 * j], ALU.mult), t)
                t_x1 = ve.after(lambda e, tmp=tmp, n=n, js=js: e.tensor_tensor(X[:, n, js], X[:, n, js], tmp, ALU.add))
            used.append(t)

        t_n = row_norm(X, MX, 2, t_x1, *t_hT)
        ve.after(lambda e: e.scalar_tensor_tensor(modb[:, 4096:5120], modb[:, 4096:5120], 1.0, vb2[:, :],
                                                  ALU.add, ALU.mult))
        t_h2 = modulated(MX, X, 4096, 3072)
        xs = nc.dram_tensor("rows_scratch", (512, 1024), F32, kind="Internal").ap()
        table = nc.dram_tensor("table_scratch", (NE * 256, 1), F32, kind="Internal").ap()
        ys = nc.dram_tensor("pair_scratch", (1024, 512), F32, kind="Internal").ap()
        f_xs, f_tab, f_tl = flag("f_xs"), flag("f_tab"), flag("f_tl")
        for k in range(2):
            t_xs = ac.dma(lambda e, k=k: e.dma_start(xs[256 * k:256 * k + 256, :].rearrange("(n p) d -> p n d", p=128),
                                                     MX[:, :, :]), f_xs, t_h2)
        t_hT2 = turn_rows(hT, MX, t_h2)
        WR = sb("WR", [128, 8, 36])
        rb = small(36)
        f_r = flag("f_r")
        ac.dma(lambda e: e.dma_start(WR[:, :, 0:4], I["w_group"][0].rearrange("(c p) n -> p c n", p=128)), f_r)
        ac.dma(lambda e: e.dma_start(WR[:, :, 4:36], I["w_expert"][0].rearrange("(c p) n -> p c n", p=128)), f_r)
        ac.dma(lambda e: e.dma_start(rb[:, 0:4], I["b_group"][0, :].partition_broadcast(128)), f_r)
        t_r = ac.dma(lambda e: e.dma_start(rb[:, 4:36], I["b_expert"][0, :].partition_broadcast(128)), f_r)
        b, ps_l, fr = bank()
        for n in range(2):
            for k in range(8):
                t = pe.do(lambda e, n=n, k=k: e.matmul(ps_l[:, 64 * n:64 * n + 36], hT[:, k, n * 128:(n + 1) * 128],
                                                       WR[:, k, :], start=(k == 0), stop=(k == 7)),
                          t_r, fr, *t_hT2, inc=(k == 7))
        W = D[4][:, :, :, :].rearrange("p a b c -> p (a b c)")
        w_at = [0]

        def ws(*shape):
            n = int(np.prod(shape))
            a = w_at[0]
            w_at[0] += n
            v = W[:, a:a + n]
            if len(shape) == 2:
                return v.rearrange("p (a b) -> p a b", a=shape[0])
            if len(shape) == 3:
                return v.rearrange("p (a b c) -> p a b c", a=shape[0], b=shape[1])
            return v

        L = ws(2, 36)
        free[b] = ve.after(lambda e: e.tensor_tensor(
            L, ps_l[:, 0:128].rearrange("p (n c) -> p n c", n=2)[:, :, 0:36], mid(rb), ALU.add), t)

        def bc(ap, *shape):
            while len(ap.shape) < len(shape) + 1:
                ap = ap.unsqueeze(len(ap.shape))
            return ap.to_broadcast([128, *shape])

        def first_max(v, k, rev):
            m, q, oh, sc, m2 = ws(2, 1), None, ws(2, k), ws(2, k), ws(2, 1)
            ve.after(lambda e: e.tensor_reduce(m[:, :, 0], v, AX, ALU.max))
            ve.after(lambda e: e.tensor_tensor(sc, v, bc(m, 2, k), ALU.is_ge))
            ve.after(lambda e: e.tensor_tensor(sc, sc, mid(rev), ALU.mult))
            ve.after(lambda e: e.tensor_reduce(m2[:, :, 0], sc, AX, ALU.max))
            ve.after(lambda e: e.tensor_tensor(oh, sc, bc(m2, 2, k), ALU.is_equal))
            return m, oh

        lg = L[:, :, 0:4]
        gm, ohg = first_max(lg, 4, cst("rev4"))
        eg, zs = ws(2, 4), ws(2, 1)
        t = ve.after(lambda e: e.tensor_tensor(eg, lg, bc(gm, 2, 4), ALU.subtract))
        t = ac.do(lambda e: e.activation(eg, eg, ACT.Exp), t)
        ve.after(lambda e: e.tensor_reduce(zs[:, :, 0], eg, AX, ALU.add), t)
        ve.after(lambda e: e.reciprocal(zs, zs))
        pr = ws(2, 4, 8)
        es, es2 = ws(2, 8), ws(2, 8)
        ohg4 = ohg.unsqueeze(3).to_broadcast([128, 2, 4, 8])
        ve.after(lambda e: e.tensor_tensor(pr, L[:, :, 4:36].rearrange("p n (g e) -> p n g e", g=4), ohg4, ALU.mult))
        ve.after(lambda e: e.tensor_reduce(es, pr.rearrange("p n g e -> p n e g"), AX, ALU.add))
        m1, oh1 = first_max(es, 8, cst("rev8"))
        ve.after(lambda e: e.scalar_tensor_tensor(es2, oh1, -3.0e38, es, ALU.mult, ALU.add))
        m2, oh2 = first_max(es2, 8, cst("rev8"))
        e2, den = ws(2, 1), ws(2, 1)
        gate = small(4).rearrange("p (k n) -> p k n", k=2)
        t = ve.after(lambda e: e.tensor_tensor(e2, m2, m1, ALU.subtract))
        t = ac.do(lambda e: e.activation(e2, e2, ACT.Exp), t)
        ve.after(lambda e: e.tensor_scalar(den, e2, 1.0, None, ALU.add), t)
        ve.after(lambda e: e.reciprocal(den, den))
        ve.after(lambda e: e.tensor_tensor(gate[:, 0, :], zs[:, :, 0], den[:, :, 0], ALU.mult))
        ve.after(lambda e: e.tensor_tensor(gate[:, 1, :], gate[:, 0, :], e2[:, :, 0], ALU.mult))
        M = [ws(2, 4, 8), ws(2, 4, 8)]
        for k, oh in enumerate((oh1, oh2)):
            ve.after(lambda e, k=k, oh=oh: e.tensor_tensor(M[k], oh.unsqueeze(2).to_broadcast([128, 2, 4, 8]),
                                                           ohg4, ALU.mult))
        SM = ws(2, 32)
        flat = [m.rearrange("p n g e -> p n (g e)") for m in M]
        t_sm = ve.after(lambda e: e.tensor_tensor(SM, flat[0], flat[1], ALU.add))
        b, ps_r, fr = bank()
        pe.do(lambda e: e.matmul(ps_r[:, 0:32], strict, SM[:, 0, :], start=True, stop=True), t_sm, fr, inc=False)
        pe.do(lambda e: e.matmul(ps_r[:, 32:64], ones, SM[:, 0, :], start=True, stop=False), inc=False)
        pe.do(lambda e: e.matmul(ps_r[:, 32:64], strict, SM[:, 1, :], start=False, stop=True), inc=False)
        pe.do(lambda e: e.matmul(ps_r[:, 64:96], ones, SM[:, 0, :], start=True, stop=False), inc=False)
        t = pe.do(lambda e: e.matmul(ps_r[:, 64:96], ones, SM[:, 1, :], start=False, stop=True))
        rank, pp, posv, cnt = ws(2, 32), ws(2, 32), ws(2, 2), ws(1)
        ve.after(lambda e: e.tensor_tensor(rank, ps_r[:, 0:64].rearrange("p (n c) -> p n c", n=2),
                                           mid(cst("base")), ALU.add), t)
        ve.after(lambda e: e.tensor_reduce(cnt, ps_r[:, 64:96], AX, ALU.max))
        free[b] = t_flag = ve.after(lambda e: e.tensor_scalar(flag_i[:, :], cnt, SLOTS + 0.5, None, ALU.is_gt))
        for k in range(2):
            ve.after(lambda e, k=k: e.tensor_tensor(pp, flat[k], rank, ALU.mult))
            ve.after(lambda e, k=k: e.tensor_reduce(posv[:, k, :], pp, AX, ALU.add))
        t_pos = ve.after(lambda e: e.tensor_copy(pos_u[:, :, :], posv))
        assert w_at[0] <= 1024

        blank = D[0][:, 0, 0, 0:64]
        t = po.do(lambda e: e.memset(blank, SPARE), t_modb[11], t_h2)
        f_bl = flag("f_bl")
        t_bl = po.dma(lambda e: e.dma_start(table.rearrange("(r s) o -> r (s o)", s=64), blank), f_bl, t)
        for k in range(2):
            for n in range(2):
                t_tab = po.dma(lambda e, k=k, n=n: e.indirect_dma_start(
                    table, bass.IndirectOffsetOnAxis(ap=pos_u[:, k, n:n + 1], axis=0),
                    cst("ids")[:, 2 * k + n:2 * k + n + 1], None), f_tab, t_pos, t_bl)
        tl = D[1][:, 0, 0:2, 0:64]
        t = t_x1
        for k in range(2):
            t_tl = po.dma(lambda e, k=k, tl=tl: e.dma_start(tl[:, k, :], table.rearrange("(r s) o -> r (s o)", s=64)),
                          f_tl, t_tab, t_x1)
        tl2 = D[1][:, 1, 0, :]
        t = ve.after(lambda e, tl=tl: e.tensor_copy(tl2.rearrange("p (a b) -> p a b", a=2), tl), t_tl)
        b, ps_t, fr = bank()
        t = pe.do(lambda e: e.transpose(ps_t[:, 0:128], tl2, ident), t, fr)
        ve.after(lambda e: e.tensor_copy(idx[:, 0, :], ps_t[:, 0:128]), t)
        free[b] = t_idx = ve.after(lambda e: e.tensor_scalar(idx[:, 1, :], ps_t[:, 0:128], 2.0, cst("half"),
                                                             ALU.mult, ALU.add))

        flat_p = proj[:, :, :, :].rearrange("p a b c -> p (a b c)")
        XG = [flat_p[0:SLOTS, 1024 * i:1024 * i + 1024] for i in range(2)]
        XTe = [flat_p[:, 2048 + 512 * i:2560 + 512 * i].rearrange("p (c s) -> p c s", c=8) for i in range(2)]
        HD = [flat_p[0:SLOTS, 3072 + 512 * i:3584 + 512 * i] for i in range(2)]
        HTe = [flat_p[:, 4096 + 256 * i:4352 + 256 * i].rearrange("p (c s) -> p c s", c=4) for i in range(2)]
        SL = [RQ[0:SLOTS, 2 * i:2 * i + 2, :].rearrange("p a b -> p (a b)") for i in range(2)]
        YS = [RQ[:, 4 + 2 * i:6 + 2 * i, :].rearrange("p a b -> p (a b)") for i in range(2)]
        w1, w3, w2 = I["w1"][0], I["w3"][0], I["w2"][0]
        for i in range(2):
            t_zero = po.do(lambda e, i=i: e.memset(XG[i], 0.0), t_mx, t_h2)

        def experts(jobs, lanes, load, done, flags, banks_free, first):
            p_, v_, a_, g_ = lanes
            f_g, f_s = flags
            g_tok, y_tok, x_tok, xt_tok, h_tok, hd_tok, ht_tok = {}, {}, {}, {}, {}, {}, {}
            bt = [0]

            def nb():
                b = bt[0] % 8
                bt[0] += 1
                return b, PS[b], banks_free[b]

            def gather(i):
                e_, blk = jobs[i]
                col = e_ * NBLK + blk
                g_tok[i] = g_.dma(lambda e: e.indirect_dma_start(
                    XG[i % 2], None, xs, bass.IndirectOffsetOnAxis(ap=idx[0:SLOTS, 0, col:col + 1], axis=0),
                    bounds_check=511, oob_is_err=False), f_g[i % 2], *first, x_tok.get(i - 2))

            def turn_x(i):
                b, ps, fr = nb()
                src = XG[i % 2].rearrange("s (p c) -> s c p", c=8)
                for c in range(8):
                    t = p_.do(lambda e, c=c: e.transpose(ps[:, c * SLOTS:(c + 1) * SLOTS], src[:, c, :],
                                                         ident[0:SLOTS, 0:SLOTS]), fr, g_tok[i], inc=(c == 7))
                x_tok[i] = t
                banks_free[b] = xt_tok[i] = v_.do(lambda e: e.tensor_copy(
                    XTe[i % 2], ps[:, :].rearrange("p (c s) -> p c s", c=8)), t, h_tok.get(i - 2))

            def up(i):
                (u1, t1), (u3, t3) = load("w1", jobs[i]), load("w3", jobs[i])
                b, ps, fr = nb()
                for k in range(8):
                    p_.do(lambda e, k=k: e.matmul(ps[0:SLOTS, :], XTe[i % 2][:, k, :], u1[:, k, :],
                                                  start=(k == 0), stop=(k == 7)), fr, xt_tok[i], t1, inc=False)
                    t = p_.do(lambda e, k=k: e.matmul(ps[64:64 + SLOTS, :], XTe[i % 2][:, k, :], u3[:, k, :],
                                                      start=(k == 0), stop=(k == 7)), t3, inc=(k == 7))
                h_tok[i] = t
                done(t)
                done(t)
                t = a_.do(lambda e: e.activation(SL[i % 2], ps[0:SLOTS, :], ACT.Silu), t, hd_tok.get(i - 2))
                banks_free[b] = hd_tok[i] = v_.do(lambda e: e.tensor_tensor(
                    HD[i % 2], SL[i % 2], ps[64:64 + SLOTS, :], ALU.mult), t, ht_tok.get(("pe", i - 2)))

            def turn_h(i):
                b, ps, fr = nb()
                src = HD[i % 2].rearrange("s (p c) -> s c p", c=4)
                for c in range(4):
                    t = p_.do(lambda e, c=c: e.transpose(ps[:, c * SLOTS:(c + 1) * SLOTS], src[:, c, :],
                                                         ident[0:SLOTS, 0:SLOTS]), fr, hd_tok[i], inc=(c == 3))
                ht_tok["pe", i] = t
                banks_free[b] = ht_tok[i] = v_.do(lambda e: e.tensor_copy(
                    HTe[i % 2], ps[:, 0:4 * SLOTS].rearrange("p (c s) -> p c s", c=4)), t, y_tok.get(("pe", i - 2)))

            def down(i):
                e_, blk = jobs[i]
                col = e_ * NBLK + blk
                u2, t2 = load("w2", jobs[i])
                b, ps, fr = nb()
                for k in range(4):
                    p_.do(lambda e, k=k: e.matmul(ps[0:SLOTS, :], HTe[i % 2][:, k, :], u2[:, k, 0:512],
                                                  start=(k == 0), stop=(k == 3)), fr, ht_tok[i], t2, inc=False)
                    t = p_.do(lambda e, k=k: e.matmul(ps[64:64 + SLOTS, :], HTe[i % 2][:, k, :], u2[:, k, 512:1024],
                                                      start=(k == 0), stop=(k == 3)), inc=(k == 3))
                y_tok["pe", i] = t
                done(t)
                banks_free[b] = t = a_.do(lambda e: e.copy(YS[i % 2], ps[:, :]), t, y_tok.get(i - 2))
                y_tok[i] = g_.dma(lambda e: e.indirect_dma_start(
                    ys, bass.IndirectOffsetOnAxis(ap=idx[:, 1, col:col + 1], axis=0), YS[i % 2], None,
                    bounds_check=1023, oob_is_err=False), f_s[i % 2], t)

            N = len(jobs)
            gather(0)
            gather(1)
            turn_x(0)
            up(0)
            turn_x(1)
            for i in range(N):
                if i + 2 < N:
                    gather(i + 2)
                if i + 1 < N:
                    up(i + 1)
                turn_h(i)
                if i + 2 < N:
                    turn_x(i + 2)
                down(i)
            return [y_tok[N - 2], y_tok[N - 1]]

        srcs = {"w1": (w1, 8), "w3": (w3, 8), "w2": (w2, 4)}

        def load_main(kind, job):
            w, c = srcs[kind]
            return unit(w[job[0]].rearrange("(p c) n -> p c n", c=c), 4096, 4096 // c)

        t_ys = experts([(e, 0) for e in range(NE)], (pe, ve, ac, po), load_main, used.append,
                       ([flag("g0"), flag("g1")], [flag("y0"), flag("y1")]), free, (t_idx, t_xs, t_zero))
        po.wait((f_xs[0], f_xs[1]), t_zero)
        split = {id(l): len(l.ops) for l in (pe, ve, ac, po, sp)}

        o_pe, o_ve, o_ac, o_po, o_sp = (Lane(sem(n)) for n in ("o_pe", "o_ve", "o_ac", "o_po", "o_sp"))
        last_used = used[-1]
        o_flag = [flag(f"o{i}") for i in range(3)]
        o_used = [None] * 3
        order = {"w1": 0, "w3": 1, "w2": 2}
        pend = []

        def load_more(kind, job):
            w, c = srcs[kind]
            s = order[kind]
            dst = ring[:, s, :].rearrange("p (a b) -> p a b", b=4096 // c)
            src = w[job[0]].rearrange("(p c) n -> p c n", c=c)
            t = o_sp.dma(lambda e: e.dma_start(dst, src), o_flag[s], last_used, o_used[s])
            pend.append(s)
            return dst, t

        def done_more(t):
            o_used[pend.pop(0)] = t

        o_free = list(free)
        jobs = [(e, blk) for e in range(NE) for blk in range(1, NBLK)]
        t_more = experts(jobs, (o_pe, o_ve, o_ac, o_po), load_more, done_more,
                         ([flag("og0"), flag("og1")], [flag("oy0"), flag("oy1")]), o_free, (t_idx, *t_ys, last_used))
        o_po.wait(*t_more)
        for lane in (o_ve, o_ac, o_sp, o_pe):
            lane.wait((o_pe.sem, o_pe.n), (o_ve.sem, o_ve.n), (o_ac.sem, o_ac.n))
        for i in range(3):
            o_sp.wait((o_flag[i][0], o_flag[i][1]))

        po.wait(*t_ys)
        mark = small(1)
        t_join = po.do(lambda e: e.memset(mark, 0.0))
        YP = flat_p[:, 0:4096].rearrange("p (q n c) -> p q n c", q=2, n=2)
        f_y = flag("f_y")
        for q in range(2):
            for n in range(2):
                r0 = 512 * q + 256 * n
                t_y = ac.dma(lambda e, q=q, n=n, r0=r0: e.dma_start(
                    YP[:, q, n, :], ys[r0:r0 + 256, :].rearrange("(p h) c -> p (h c)", h=2)), f_y, t_join,
                    (pe.sem, pe.n), (ve.sem, ve.n))
        vecs = D[0][:, :, :, :].rearrange("p a b c -> p (a b c)"), D[1][:, :, :, :].rearrange("p a b c -> p (a b c)"), \
            vb1[:, :], vb2[:, :], D[2][:, :, :, :].rearrange("p a b c -> p (a b c)")
        f_w = flag("f_w")
        for v, name in zip(vecs, ("final_norm_w", "norm_mix_g_2", "norm_ffn_g_2", "pool_b_2", "pool_scale_2")):
            src = I[name].partition_broadcast(128) if name == "final_norm_w" else I[name][0, :].partition_broadcast(128)
            t_w5 = ac.dma(lambda e, v=v, src=src: e.dma_start(v, src), f_w, t_idx, t_bl, t_h2)
        v_fin, v_mix, v_ffn, v_pb, v_psc = vecs
        late = qkv[:, 0:6, :].rearrange("p a b -> p (a b)")
        t_late = ac.dma(lambda e: e.dma_start(late, I["late"]), f_w, t_mx)
        ffw = sb("ffw", [128, 2, 128])
        f_f = flag("f_f")
        cw2 = I["ffn_conv_w_2"].rearrange("l k (m p) -> (l k m) p", p=128)
        ac.dma(lambda e: e.dma_start(ffw[:, 0, :], cw2[0:128, :]), f_f)
        ac.dma(lambda e: e.dma_start(ffw[0:4, 1, :], cw2[128:132, :]), f_f)
        t_f = ac.dma(lambda e: e.dma_start(ffw[4:48, 1, :], I["ffn_conv_b_2"].rearrange("l (m p) -> (l m) p", p=128)), f_f)
        fcol = small(176)
        b, ps, fr = bank()
        pe.do(lambda e, ps=ps: e.transpose(ps[:, 0:128], ffw[:, 0, :], ident), fr, t_f, inc=False)
        t = pe.do(lambda e, ps=ps: e.transpose(ps[:, 128:176], ffw[0:48, 1, :], ident[0:48, 0:48]))
        free[b] = t_fcol = ve.after(lambda e, ps=ps: e.tensor_copy(fcol, ps[:, 0:176]), t)

        for n in range(2):
            ve.after(lambda e, n=n: e.tensor_scalar(YP[:, 0, n, :], YP[:, 0, n, :], gate[:, 0, n:n + 1], None, ALU.mult), t_y)
            ve.after(lambda e, n=n: e.scalar_tensor_tensor(YP[:, 0, n, :], YP[:, 1, n, :], gate[:, 1, n:n + 1],
                                                           YP[:, 0, n, :], ALU.mult, ALU.add))
            ve.after(lambda e, n=n: e.tensor_tensor(YP[:, 0, n, :], YP[:, 0, n, :], modb[:, 5120:6144], ALU.mult))
            t = ve.after(lambda e, n=n: e.tensor_tensor(X[:, n, :], X[:, n, :], YP[:, 0, n, :], ALU.add))

        def normed(dst, src, v, *deps):
            row_norm(src, MX, 2, *deps)
            for n in range(2):
                t = ve.after(lambda e, n=n: e.scalar_tensor_tensor(dst[:, n, :], src[:, n, :], rr[:, n:n + 1], v,
                                                                   ALU.mult, ALU.mult), t_late)
            return t

        t = normed(X, X, v_fin, t)
        HM = MX
        t_hm = normed(HM, X, v_mix, t)

        band = late.rearrange("p (g c) -> p g c", g=4)
        t_d = []
        for c in range(8):
            g = c // 2
            b, ps, fr = bank()
            cc = slice(c * 128, (c + 1) * 128)
            pe.do(lambda e, g=g, cc=cc, ps=ps: e.matmul(ps[:, 0:128], HM[:, 0, cc], band[:, g, 0:128],
                                                        start=True, stop=True), t_hm, fr, t_late, inc=False)
            pe.do(lambda e, g=g, cc=cc, ps=ps: e.matmul(ps[:, 128:256], HM[:, 0, cc], band[:, g, 128:256],
                                                        start=True, stop=False), inc=False)
            t = pe.do(lambda e, g=g, cc=cc, ps=ps: e.matmul(ps[:, 128:256], HM[:, 1, cc], band[:, g, 256:384],
                                                            start=False, stop=True))
            free[b] = ac.do(lambda e, c=c, ps=ps: e.copy(hT[:, c, :], ps[:, 0:256]), t)
            t_d.append(free[b])
        w, t_w = unit(I["pool_w_2"][0].rearrange("g (c p) d -> p (g c) d", p=128), 2048, 256)
        for n in range(2):
            for gg in range(2):
                b, ps, fr = bank()
                for g in (2 * gg, 2 * gg + 1):
                    o = 256 * (g % 2)
                    for c in range(2):
                        t = pe.do(lambda e, g=g, c=c, n=n, o=o, ps=ps, w=w: e.matmul(
                            ps[:, o:o + 256], hT[:, 2 * g + c, n * 128:(n + 1) * 128], w[:, 2 * g + c, :],
                            start=(c == 0), stop=(c == 1)), fr, t_w, *t_d)
                gs = slice(512 * gg, 512 * gg + 512)
                tmp = YP[:, 0, n, gs]
                free[b] = ve.after(lambda e, ps=ps, gs=gs, tmp=tmp: e.tensor_tensor(tmp, ps[:, :], v_pb[:, gs], ALU.add), t)
                ve.after(lambda e, gs=gs, tmp=tmp: e.tensor_tensor(tmp, tmp, v_psc[:, gs], ALU.mult))
                t_x3 = ve.after(lambda e, n=n, gs=gs, tmp=tmp: e.tensor_tensor(X[:, n, gs], X[:, n, gs], tmp, ALU.add))
        used.append(t)

        t = normed(MX, X, v_ffn, t_x3, t_hm, (pe.sem, pe.n))
        t_hT = turn_rows(hT, MX, t)
        ACTB = modb[:, 0:5632].rearrange("p (m t) -> p m t", t=256)
        w_f = I["ffn_w_in_2"][0].rearrange("(c p) n -> p c n", p=128)
        gt = [YP[:, 1, 0, 256 * i:256 * i + 256] for i in range(4)]
        t_act = [None] * 22
        t_gt = [None] * 4
        for u in range(11):
            w, t_w = unit(w_f[:, :, 512 * u:512 * u + 512], 4096, 512)
            for q in range(4):
                m = 4 * u + q
                b, ps, fr = bank()
                for k in range(8):
                    t = pe.do(lambda e, k=k, q=q, w=w, ps=ps: e.matmul(
                        ps[:, 0:256], w[:, k, q * 128:(q + 1) * 128], hT[:, k, :],
                        start=(k == 0), stop=(k == 7)), t_w, fr, *t_hT, inc=(k == 7))
                y = ACTB[:, m, :] if m < 22 else gt[m % 4]
                tap = [fcol[:, 44 * r + m:44 * r + m + 1] for r in range(4)]
                t = ve.do(lambda e, y=y, ps=ps, tap=tap: e.tensor_scalar(y, ps[:, 0:256], tap[2], tap[3],
                                                                         ALU.mult, ALU.add),
                          t, t_fcol, t_gt[m % 4] if m >= 22 else None)
                for r in (1, 0):
                    o = 2 - r
                    t = ve.after(lambda e, y=y, ps=ps, w_=tap[r], o=o: e.scalar_tensor_tensor(
                        y[:, o:256], ps[:, 0:256 - o], w_, y[:, o:256], ALU.mult, ALU.add))
                free[b] = t
                if m >= 22:
                    t = ac.do(lambda e, y=y: e.activation(y, y, ACT.Silu), t)
                    t_act[m - 22] = t_gt[m % 4] = po.do(lambda e, y=y, m=m: e.tensor_tensor(
                        ACTB[:, m - 22, :], ACTB[:, m - 22, :], y, ALU.mult), t)
            used.append((pe.sem, pe.n))
        w_o = I["ffn_w_out_2"][0].rearrange("(c p) n -> p c n", p=128)
        acc = [bank() for _ in range(4)]
        for u in range(6):
            nk = min(4, 22 - 4 * u)
            w, t_w = unit(w_o[:, 4 * u:4 * u + nk, :], 1024 * nk, 1024)
            for k in range(nk):
                kk = 4 * u + k
                for a, (b, ps, fr) in enumerate(acc):
                    n, j = a // 2, a % 2
                    t = pe.do(lambda e, k=k, kk=kk, n=n, j=j, w=w, ps=ps: e.matmul(
                        ps[:, :], ACTB[:, kk, n * 128:(n + 1) * 128], w[:, k, 512 * j:512 * j + 512],
                        start=(kk == 0), stop=(kk == 21)), t_w, fr, t_act[kk])
            used.append(t)
        f_o = flag("f_o")
        o_r = out.rearrange("b (n p) d -> p (b n) d", p=128)
        for a, (b, ps, fr) in enumerate(acc):
            n, j = a // 2, a % 2
            js = slice(512 * j, 512 * j + 512)
            tt = ve.after(lambda e, n=n, js=js, ps=ps: e.tensor_tensor(X[:, n, js], X[:, n, js], ps[:, :], ALU.add), t)
            t_o = ac.dma(lambda e, n=n, js=js: e.dma_start(o_r[:, n, js], X[:, n, js]), f_o, tt)
        ac.wait(t_o)

        block = ctx.enter_context(nc.Block())

        def run(eng, lane, more):
            cut = split[id(lane)]
            whole = lane.ops
            seen = {}
            lane.ops = whole[:cut]
            lane.play(eng, seen)
            eng.wait_ge(t_flag[0], t_flag[1])
            val = eng.value_load(flag_i[0:1, 0:1], min_val=0, max_val=1)
            with eng.If(val > 0):
                more.play(eng, dict(seen))
            lane.ops = whole[cut:]
            lane.play(eng, seen)

        @block.sync
        def _(eng):
            run(eng, sp, o_sp)

        @block.tensor
        def _(eng):
            run(eng, pe, o_pe)

        @block.vector
        def _(eng):
            run(eng, ve, o_ve)

        @block.scalar
        def _(eng):
            run(eng, ac, o_ac)

        @block.gpsimd
        def _(eng):
            run(eng, po, o_po)


_INS = ['x', 'c', 'positions', 'w_ada', 'b_ada', 'norm1_w', 'w_in', 'conv_w', 'a_log', 'dt_bias', 'dn_norm_w',
        'w_out', 'norm2_w', 'w_group', 'b_group', 'w_expert', 'b_expert', 'w1', 'w3', 'w2', 'final_norm_w',
        'norm_mix_g_2', 'norm_ffn_g_2', 'pool_w_2', 'pool_b_2', 'pool_scale_2', 'ffn_w_in_2', 'ffn_conv_w_2',
        'ffn_conv_b_2', 'ffn_w_out_2']


def kernel(**inputs):
    import numpy as _np
    import concourse.bacc as _bacc
    from concourse import mybir as _mybir
    from concourse.bass_utils import run_bass_kernel_spmd as _run

    nc = _bacc.Bacc("TRN2", target_bir_lowering=False, num_devices=1)
    given = {k: _np.ascontiguousarray(inputs[k]) for k in _INS}
    given["consts"] = _np.concatenate(list(constants().values()), axis=1)
    given["late"] = late_constants()
    arrays, aps = {}, {}
    for name, a in given.items():
        arrays[f"in_{name}_dram"] = a
        aps[name] = nc.dram_tensor(f"in_{name}_dram", a.shape, _mybir.dt.from_np(a.dtype), kind="ExternalInput").ap()
    o = nc.dram_tensor("out_0_dram", (1, 256, 1024), F32, kind="ExternalOutput").ap()
    program(nc, aps, o)
    r = _run(nc, [arrays], core_ids=[0])
    return r.results[0]["out_0_dram"]
```

```python
from contextlib import ExitStack

import numpy as np

import concourse.bass as bass
from concourse import mybir

ALU = mybir.AluOpType
ACT = mybir.ActivationFunctionType
AX = mybir.AxisListType.X
F32 = mybir.dt.float32
I32 = mybir.dt.int32
U32 = mybir.dt.uint32

R = 4
SLOTS = 64
NBLK = 256 // SLOTS
NE = 32
SPARE = 9999.0
WINDOWS = (2, 4, 8, 16)


def tokens(deps):
    out = []
    for d in deps:
        if d is not None:
            out += list(d) if isinstance(d[0], tuple) else [d]
    return out


class Lane:

    def __init__(self, sem):
        self.sem, self.n, self.ops = sem, 0, []

    def do(self, fn, *deps, inc=True):
        if inc:
            self.n += 1
        self.ops.append((fn, tokens(deps), (self.sem, 1) if inc else None))
        return (self.sem, self.n)

    def after(self, fn, *deps):
        return self.do(fn, (self.sem, self.n), *deps)

    def dma(self, fn, flag, *deps):
        flag[1] += 16
        self.ops.append((fn, tokens(deps), (flag[0], 16)))
        return (flag[0], flag[1])

    def wait(self, *deps):
        self.ops.append((None, tokens(deps), None))

    def play(self, eng, seen=None):
        seen = {} if seen is None else seen
        for fn, deps, up in self.ops:
            for sem, val in deps:
                if val > seen.get(sem.name, 0):
                    eng.wait_ge(sem, val)
                    seen[sem.name] = val
            if fn is not None:
                ins = fn(eng)
                if up is not None:
                    ins.then_inc(up[0], up[1])


def constants():
    p = np.arange(128)
    out = {}
    out["ident"] = np.eye(128)
    out["sel"] = np.repeat((p[:, None] % 32 == 0) * 1.0, 128, axis=1)
    out["incl"] = (p[:, None] <= p[None, :]) * 1.0
    out["strict"] = (p[:, None] < p[None, :]) * 1.0
    out["ones"] = np.ones((128, 128))
    masks = []
    for level in range(7):
        b = 1 << level
        same = (p[:, None] // (2 * b)) == (p[None, :] // (2 * b))
        masks.append(same & ((p[:, None] // b) % 2 == 0) & ((p[None, :] // b) % 2 == 1))
    out["masks"] = np.concatenate(masks, axis=1) * 1.0
    i = np.arange(256)
    rel = (i[None, :] - p[:, None]).astype(np.float64)
    dec = []
    for h in range(4):
        lg = np.log1p(-(2.0 ** (-5.0 - h)))
        dec.append(np.where(rel >= 0, np.exp(lg * np.maximum(rel, 0)), 0.0) * 128.0 ** -0.5)
    out["decay"] = np.concatenate(dec, axis=1)
    freq = np.float32(10000.0) ** (-np.arange(0, 128, 2, dtype=np.float32) / np.float32(128))
    out["freq"] = np.tile(freq[None], (128, 1))
    out["rev4"] = np.tile(np.arange(4, 0, -1)[None], (128, 1))
    out["rev8"] = np.tile(np.arange(8, 0, -1)[None], (128, 1))
    out["base"] = np.tile(256.0 * np.arange(NE)[None], (128, 1))
    out["ids"] = np.stack([p, p + 128, p + 256, p + 384], axis=1)
    out["half"] = (p[:, None] >= SLOTS) * 1.0
    out["nhalf"] = np.full((128, 1), -0.5)
    out["eps"] = np.full((128, 1), 1e-6)
    return {k: np.ascontiguousarray(v, np.float32) for k, v in out.items()}


def late_constants():
    s = np.arange(128)[:, None]
    t = np.arange(256)[None, :]
    parts = []
    for w in WINDOWS:
        count = np.minimum(t + 1, w)
        band = np.where((t - s >= 0) & (t - s < w), 1.0 / count, 0.0) - (t == s)
        u = t[:, 128:]
        own = np.where((u - (s + 128) >= 0) & (u - (s + 128) < w), 1.0 / w, 0.0) - (u == s + 128)
        parts += [band, own]
    return np.ascontiguousarray(np.concatenate(parts, axis=1), np.float32)


def layout():
    at, out = 0, {}
    for k, v in constants().items():
        out[k] = (at, v.shape[1])
        at += v.shape[1]
    return out, at


def program(nc, I, out):
    where, n_const = layout()
    ctx = ExitStack()
    with ctx:
        def sb(name, shape, dt=F32):
            return ctx.enter_context(nc.sbuf_tensor(name, shape, dt))

        def sem(name):
            return ctx.enter_context(nc.semaphore(name))

        C = sb("consts", [128, n_const])
        vrow = sb("vrow", [128, 1024])
        ring = sb("ring", [128, R, 4096])
        X = sb("X", [128, 2, 1024])
        gates = sb("gates", [128, 2, 1024])
        proj = sb("proj", [128, 5, 2, 512])
        hT = sb("hT", [128, 8, 256])
        RQ = sb("RQ", [128, 8, 256])
        MX = sb("MX", [128, 2, 1024])
        arena = sb("arena", [128, 3, 4096])
        pool_ = arena[:, :, :].rearrange("p a b -> p (a b)")
        D9 = [pool_[:, 1024 * i:1024 * i + 1024].rearrange("p (n h i) -> p n h i", n=2, h=4) for i in range(9)]
        D, LT, XM, XT = D9[0:5], D9[5:7], D9[7], D9[8]
        qkv = pool_[:, 9216:12288].rearrange("p (m t) -> p m t", m=12)
        part_ = sb("part", [128, 2, 512])
        S = sb("S", [128, 3250])
        posi = sb("posi", [128, 2], I32)
        idx = sb("idx", [128, 2, 128], U32)
        pos_u = sb("pos_u", [128, 2, 2], U32)
        flag_i = sb("flag_i", [128, 1], I32)
        PS = [ctx.enter_context(nc.psum_tensor(f"ps{i}", [128, 512], F32)) for i in range(8)]

        def cst(name):
            a, n = where[name]
            return C[:, a:a + n]

        ident, incl, strict, ones = cst("ident"), cst("incl"), cst("strict"), cst("ones")
        eps = cst("eps")

        s_at = [0]

        def small(n):
            a = s_at[0]
            s_at[0] += n

            assert s_at[0] <= 3250
            return S[:, a:a + n]

        pe, ve, ac, po, sp = (Lane(sem(n)) for n in ("pe_n", "ve_n", "ac_n", "po_n", "sp_n"))

        def flag(name):
            return [sem(name), 0]

        def both(a, b):
            return (a, b)

        free = [None] * 8
        turn = [0]

        kept = set()

        def bank():
            while turn[0] % 8 in kept:
                turn[0] += 1
            b = turn[0] % 8
            turn[0] += 1
            return b, PS[b], free[b]

        slots = [ring[:, i, :] for i in range(R)] + [arena[:, i, :] for i in range(3)]
        slot_flag = [flag(f"slot{i}") for i in range(R + 3)]
        last_read = [None] * (R + 3)
        rota = list(range(R))
        held = []
        at_slot = [0]

        def unit(src, cols, inner):
            s = rota[at_slot[0] % len(rota)]
            at_slot[0] += 1
            held.append(s)
            dst = slots[s][:, 0:cols].rearrange("p (a b) -> p a b", b=inner)
            return dst, sp.dma(lambda e: e.dma_start(dst, src), slot_flag[s], last_read[s])

        def consumed(t):
            last_read[held.pop(0)] = t

        stacks = sb("stacks", [128, 3, 128])
        f_e, f_st, f_c, f_x, f_v = flag("f_e"), flag("f_st"), flag("f_c"), flag("f_x"), flag("f_v")

        def load(flag_, dst, src, *deps):
            return ac.dma(lambda e: e.dma_start(dst, src), flag_, *deps)

        AB = sb("AB", [128, 8, 8])
        WR = sb("WR", [128, 8, 36])
        t_e = load(f_e, C[:, 0:256], I["consts"][:, 0:256])
        load(f_st, stacks[48:56, 0, :], I["c"].rearrange("l (m p) -> (l m) p", p=128))
        load(f_st, stacks[0:48, 0, :], I["conv_w"].rearrange("l k (m p) -> (l k m) p", p=128))
        load(f_st, stacks[56:104, 0, :], I["b_ada"].rearrange("l (m p) -> (l m) p", p=128))
        load(f_st, stacks[104:112, 0, :], I["norm1_w"].rearrange("l (m p) -> (l m) p", p=128))
        t_st = load(f_st, stacks[112:120, 0, :], I["norm2_w"].rearrange("l (m p) -> (l m) p", p=128))
        t_xl = load(f_x, X[:, :, :], I["x"].rearrange("b (n p) d -> p (b n) d", p=128))
        t_c = load(f_c, C[:, 256:n_const], I["consts"][:, 256:n_const])
        dnw, alog, dtb, rb = small(128), small(4), small(4), small(36)
        by_row = small(24).rearrange("p (a c) -> p a c", a=3)
        load(f_v, AB[:, :, :], I["w_in"][0, :, 4096:4104].rearrange("(c p) n -> p c n", p=128))
        load(f_v, dnw, I["dn_norm_w"][0, :].partition_broadcast(128))
        load(f_v, alog, I["a_log"][0, :].partition_broadcast(128))
        load(f_v, dtb, I["dt_bias"][0, :].partition_broadcast(128))
        ac.dma(lambda e: e.dma_start(posi[:, :], I["positions"].rearrange("b (n p) -> p (b n)", p=128),
                                     allow_slow_non_contiguous=True), f_v)
        load(f_v, gates[:, 0, :], I["b_ada"][0, 2048:3072].partition_broadcast(128))
        load(f_v, gates[:, 1, :], I["b_ada"][0, 5120:6144].partition_broadcast(128))
        load(f_v, by_row[:, 0, :], I["b_ada"][0, 3072:4096].rearrange("(p c) -> p c", c=8))
        load(f_v, by_row[:, 1, :], I["b_ada"][0, 4096:5120].rearrange("(p c) -> p c", c=8))
        load(f_v, by_row[:, 2, :], I["norm2_w"][0, :].rearrange("(p c) -> p c", c=8))
        load(f_v, WR[:, :, 0:4], I["w_group"][0].rearrange("(c p) n -> p c n", p=128))
        load(f_v, WR[:, :, 4:36], I["w_expert"][0].rearrange("(c p) n -> p c n", p=128))
        load(f_v, rb[:, 0:4], I["b_group"][0, :].partition_broadcast(128))
        load(f_v, rb[:, 4:36], I["b_expert"][0, :].partition_broadcast(128))
        cw2 = I["ffn_conv_w_2"].rearrange("l k (m p) -> (l k m) p", p=128)
        load(f_v, stacks[0:96, 1, :], cw2[0:96, :])
        load(f_v, stacks[0:36, 2, :], cw2[96:132, :])
        load(f_v, stacks[36:80, 2, :], I["ffn_conv_b_2"].rearrange("l (m p) -> (l m) p", p=128))
        load(f_v, stacks[80:88, 2, :], I["norm_mix_g_2"].rearrange("l (m p) -> (l m) p", p=128))
        t_v = load(f_v, stacks[88:96, 2, :], I["norm_ffn_g_2"].rearrange("l (m p) -> (l m) p", p=128))

        half = cst("nhalf")

        def rsqrt(dst, src, scale, eps_val, tmp, *deps):
            m, y, t = tmp
            k = half.to_broadcast([128, src.shape[1]])
            po.after(lambda e: e.tensor_scalar(m, src, scale, eps_val, ALU.mult, ALU.add), *deps)
            t1 = po.after(lambda e: e.tensor_tensor(y, m, k, ALU.pow), t_c)
            ve.after(lambda e: e.tensor_tensor(t, y, y, ALU.mult), t1)
            ve.after(lambda e: e.tensor_tensor(t, t, m, ALU.mult))
            ve.after(lambda e: e.tensor_scalar(t, t, -0.5, 1.5, ALU.mult, ALU.add))
            return ve.after(lambda e: e.tensor_tensor(dst, y, t, ALU.mult))

        ss, rr = small(16), small(16)
        tms = [[small(8) for _ in range(3)] for _ in range(2)]

        def row_norm(n, src, junk, *deps):
            t = ac.after(lambda e: e.activation(junk, src, ACT.Square, accum_out=ss[:, n:n + 1]), *deps)
            return rsqrt(rr[:, n:n + 1], ss[:, n:n + 1], 1.0 / 1024, 1e-6, [q[:, 0:1] for q in tms[n]], t)

        def turn_rows(dst, src, n, scale, shift, *deps):
            toks = []
            for g in range(2):
                b, ps, fr = bank()
                for c in range(4):
                    t = pe.do(lambda e, ps=ps, c=c, g=g: e.transpose(
                        ps[:, c * 128:(c + 1) * 128], src[:, (4 * g + c) * 128:(4 * g + c + 1) * 128], ident),
                        fr, *deps, inc=(c == 3))
                d = dst[:, 4 * g:4 * g + 4, n * 128:(n + 1) * 128]
                q = ps[:, :].rearrange("p (c t) -> p c t", c=4)
                if scale is None:
                    if g:
                        t = ve.do(lambda e, d=d, q=q: e.tensor_copy(d, q), t)
                    else:
                        t = ac.do(lambda e, d=d, q=q: e.copy(d, q), t)
                    free[b] = t
                    toks.append(t)
                    continue
                for c in range(4):
                    m = 4 * g + c
                    if shift is None and g == 0:
                        u = ac.do(lambda e, d=d, q=q, c=c, m=m: e.activation(d[:, c, :], q[:, c, :], ACT.Copy, scale=scale[:, m:m + 1]), t)
                    elif shift is None:
                        u = ve.do(lambda e, d=d, q=q, c=c, m=m: e.tensor_scalar(d[:, c, :], q[:, c, :], scale[:, m:m + 1], None,
                                                            ALU.mult), t)
                    elif g == 0:
                        u = ac.do(lambda e, d=d, q=q, c=c, m=m: e.activation(d[:, c, :], q[:, c, :], ACT.Identity,
                                                         scale=scale[:, m:m + 1], bias=shift[:, m:m + 1]), t)
                    else:
                        u = ve.do(lambda e, d=d, q=q, c=c, m=m: e.tensor_scalar(d[:, c, :], q[:, c, :], scale[:, m:m + 1],
                                                            shift[:, m:m + 1], ALU.mult, ALU.add), t)
                    toks.append(u)
                free[b] = toks[-1]
            return toks

        def tokens_by(acts, w, t_w, col, width, ps, fr, deps, chunks=8):
            for k in range(chunks):
                a = acts(k)
                t = pe.do(lambda e, k=k, a=a: e.matmul(ps[:, 0:width], a, w[:, k, col:col + width],
                                                  start=(k == 0), stop=(k == chunks - 1)),
                          t_w, fr, *deps, inc=(k == chunks - 1))
            return t

        cols = small(120)
        t = pe.do(lambda e: e.transpose(PS[0][:, 0:120], stacks[0:120, 0, :], ident[0:120, 0:120]), t_e, t_st)
        t = free[0] = ve.do(lambda e: e.tensor_copy(cols, PS[0][:, 0:120]), t)
        turn[0] = 1
        ccol = small(8)
        t = ac.do(lambda e: e.activation(ccol, cols[:, 48:56], ACT.Silu), t)
        crep = small(256).rearrange("p (a b) -> p a b", a=8)
        t_crep = ve.after(lambda e: e.tensor_copy(crep, ccol.unsqueeze(2).to_broadcast([128, 8, 32])), t)

        for n in range(2):
            row_norm(n, X[:, n, :], MX[:, n, :], t_xl)
            t_h = ve.after(lambda e, n=n: e.tensor_scalar(MX[:, n, :], X[:, n, :], rr[:, n:n + 1], None, ALU.mult))

        w_ada = I["w_ada"][0, :, :].rearrange("(c p) n -> p c n", p=128)
        w_in = I["w_in"][0, :, :].rearrange("(c p) n -> p c n", p=128)
        part = [part_[:, n, :] for n in range(2)]
        modc = small(32).rearrange("p (a c) -> p a c", a=4)
        modr = small(16).rearrange("p (a c) -> p a c", a=2)
        sel = cst("sel")
        t_part, t_sum, t_mod = [None, None], [None, None], [None] * 12

        def ada(j):
            w, t_w = unit(w_ada[:, :, 512 * j:512 * j + 512], 4096, 512)
            b, ps, fr = bank()
            for k in range(2):
                for q in range(4):
                    t = pe.do(lambda e, k=k, q=q: e.matmul(ps[32 * q:32 * q + 32, :], crep[:, 4 * k + q, :],
                                                 w[:, 4 * k + q, :], start=(k == 0), stop=(k == 1)),
                              t_w, fr, t_crep, inc=(k == 1 and q == 3))
            consumed(t)
            pt = part[j % 2]
            free[b] = t_p_ = ac.do(lambda e: e.copy(pt, ps[:, :]), t, t_sum[j % 2])

            def total():
                seg = j // 2
                b, ps, fr = bank()
                if seg in (2, 5):
                    g = gates[:, seg // 3, 512 * (j % 2):512 * (j % 2) + 512]
                    t = t_sum[j % 2] = pe.do(lambda e, ps=ps: e.matmul(ps[:, :], sel, pt, start=True, stop=True), t_p_, fr)
                    free[b] = t_mod[j] = ve.do(lambda e, ps=ps: e.tensor_tensor(g, ps[:, :], g, ALU.add), t, t_v)
                    return
                o = 4 * (j % 2)
                for c in range(4):
                    t = pe.do(lambda e, ps=ps, c=c: e.matmul(ps[:, c:c + 1], pt[:, 128 * c:128 * c + 128], sel[:, 0:1],
                                                 start=True, stop=True), t_p_, fr)
                t_sum[j % 2] = t
                s4 = (0, 1, None, 2, 3, None)[seg]
                free[b] = t_mod[j] = ve.do(lambda e, ps=ps: e.tensor_tensor(
                    modc[:, s4, o:o + 4], ps[:, 0:4], cols[:, 56 + 8 * seg + o:60 + 8 * seg + o], ALU.add), t)
                if seg >= 3:
                    b, ps, fr = bank()
                    r0 = 64 * (j % 2)
                    view = pt.rearrange("k (p c) -> k c p", c=8)
                    for c in range(8):
                        t = pe.do(lambda e, ps=ps, c=c: e.matmul(ps[r0:r0 + 64, c:c + 1], view[:, c, :], sel[:, 0:1],
                                                     start=True, stop=True), fr)
                    t_sum[j % 2] = t
                    free[b] = t_mod[j] = ve.do(lambda e, ps=ps: e.tensor_tensor(
                        modr[r0:r0 + 64, seg - 3, :], ps[r0:r0 + 64, 0:8], by_row[r0:r0 + 64, seg - 3, :],
                        ALU.add), t, t_v)
            return total

        for j in range(4):
            tot = ada(j)
            if j:
                prev()
            prev = tot
        prev()
        t_a1 = ve.after(lambda e: e.scalar_tensor_tensor(modc[:, 1, :], modc[:, 1, :], 1.0, cols[:, 104:112],
                                                         ALU.add, ALU.mult))
        t_hT = []
        for n in range(2):
            t_hT += turn_rows(hT, MX[:, n, :], n, modc[:, 1, :], modc[:, 0, :], t_h, t_a1)

        def mid(ap, n=2):
            return ap.unsqueeze(1).to_broadcast([128, n, ap.shape[1]])

        def v4(ps):
            return ps[:, :].rearrange("p (h i) -> p h i", h=4)

        def four(lhs, rhs, *deps):
            b, ps, fr = bank()
            for h in range(4):
                a, m = lhs(h), rhs(h)
                t = pe.do(lambda e, a=a, m=m, h=h: e.matmul(ps[:, h * 128:(h + 1) * 128], a, m,
                                             start=True, stop=True), fr, *deps, inc=(h == 3))
            return b, ps, t

        def four_turned(src, *deps):
            b, ps, fr = bank()
            for h in range(4):
                a = src(h)
                t = pe.do(lambda e, a=a, h=h: e.transpose(ps[:, h * 128:(h + 1) * 128], a, ident), fr, *deps, inc=(h == 3))
            return b, ps, t

        def heads_bc(ap):
            return ap.unsqueeze(2).to_broadcast([128, 4, 128])

        t_qkv = []

        def delta_project(seg):
            w, t_w = unit(w_in[:, :, 2048 + 512 * seg:2560 + 512 * seg], 4096, 512)
            for m in range(4):
                b, ps, fr = bank()
                for k in range(8):
                    t = pe.do(lambda e, ps=ps, k=k, m=m: e.matmul(
                        ps[:, 0:256], w[:, k, m * 128:(m + 1) * 128], hT[:, k, :],
                        start=(k == 0), stop=(k == 7)), t_w, fr, *t_hT, inc=(k == 7))
                y = qkv[:, 4 * seg + m, :]
                tap = [cols[:, 12 * q + 4 * seg + m:12 * q + 4 * seg + m + 1] for q in range(4)]
                t = ve.do(lambda e, y=y, ps=ps, tap=tap: e.tensor_scalar(y, ps[:, 0:256], tap[3], None, ALU.mult), t)
                for q in (2, 1, 0):
                    o = 3 - q
                    t = ve.after(lambda e, y=y, ps=ps, tap=tap, q=q, o=o: e.scalar_tensor_tensor(
                        y[:, o:256], ps[:, 0:256 - o], tap[q], y[:, o:256], ALU.mult, ALU.add))
                free[b] = t
                t_qkv.append(ac.do(lambda e, y=y: e.activation(y, y, ACT.Silu), t))
            consumed((pe.sem, pe.n))

        delta_project(0)
        delta_project(1)

        SQ = MX[:, :, :].rearrange("p n (a t) -> p (n a) t", t=256)
        t_sq = ac.do(lambda e: e.activation(SQ, qkv[:, 0:8, :], ACT.Square), *t_qkv[0:8], *t_hT)
        b, ps_ab, fr = bank()
        for n in range(2):
            for k in range(8):
                t = pe.do(lambda e, k=k, n=n: e.matmul(
                    ps_ab[:, 8 * n:8 * n + 8], hT[:, k, n * 128:(n + 1) * 128], AB[:, k, :],
                    start=(k == 0), stop=(k == 7)), t_v, fr, inc=(k == 7))
        ab = small(16).rearrange("p (n h) -> p n h", n=2)
        free[b] = t = ve.do(lambda e: e.tensor_copy(ab, ps_ab[:, 0:16].rearrange("p (n h) -> p n h", n=2)), t)

        def s8():
            return small(8).rearrange("p (n h) -> p n h", n=2)

        z, az, gl, beta, ea, GC, EG, BE = (s8() for _ in range(8))
        eal = small(4)
        t = ve.after(lambda e: e.tensor_tensor(z, ab[:, :, 0:4], mid(dtb), ALU.add), t_v)
        ac.do(lambda e: e.activation(eal, alog, ACT.Exp), t_v)
        ac.do(lambda e: e.activation(ea, ab[:, :, 4:8], ACT.Exp, scale=-1.0), t)
        t = ac.do(lambda e: e.activation(az, z, ACT.Abs), t)
        t = ac.after(lambda e: e.activation(az, az, ACT.Exp, scale=-1.0))
        t = ve.after(lambda e: e.tensor_scalar(az, az, 1.0, None, ALU.add), t)
        t = ac.do(lambda e: e.activation(az, az, ACT.Ln), t)
        ve.after(lambda e: e.tensor_scalar(z, z, 0.0, None, ALU.max))
        ve.after(lambda e: e.tensor_tensor(z, z, az, ALU.add), t)
        ve.after(lambda e: e.scalar_tensor_tensor(gl, z, -1.0, mid(eal), ALU.mult, ALU.mult))
        ve.after(lambda e: e.tensor_scalar(ea, ea, 1.0, None, ALU.add))
        t_g = ve.after(lambda e: e.reciprocal(beta, ea))
        heads = "p (n h i) -> p n h i"
        GR = RQ[:, 0:4, :].rearrange("p a b -> p (a b)").rearrange(heads, n=2, h=4)
        BR = RQ[:, 4:8, :].rearrange("p a b -> p (a b)").rearrange(heads, n=2, h=4)
        for n in range(2):
            po.do(lambda e, n=n: e.tensor_copy(GR[:, n], heads_bc(gl[:, n, :])), t_g)
            t_gr = po.do(lambda e, n=n: e.tensor_copy(BR[:, n], heads_bc(beta[:, n, :])), t_g)

        def norm_sums(m):
            b, ps, fr = bank()
            t = pe.do(lambda e: e.matmul(ps[:, :], ones, SQ[:, 2 * m:2 * m + 2, :], start=True, stop=True), t_sq, fr)
            v2 = SQ[:, 2 * m:2 * m + 2, :]
            free[b] = ac.do(lambda e: e.activation(
                v2, ps[:, :].rearrange("p (a t) -> p a t", a=2), ACT.Ln, bias=eps), t)

        for m in (2, 3, 0, 1):
            norm_sums(m)
            if m in (3, 1):
                h4 = slice(0, 4) if m == 1 else slice(4, 8)
                t = ac.after(lambda e, h4=h4: e.activation(SQ[:, h4, :], SQ[:, h4, :], ACT.Exp, scale=-0.5))
                c0 = 128.0 ** -0.5 if m == 1 else 1.0
                t_qk = ve.do(lambda e, c0=c0, h4=h4: e.scalar_tensor_tensor(qkv[:, h4, :], qkv[:, h4, :], c0, SQ[:, h4, :],
                                                              ALU.mult, ALU.mult), t)
                if m == 3:
                    t_kn = t_qk

        DEC, BT, ATT, AT, PM = D
        b, ps, fr = bank()
        for n in range(2):
            t = pe.do(lambda e, ps=ps, n=n: e.matmul(ps[:, 4 * n:4 * n + 4], incl, gl[:, n, :], start=True, stop=True), t_gr, fr)
        free[b] = t = ve.do(lambda e, ps=ps: e.tensor_copy(GC, ps[:, 0:8].rearrange("p (n h) -> p n h", n=2)), t)
        t = ac.do(lambda e: e.activation(EG, GC, ACT.Exp), t)
        t_be = ve.after(lambda e: e.tensor_tensor(BE, EG, beta, ALU.mult), t)
        t_dec, t_bt = [], []
        for n in range(2):
            b, ps, t = four(lambda h, n=n: GR[:, n, h, :], lambda h: incl, t_gr)
            for h in range(4):
                t = ve.do(lambda e, ps=ps, n=n, h=h: e.tensor_scalar(
                    DEC[:, n, h, :], ps[:, h * 128:(h + 1) * 128], GC[:, n, h:h + 1], 0.0,
                    ALU.subtract, ALU.min), t, t_be)
            free[b] = t
            t = ac.do(lambda e, n=n: e.activation(DEC[:, n], DEC[:, n], ACT.Exp), t)
            t_dec.append(po.do(lambda e, n=n: e.tensor_tensor(DEC[:, n], DEC[:, n], mid(incl, 4), ALU.mult), t))
        delta_project(2)
        for n in range(2):
            b, ps, t = four(lambda h, n=n: BR[:, n, h, :], lambda h: ident, t_gr)
            free[b] = ve.do(lambda e, ps=ps, n=n: e.tensor_tensor(BT[:, n], v4(ps), DEC[:, n], ALU.mult), t, t_dec[n])
            t_bt.append(free[b])
        t_br_used = (pe.sem, pe.n)

        t_seg = [[None, None] for _ in range(5)]
        t_rot = {}
        R_ = {}

        def project(seg, col, func):
            def half(n):
                if n == 0:
                    R_["w"] = unit(w_in[:, :, col:col + 512], 4096, 512)
                w, t_w = R_["w"]
                b, ps, fr = bank()
                t = tokens_by(lambda k: hT[:, k, n * 128:(n + 1) * 128], w, t_w, 0, 512, ps, fr, t_hT)
                free[b] = t_seg[seg][n] = ac.do(lambda e: e.activation(proj[:, seg, n, :], ps[:, :], func), t)
                if n == 1:
                    consumed(t)
                if seg < 2:
                    rotate(seg, n)
            return [lambda: half(0), lambda: half(1)]

        ang, kk_, cs, sn = (small(128).rearrange("p (n f) -> p n f", n=2) for _ in range(4))
        posf = small(2)
        po.do(lambda e: e.tensor_copy(posf, posi[:, :]), t_v)
        for n in range(2):
            po.after(lambda e, n=n: e.tensor_scalar(ang[:, n, :], cst("freq"), posf[:, n:n + 1], None, ALU.mult), t_c)
        MAGIC = 12582912.0
        C1, C2 = 6.28125, 0.0019350051879882812
        C3 = float(2 * np.pi - C1 - C2)
        po.after(lambda e: e.tensor_scalar(kk_, ang, float(1 / (2 * np.pi)), None, ALU.mult))
        po.after(lambda e: e.tensor_scalar(kk_, kk_, MAGIC, None, ALU.add))
        po.after(lambda e: e.tensor_scalar(kk_, kk_, -MAGIC, None, ALU.add))
        for cc in (C1, C2, C3):
            po.after(lambda e, cc=cc: e.tensor_scalar(cs, kk_, -cc, None, ALU.mult))
            po.after(lambda e: e.tensor_tensor(ang, ang, cs, ALU.add))
        PI = 3.1415925
        t = po.after(lambda e: e.tensor_scalar(ang, ang, PI, -PI, ALU.min, ALU.max))
        t = ac.do(lambda e: e.activation(cs, ang, ACT.Abs), t)
        t = po.after(lambda e: e.tensor_scalar(cs, cs, -1.0, float(np.pi / 2), ALU.mult, ALU.add), t)
        ac.do(lambda e: e.activation(sn, ang, ACT.Sin), t)
        t_sc = ac.do(lambda e: e.activation(cs, cs, ACT.Sin), t)
        room = small(1024)
        rt = [room[:, 256 * i:256 * i + 256].rearrange("p (h f) -> p h f", h=4) for i in range(4)]

        def rotate(seg, n):
            pv = proj[:, seg, n, :].rearrange("p (h a f) -> p h a f", h=4, a=2)
            x1, x2 = pv[:, :, 0, :], pv[:, :, 1, :]
            cb, sb_ = mid(cs[:, n, :], 4), mid(sn[:, n, :], 4)
            for q, (xa, tr) in enumerate(((x1, cb), (x2, sb_), (x2, cb), (x1, sb_))):
                t = po.do(lambda e, xa=xa, tr=tr, q=q: e.tensor_tensor(rt[q], xa, tr, ALU.mult), t_sc, t_seg[seg][n],
                          t_rot.get("last"))
            po.do(lambda e: e.tensor_tensor(x1, rt[0], rt[1], ALU.subtract), t)
            t_rot[seg, n] = t_rot["last"] = po.do(lambda e: e.tensor_tensor(x2, rt[2], rt[3], ALU.add), t)

        t_rq = []

        def turn_rotated(seg):
            for n in range(2):
                b, ps, t = four_turned(lambda h, n=n: proj[:, seg, n, h * 128:(h + 1) * 128], t_rot[seg, n])
                free[b] = ac.do(lambda e, ps=ps, n=n: e.copy(
                    RQ[:, 4 * seg:4 * seg + 4, n * 128:(n + 1) * 128], v4(ps)), t, t_br_used)
                t_rq.append(free[b])
            R_["turned"] = (pe.sem, pe.n)

        WT = proj[:, 0:2, :, :].rearrange("p a n c -> p (a n c)")[:, 0:1536].rearrange("p (h c) -> p h c", h=4)
        dec_r = cst("decay").rearrange("p (h i) -> p h i", h=4)

        def scores(pair):
            for h in pair:
                b, ps, fr = bank()
                pe.do(lambda e, ps=ps, h=h: e.matmul(ps[:, 0:256], RQ[:, 4 + h, 0:128], RQ[:, h, :],
                                         start=True, stop=True), fr, *t_rq, inc=False)
                t = pe.do(lambda e, ps=ps, h=h: e.matmul(ps[:, 256:384], RQ[:, 4 + h, 128:256], RQ[:, h, 128:256],
                                             start=True, stop=True))
                ve.do(lambda e, ps=ps, h=h: e.tensor_tensor(WT[:, h, 0:256], ps[:, 0:256], dec_r[:, h, :], ALU.mult),
                      t, R_["turned"])
                free[b] = R_["wt"] = ve.do(lambda e, ps=ps, h=h: e.tensor_tensor(WT[:, h, 256:384], ps[:, 256:384],
                                                                     dec_r[:, h, 0:128], ALU.mult))

        def head_norm(o, n, dst, gate_seg, weight, junk, on, *deps):
            s4, r4 = ss[:, 4 * n + 4:4 * n + 8], rr[:, 4 * n + 4:4 * n + 8]
            t = ac.do(lambda e: e.activation(junk, o, ACT.Square), *deps)
            t = ve.do(lambda e: e.tensor_reduce(s4, junk, AX, ALU.add), t)
            t = rsqrt(r4, s4, 1.0 / 128, 1e-6, [q[:, 4:8] for q in tms[n]], t)
            t = ve.after(lambda e: e.tensor_tensor(o, o, heads_bc(r4), ALU.mult))
            if weight is not None:
                t = on.do(lambda e: e.tensor_tensor(o, o, mid(weight, 4), ALU.mult), t)
            return on.do(lambda e: e.tensor_tensor(
                dst, o, proj[:, gate_seg, n, :].rearrange("p (h d) -> p h d", h=4), ALU.mult),
                t, t_seg[gate_seg][n])

        OR = [room[:, 512 * n:512 * n + 512].rearrange("p (h d) -> p h d", h=4) for n in range(2)]
        t_ret = [None, None]

        def retained(n):
            b, ps, fr = bank()
            for h in range(4):
                hs = slice(h * 128, (h + 1) * 128)
                if n == 0:
                    t = pe.do(lambda e, hs=hs, h=h: e.matmul(ps[:, hs], WT[:, h, 0:128], proj[:, 2, 0, hs],
                                                 start=True, stop=True),
                              fr, R_["wt"], *t_seg[2], inc=(h == 3))
                else:
                    pe.do(lambda e, hs=hs, h=h: e.matmul(ps[:, hs], WT[:, h, 128:256], proj[:, 2, 0, hs],
                                             start=True, stop=False), fr, inc=False)
                    t = pe.do(lambda e, hs=hs, h=h: e.matmul(ps[:, hs], WT[:, h, 256:384], proj[:, 2, 1, hs],
                                                 start=False, stop=True), inc=(h == 3))
            free[b] = t = ac.do(lambda e: e.copy(OR[n], v4(ps)), t, t_rot["last"])
            t_ret[n] = head_norm(OR[n], n, MX[:, n, 0:512].rearrange("p (h d) -> p h d", h=4), 3, None,
                                 MX[:, n, 0:512].rearrange("p (h d) -> p h d", h=4), po, t, t_qk)

        def ada_pair(j):
            def first():
                R_["tot"] = ada(j)

            def second():
                R_["tot"]()
            return [first, second]

        t_at, t_att = [], []
        for n in range(2):
            tl = slice(n * 128, (n + 1) * 128)
            b, ps, t = four(lambda h, tl=tl: qkv[:, 4 + h, tl], lambda h, tl=tl: qkv[:, 4 + h, tl], t_kn)
            free[b] = ve.do(lambda e, ps=ps, n=n: e.tensor_tensor(AT[:, n], v4(ps), BT[:, n], ALU.mult), t, t_bt[n])
            t_at.append(free[b])

        KT = small(512).rearrange("p (h d) -> p h d", h=4)
        VBT = qkv[:, 8:12, :].rearrange("p a b -> p (a b)").rearrange(heads, n=2, h=4)
        t_keep = {}

        def by_token():
            b, ps, t = four_turned(lambda h: qkv[:, 4 + h, 0:128], t_kn)
            free[b] = t_keep["kt"] = ac.do(lambda e, ps=ps: e.copy(KT, v4(ps)), t)
            vb_ps = [four_turned(lambda h, n=n: qkv[:, 8 + h, n * 128:(n + 1) * 128], *t_qkv[8:12]) for n in range(2)]
            for n, (b, ps, _) in enumerate(vb_ps):
                t = vb_ps[1][2]
                free[b] = t_keep["vbt"] = ve.do(lambda e, ps=ps, n=n: e.tensor_tensor(
                    VBT[:, n], v4(ps), heads_bc(beta[:, n, :]), ALU.mult), t)

        def queries(n):
            tl = slice(n * 128, (n + 1) * 128)
            b, ps, t = four(lambda h: qkv[:, 4 + h, tl], lambda h: qkv[:, h, tl], t_qk)
            free[b] = ve.do(lambda e: e.tensor_tensor(ATT[:, n], v4(ps), DEC[:, n], ALU.mult), t, t_dec[n])
            t_att.append(free[b])

        more = [by_token, lambda: queries(0), lambda: queries(1)]
        more += project(0, 0, ACT.Copy) + project(1, 512, ACT.Copy) + project(2, 1024, ACT.Copy)
        more += [lambda: turn_rotated(0), lambda: turn_rotated(1), lambda: scores((0, 1)), lambda: scores((2, 3))]
        more += project(3, 1536, ACT.Silu) + [lambda: retained(0), lambda: retained(1)]
        more += project(4, 3584, ACT.Silu)
        for j in range(4, 12):
            more += ada_pair(j)

        def fill(k):
            for _ in range(k):
                if more:
                    more.pop(0)()

        masks = cst("masks").rearrange("p (l i) -> p l i", l=7)
        t_x, t_xt = [None] * 2, [None] * 2
        t_p = [[None] * 2, [None] * 2]
        for level in range(7):
            L2 = LT[level % 2]
            t_l = [po.do(lambda e, L2=L2, n=n, level=level: e.tensor_tensor(
                L2[:, n], AT[:, n], mid(masks[:, level, :], 4), ALU.mult), t_at[n], t_p[level % 2][n])
                for n in range(2)]
            if level == 0:
                idb = mid(ident, 4)
                for n in range(2):
                    b, ps, tq = four(lambda h, L2=L2, n=n: L2[:, n, h, :], lambda h: ident, t_l[n])
                    t_p[0][n] = tq
                    ve.do(lambda e, idb=idb, L2=L2, n=n: e.tensor_tensor(XT[:, n], idb, L2[:, n], ALU.subtract), t_l[n])
                    free[b] = t_x[n] = t_xt[n] = ve.do(lambda e, idb=idb, ps=ps, n=n: e.tensor_tensor(
                        XM[:, n], idb, v4(ps), ALU.subtract), tq)
                    t_p[0][n] = both(tq, t_x[n])
                fill(2)
                continue
            prod = []
            for n in range(2):
                b, ps, tq = four(lambda h, L2=L2, n=n: L2[:, n, h, :], lambda h, n=n: XM[:, n, h, :], t_l[n], t_x[n])
                t_p[level % 2][n] = tq
                free[b] = ac.do(lambda e, ps=ps, n=n: e.copy(PM[:, n], v4(ps)), tq, t_xt[n])
                prod.append(free[b])
            fill(1 if level < 3 else 2)
            for n in range(2):
                b2, ps2, tr = four(lambda h, n=n: PM[:, n, h, :], lambda h, n=n: XT[:, n, h, :], prod[n], t_xt[n])
                if level < 6:
                    b1, ps1, tr = four(lambda h, n=n: XT[:, n, h, :], lambda h, n=n: PM[:, n, h, :])
                    free[b1] = t_x[n] = ve.do(lambda e, ps1=ps1, n=n: e.tensor_tensor(
                        XM[:, n], XM[:, n], v4(ps1), ALU.subtract), tr)
                free[b2] = t_xt[n] = ve.do(lambda e, ps2=ps2, n=n: e.tensor_tensor(
                    XT[:, n], XT[:, n], v4(ps2), ALU.subtract), tr)
            fill(2)

        U0, UK = PM[:, 0], PM[:, 1]
        ST, VN = LT[0][:, 0], LT[0][:, 1]
        O0, O1 = OR
        b, ps, t = four(lambda h: XT[:, 0, h, :], lambda h: VBT[:, 0, h, :], t_xt[0], t_xt[1], t_keep["vbt"])
        ve.do(lambda e, ps=ps: e.tensor_copy(U0, v4(ps)), t)
        free[b] = t_uk = ve.do(lambda e, ps=ps: e.tensor_tensor(
            UK, v4(ps), DEC[:, 0, :, 127:128].to_broadcast([128, 4, 128]), ALU.mult), t)
        fill(2)
        b, ps, t = four(lambda h: KT[:, h, :], lambda h: UK[:, h, :], t_uk, t_keep["kt"])
        free[b] = t_stt = ve.do(lambda e, ps=ps: e.tensor_copy(ST, v4(ps)), t)
        b0, ps0, t0 = four(lambda h: ATT[:, 0, h, :], lambda h: U0[:, h, :], t_uk, t_att[0])
        kept.add(b0)
        fill(2)
        b, ps, t = four(lambda h: qkv[:, 4 + h, 128:256], lambda h: ST[:, h, :], t_stt)
        ve.do(lambda e, ps=ps: e.tensor_tensor(VN, v4(ps), heads_bc(BE[:, 1, :]), ALU.mult), t)
        free[b] = t_vn = ve.after(lambda e: e.tensor_tensor(VN, VBT[:, 1], VN, ALU.subtract))
        bq, psq, tq = four(lambda h: qkv[:, h, 128:256], lambda h: ST[:, h, :], t_stt)
        kept.add(bq)
        fill(2)
        b, ps, t = four(lambda h: XT[:, 1, h, :], lambda h: VN[:, h, :], t_vn, t_xt[1])
        U1 = UK
        free[b] = t_u1 = ve.do(lambda e, ps=ps: e.tensor_copy(U1, v4(ps)), t)
        fill(2)
        b1, ps1, t1 = four(lambda h: ATT[:, 1, h, :], lambda h: U1[:, h, :], t_u1, t_att[1])
        jn = [XM[:, n] for n in range(2)]
        free[b0] = t = ac.do(lambda e: e.copy(O0, v4(ps0)), t0, *t_ret)
        t_mx = [None, None]
        t_mx[0] = head_norm(O0, 0, MX[:, 0, 512:1024].rearrange("p (h d) -> p h d", h=4), 4, dnw, jn[0], ve, t)
        free[bq] = ve.do(lambda e: e.tensor_tensor(O1, v4(psq), heads_bc(EG[:, 1, :]), ALU.mult), tq, *t_ret)
        free[b1] = t = ve.after(lambda e, ps1=ps1: e.tensor_tensor(O1, O1, v4(ps1), ALU.add), t1)
        t_mx[1] = head_norm(O1, 1, MX[:, 1, 512:1024].rearrange("p (h d) -> p h d", h=4), 4, dnw, jn[1], ve, t)
        kept.clear()
        fill(len(more))

        xs = nc.dram_tensor("rows_scratch", (512, 1024), F32, kind="Internal").ap()
        table = nc.dram_tensor("table_scratch", (NE * 256, 1), F32, kind="Internal").ap()
        ys = nc.dram_tensor("pair_scratch", (1024, 512), F32, kind="Internal").ap()
        f_xs, f_tab, f_tl, f_bl = flag("f_xs"), flag("f_tab"), flag("f_tl"), flag("f_bl")
        ve.after(lambda e: e.scalar_tensor_tensor(modr[:, 1, :], modr[:, 1, :], 1.0, by_row[:, 2, :],
                                                  ALU.add, ALU.mult))
        t_a2 = ve.after(lambda e: e.scalar_tensor_tensor(modc[:, 3, :], modc[:, 3, :], 1.0, cols[:, 112:120],
                                                         ALU.add, ALU.mult))
        w_out = I["w_out"][0, :, :].rearrange("(c p) n -> p c n", p=128)
        w_o2 = [unit(w_out[:, :, 512 * j:512 * j + 512], 4096, 512) for j in range(2)]
        t_x1, t_h2, t_hT, t_hT2 = [None] * 2, [None] * 2, [None] * 2, []
        proj_room = LT[1]
        for n in range(2):
            t_hT[n] = turn_rows(hT, MX[:, n, :], n, None, None, t_mx[n], t_ret[n])
        for n in range(2):
            for j in range(2):
                w, t_w = w_o2[j]
                js = slice(512 * j, 512 * j + 512)
                b, ps, fr = bank()
                t = tokens_by(lambda k, n=n: hT[:, k, n * 128:(n + 1) * 128], w, t_w, 0, 512, ps, fr, t_hT[n])
                tmp = proj_room[:, j].rearrange("p h d -> p (h d)")
                free[b] = ve.after(lambda e, tmp=tmp, ps=ps, js=js: e.tensor_tensor(tmp, ps[:, :], gates[:, 0, js], ALU.mult), t)
                t_x1[n] = ve.after(lambda e, tmp=tmp, n=n, js=js: e.tensor_tensor(X[:, n, js], X[:, n, js], tmp, ALU.add))
                if n:
                    consumed(t)
            row_norm(n, X[:, n, :], MX[:, n, :], t_x1[n], *t_hT[n])
            t_h2[n] = ve.after(lambda e, n=n: e.tensor_scalar(MX[:, n, :], X[:, n, :], rr[:, n:n + 1], None, ALU.mult))
            for k in range(2):
                t_xs = po.dma(lambda e, n=n, k=k: e.dma_start(xs[256 * k + 128 * n:256 * k + 128 * n + 128, :], MX[:, n, :]),
                              f_xs, t_h2[n])
        for n in range(2):
            t_hT2 += turn_rows(hT, MX[:, n, :], n, modc[:, 3, :], modc[:, 2, :], t_h2[n], t_a2, (pe.sem, pe.n))

        b, ps_l, fr = bank()
        for n in range(2):
            for k in range(8):
                t = pe.do(lambda e, k=k, n=n: e.matmul(ps_l[:, 64 * n:64 * n + 36], hT[:, k, n * 128:(n + 1) * 128],
                                             WR[:, k, :], start=(k == 0), stop=(k == 7)),
                          t_v, fr, *t_hT2, inc=(k == 7))
        W = part_[:, :, :].rearrange("p a b -> p (a b)")
        done_all = tuple((l.sem, l.n) for l in (pe, ve, ac, po))
        for i in range(3):
            last_read[R + i] = done_all
        q0 = at_slot[0]
        rota[:] = [q0 % R, (q0 + 1) % R, R, R + 1, R + 2, (q0 + 2) % R, (q0 + 3) % R]
        at_slot[0] = 0
        w_at = [0]

        def ws(*shape):
            n = int(np.prod(shape))
            a = w_at[0]
            w_at[0] += n
            v = W[:, a:a + n]
            if len(shape) == 2:
                return v.rearrange("p (a b) -> p a b", a=shape[0])
            if len(shape) == 3:
                return v.rearrange("p (a b c) -> p a b c", a=shape[0], b=shape[1])
            return v

        L = ws(2, 36)
        free[b] = ve.after(lambda e: e.tensor_tensor(
            L, ps_l[:, 0:128].rearrange("p (n c) -> p n c", n=2)[:, :, 0:36], mid(rb), ALU.add), t)

        def bc(ap, *shape):
            while len(ap.shape) < len(shape) + 1:
                ap = ap.unsqueeze(len(ap.shape))
            return ap.to_broadcast([128, *shape])

        def first_max(v, k, rev):
            m, q, oh, sc, m2 = ws(2, 1), None, ws(2, k), ws(2, k), ws(2, 1)
            ve.after(lambda e: e.tensor_reduce(m[:, :, 0], v, AX, ALU.max))
            ve.after(lambda e: e.tensor_tensor(sc, v, bc(m, 2, k), ALU.is_ge))
            ve.after(lambda e: e.tensor_tensor(sc, sc, mid(rev), ALU.mult))
            ve.after(lambda e: e.tensor_reduce(m2[:, :, 0], sc, AX, ALU.max))
            ve.after(lambda e: e.tensor_tensor(oh, sc, bc(m2, 2, k), ALU.is_equal))
            return m, oh

        lg = L[:, :, 0:4]
        gm, ohg = first_max(lg, 4, cst("rev4"))
        eg, zs = ws(2, 4), ws(2, 1)
        t = ve.after(lambda e: e.tensor_tensor(eg, lg, bc(gm, 2, 4), ALU.subtract))
        t = ac.do(lambda e: e.activation(eg, eg, ACT.Exp), t)
        ve.after(lambda e: e.tensor_reduce(zs[:, :, 0], eg, AX, ALU.add), t)
        ve.after(lambda e: e.reciprocal(zs, zs))
        pr = ws(2, 4, 8)
        es, es2 = ws(2, 8), ws(2, 8)
        ohg4 = ohg.unsqueeze(3).to_broadcast([128, 2, 4, 8])
        ve.after(lambda e: e.tensor_tensor(pr, L[:, :, 4:36].rearrange("p n (g e) -> p n g e", g=4), ohg4, ALU.mult))
        ve.after(lambda e: e.tensor_reduce(es, pr.rearrange("p n g e -> p n e g"), AX, ALU.add))
        m1, oh1 = first_max(es, 8, cst("rev8"))
        ve.after(lambda e: e.scalar_tensor_tensor(es2, oh1, -3.0e38, es, ALU.mult, ALU.add))
        m2, oh2 = first_max(es2, 8, cst("rev8"))
        e2, den = ws(2, 1), ws(2, 1)
        gate = small(4).rearrange("p (k n) -> p k n", k=2)
        t = ve.after(lambda e: e.tensor_tensor(e2, m2, m1, ALU.subtract))
        t = ac.do(lambda e: e.activation(e2, e2, ACT.Exp), t)
        ve.after(lambda e: e.tensor_scalar(den, e2, 1.0, None, ALU.add), t)
        ve.after(lambda e: e.reciprocal(den, den))
        ve.after(lambda e: e.tensor_tensor(gate[:, 0, :], zs[:, :, 0], den[:, :, 0], ALU.mult))
        ve.after(lambda e: e.tensor_tensor(gate[:, 1, :], gate[:, 0, :], e2[:, :, 0], ALU.mult))
        M = [ws(2, 4, 8), ws(2, 4, 8)]
        for k, oh in enumerate((oh1, oh2)):
            ve.after(lambda e, k=k, oh=oh: e.tensor_tensor(M[k], oh.unsqueeze(2).to_broadcast([128, 2, 4, 8]),
                                                           ohg4, ALU.mult))
        SM = ws(2, 32)
        flat = [m.rearrange("p n g e -> p n (g e)") for m in M]
        t_sm = ve.after(lambda e: e.tensor_tensor(SM, flat[0], flat[1], ALU.add))
        b, ps_r, fr = bank()
        pe.do(lambda e: e.matmul(ps_r[:, 0:32], strict, SM[:, 0, :], start=True, stop=True), t_sm, fr, inc=False)
        pe.do(lambda e: e.matmul(ps_r[:, 32:64], ones, SM[:, 0, :], start=True, stop=False), inc=False)
        pe.do(lambda e: e.matmul(ps_r[:, 32:64], strict, SM[:, 1, :], start=False, stop=True), inc=False)
        pe.do(lambda e: e.matmul(ps_r[:, 64:96], ones, SM[:, 0, :], start=True, stop=False), inc=False)
        t = pe.do(lambda e: e.matmul(ps_r[:, 64:96], ones, SM[:, 1, :], start=False, stop=True))
        rank, pp, posv, cnt = ws(2, 32), ws(2, 32), ws(2, 2), ws(1)
        ve.after(lambda e: e.tensor_tensor(rank, ps_r[:, 0:64].rearrange("p (n c) -> p n c", n=2),
                                           mid(cst("base")), ALU.add), t)
        ve.after(lambda e: e.tensor_reduce(cnt, ps_r[:, 64:96], AX, ALU.max))
        free[b] = t_flag = ve.after(lambda e: e.tensor_scalar(flag_i[:, :], cnt, SLOTS + 0.5, None, ALU.is_gt))
        for k in range(2):
            ve.after(lambda e, k=k: e.tensor_tensor(pp, flat[k], rank, ALU.mult))
            ve.after(lambda e, k=k: e.tensor_reduce(posv[:, k, :], pp, AX, ALU.add))
        t_pos = ve.after(lambda e: e.tensor_copy(pos_u[:, :, :], posv))
        assert w_at[0] <= 1024

        tlb = RQ[:, 0:1, :].rearrange("p a (b c) -> p (a b) c", b=2)
        blank = sb("blank", [128, 64])
        t = po.do(lambda e: e.memset(blank[:, :], SPARE))
        t_bl = po.dma(lambda e: e.dma_start(table.rearrange("(r s) o -> r (s o)", s=64), blank[:, :]), f_bl, t)
        for k in range(2):
            for n in range(2):
                t_tab = po.dma(lambda e, k=k, n=n: e.indirect_dma_start(
                    table, bass.IndirectOffsetOnAxis(ap=pos_u[:, k, n:n + 1], axis=0),
                    cst("ids")[:, 2 * k + n:2 * k + n + 1], None), f_tab, t_pos, t_bl)
        tl2 = tlb[:, 0, :]
        tl = tlb[:, 1, :].rearrange("p (a b) -> p a b", a=2)
        for k in range(2):
            t_tl = po.dma(lambda e, k=k, tl=tl: e.dma_start(tl[:, k, :], table.rearrange("(r s) o -> r (s o)", s=64)),
                          f_tl, t_tab)
        t = ve.after(lambda e, tl=tl: e.tensor_copy(tl2.rearrange("p (a b) -> p a b", a=2), tl), t_tl)
        b, ps_t, fr = bank()
        t = pe.do(lambda e: e.transpose(ps_t[:, 0:128], tl2, ident), t, fr)
        ve.after(lambda e: e.tensor_copy(idx[:, 0, :], ps_t[:, 0:128]), t)
        free[b] = t_idx = ve.after(lambda e: e.tensor_scalar(idx[:, 1, :], ps_t[:, 0:128], 2.0, cst("half"),
                                                             ALU.mult, ALU.add))

        flat_p = proj[:, :, :, :].rearrange("p a b c -> p (a b c)")
        XG = [flat_p[0:SLOTS, 1024 * i:1024 * i + 1024] for i in range(2)]
        XTe = [flat_p[:, 2048 + 512 * i:2560 + 512 * i].rearrange("p (c s) -> p c s", c=8) for i in range(2)]
        HD = [flat_p[0:SLOTS, 3072 + 512 * i:3584 + 512 * i] for i in range(2)]
        HTe = [flat_p[:, 4096 + 256 * i:4352 + 256 * i].rearrange("p (c s) -> p c s", c=4) for i in range(2)]
        SL = [RQ[0:SLOTS, 2 * i:2 * i + 2, :].rearrange("p a b -> p (a b)") for i in range(2)]
        YS = [RQ[:, 4 + 2 * i:6 + 2 * i, :].rearrange("p a b -> p (a b)") for i in range(2)]
        w1, w3, w2 = I["w1"][0], I["w3"][0], I["w2"][0]
        for i in range(2):
            t_zero = po.do(lambda e, i=i: e.memset(XG[i], 0.0), (ve.sem, t_h2[1][1]), t_hT2[-1])

        def experts(jobs, lanes, load, done, flags, banks_free, first):
            p_, v_, a_, g_ = lanes
            f_g, f_s = flags
            g_tok, y_tok, x_tok, xt_tok, h_tok, hd_tok, ht_tok = {}, {}, {}, {}, {}, {}, {}
            bt = [0]

            def nb():
                b = bt[0] % 8
                bt[0] += 1
                return b, PS[b], banks_free[b]

            def gather(i):
                e_, blk = jobs[i]
                col = e_ * NBLK + blk
                g_tok[i] = g_.dma(lambda e: e.indirect_dma_start(
                    XG[i % 2], None, xs, bass.IndirectOffsetOnAxis(ap=idx[0:SLOTS, 0, col:col + 1], axis=0),
                    bounds_check=511, oob_is_err=False), f_g[i % 2], *first, x_tok.get(i - 2))

            def turn_x(i):
                b, ps, fr = nb()
                src = XG[i % 2].rearrange("s (p c) -> s c p", c=8)
                for c in range(8):
                    t = p_.do(lambda e, c=c: e.transpose(ps[:, c * SLOTS:(c + 1) * SLOTS], src[:, c, :],
                                                         ident[0:SLOTS, 0:SLOTS]), fr, g_tok[i], inc=(c == 7))
                x_tok[i] = t
                banks_free[b] = t = v_.do(lambda e: e.tensor_tensor(
                    XTe[i % 2], ps[:, :].rearrange("p (c s) -> p c s", c=8),
                    modr[:, 1, :].unsqueeze(2).to_broadcast([128, 8, SLOTS]), ALU.mult), t, h_tok.get(i - 2))
                xt_tok[i] = v_.do(lambda e: e.tensor_tensor(
                    XTe[i % 2], XTe[i % 2], modr[:, 0, :].unsqueeze(2).to_broadcast([128, 8, SLOTS]), ALU.add), t)

            def up(i):
                (u1, t1), (u3, t3) = load("w1", jobs[i]), load("w3", jobs[i])
                b, ps, fr = nb()
                for k in range(8):
                    p_.do(lambda e, k=k: e.matmul(ps[0:SLOTS, :], XTe[i % 2][:, k, :], u1[:, k, :],
                                                  start=(k == 0), stop=(k == 7)), fr, xt_tok[i], t1, inc=False)
                    t = p_.do(lambda e, k=k: e.matmul(ps[64:64 + SLOTS, :], XTe[i % 2][:, k, :], u3[:, k, :],
                                                      start=(k == 0), stop=(k == 7)), t3, inc=(k == 7))
                h_tok[i] = t
                done(t)
                done(t)
                t = a_.do(lambda e: e.activation(SL[i % 2], ps[0:SLOTS, :], ACT.Silu), t, hd_tok.get(i - 2))
                banks_free[b] = hd_tok[i] = v_.do(lambda e: e.tensor_tensor(
                    HD[i % 2], SL[i % 2], ps[64:64 + SLOTS, :], ALU.mult), t, ht_tok.get(("pe", i - 2)))

            def turn_h(i):
                b, ps, fr = nb()
                src = HD[i % 2].rearrange("s (p c) -> s c p", c=4)
                for c in range(4):
                    t = p_.do(lambda e, c=c: e.transpose(ps[:, c * SLOTS:(c + 1) * SLOTS], src[:, c, :],
                                                         ident[0:SLOTS, 0:SLOTS]), fr, hd_tok[i], inc=(c == 3))
                ht_tok["pe", i] = t
                banks_free[b] = ht_tok[i] = v_.do(lambda e: e.tensor_copy(
                    HTe[i % 2], ps[:, 0:4 * SLOTS].rearrange("p (c s) -> p c s", c=4)), t, y_tok.get(("pe", i - 2)))

            def down(i):
                e_, blk = jobs[i]
                col = e_ * NBLK + blk
                u2, t2 = load("w2", jobs[i])
                b, ps, fr = nb()
                for k in range(4):
                    p_.do(lambda e, k=k: e.matmul(ps[0:SLOTS, :], HTe[i % 2][:, k, :], u2[:, k, 0:512],
                                                  start=(k == 0), stop=(k == 3)), fr, ht_tok[i], t2, inc=False)
                    t = p_.do(lambda e, k=k: e.matmul(ps[64:64 + SLOTS, :], HTe[i % 2][:, k, :], u2[:, k, 512:1024],
                                                      start=(k == 0), stop=(k == 3)), inc=(k == 3))
                y_tok["pe", i] = t
                done(t)
                banks_free[b] = t = a_.do(lambda e: e.copy(YS[i % 2], ps[:, :]), t, y_tok.get(i - 2))
                y_tok[i] = g_.dma(lambda e: e.indirect_dma_start(
                    ys, bass.IndirectOffsetOnAxis(ap=idx[:, 1, col:col + 1], axis=0), YS[i % 2], None,
                    bounds_check=1023, oob_is_err=False), f_s[i % 2], t)

            N = len(jobs)
            gather(0)
            gather(1)
            turn_x(0)
            up(0)
            turn_x(1)
            for i in range(N):
                if i + 2 < N:
                    gather(i + 2)
                if i + 1 < N:
                    up(i + 1)
                turn_h(i)
                if i + 2 < N:
                    turn_x(i + 2)
                down(i)
            return [y_tok[N - 2], y_tok[N - 1]]

        fcol = small(192)
        v_fin, v_psc, v_pb = W, gates[:, 0, :], vrow[:, :]
        b, ps, fr = bank()
        pe.do(lambda e, ps=ps: e.transpose(ps[:, 0:96], stacks[0:96, 1, :], ident[0:96, 0:96]), fr, t_v, inc=False)
        t = pe.do(lambda e, ps=ps: e.transpose(ps[:, 96:192], stacks[0:96, 2, :], ident[0:96, 0:96]))
        free[b] = t_fcol = ve.after(lambda e, ps=ps: e.tensor_copy(fcol, ps[:, 0:192]), t)
        f_w = flag("f_w")
        load(f_w, v_fin, I["final_norm_w"].partition_broadcast(128), t_idx)
        load(f_w, v_psc, I["pool_scale_2"][0, :].partition_broadcast(128), t_idx)
        t_w5 = load(f_w, v_pb, I["pool_b_2"][0, :].partition_broadcast(128), t_idx)
        t_pbs = ve.do(lambda e: e.tensor_tensor(v_pb, v_pb, v_psc, ALU.mult), t_w5)

        srcs = {"w1": (w1, 8), "w3": (w3, 8), "w2": (w2, 4)}

        def load_main(kind, job):
            w, c = srcs[kind]
            return unit(w[job[0]].rearrange("(p c) n -> p c n", c=c), 4096, 4096 // c)

        t_ys = experts([(e, 0) for e in range(NE)], (pe, ve, ac, po), load_main, consumed,
                       ([flag("g0"), flag("g1")], [flag("y0"), flag("y1")]), free, (t_idx, t_xs, t_zero))
        po.wait((f_xs[0], f_xs[1]), t_zero)
        split = {id(l): len(l.ops) for l in (pe, ve, ac, po, sp)}

        o_pe, o_ve, o_ac, o_po, o_sp = (Lane(sem(n)) for n in ("o_pe", "o_ve", "o_ac", "o_po", "o_sp"))
        last_used = (pe.sem, pe.n)
        o_flag = [flag(f"o{i}") for i in range(3)]
        o_used = [None] * 3
        order = {"w1": 0, "w3": 1, "w2": 2}
        pend = []

        def load_more(kind, job):
            w, c = srcs[kind]
            s = order[kind]
            dst = ring[:, s, :].rearrange("p (a b) -> p a b", b=4096 // c)
            src = w[job[0]].rearrange("(p c) n -> p c n", c=c)
            t = o_sp.dma(lambda e: e.dma_start(dst, src), o_flag[s], last_used, o_used[s])
            pend.append(s)
            return dst, t

        def done_more(t):
            o_used[pend.pop(0)] = t

        o_free = list(free)
        jobs = [(e, blk) for e in range(NE) for blk in range(1, NBLK)]
        t_more = experts(jobs, (o_pe, o_ve, o_ac, o_po), load_more, done_more,
                         ([flag("og0"), flag("og1")], [flag("oy0"), flag("oy1")]), o_free, (t_idx, *t_ys, last_used))
        o_po.wait(*t_more)
        for lane in (o_ve, o_ac, o_sp, o_pe):
            lane.wait((o_pe.sem, o_pe.n), (o_ve.sem, o_ve.n), (o_ac.sem, o_ac.n))
        for i in range(3):
            o_sp.wait((o_flag[i][0], o_flag[i][1]))

        po.wait(*t_ys)
        mark = small(1)
        t_join = po.do(lambda e: e.memset(mark, 0.0))
        YP = flat_p[:, 0:4096].rearrange("p (q n c) -> p q n c", q=2, n=2)
        q0 = at_slot[0]
        rota[:] = [rota[(q0 + i) % (R + 3)] for i in range(R + 3)]
        rota[:] = [i for i in rota if i < R]
        at_slot[0] = 0
        after_ring = last_read[R:]
        lateb, t_band = unit(I["late"].unsqueeze(1), 1536, 1536)
        band = lateb[:, 0, :].rearrange("p (g c) -> p g c", g=4)
        w_pool, t_wp = unit(I["pool_w_2"][0].rearrange("g (c p) d -> p (g c) d", p=128), 2048, 256)
        w_f = I["ffn_w_in_2"][0].rearrange("(c p) n -> p c n", p=128)
        ACTB = pool_[:, 0:5632].rearrange("p (m t) -> p m t", t=256)
        gt = [pool_[:, 8192 + 256 * i:8448 + 256 * i] for i in range(4)]
        ve.wait(*after_ring)
        f_y = [flag("f_y0"), flag("f_y1")]
        t_y, t_m2, t_hm = [None] * 2, [None] * 2, [None] * 2
        for n in range(2):
            for q in range(2):
                r0 = 512 * q + 256 * n
                t_y[n] = ac.dma(lambda e, q=q, n=n, r0=r0: e.dma_start(
                    YP[:, q, n, :], ys[r0:r0 + 256, :].rearrange("(p h) c -> p (h c)", h=2)), f_y[n], t_join,
                    (pe.sem, pe.n), (ve.sem, ve.n))
        for n in range(2):
            y0, y1 = YP[:, 0, n, :], YP[:, 1, n, :]
            t = ac.do(lambda e, y0=y0, n=n: e.activation(y0, y0, ACT.Copy, scale=gate[:, 0, n:n + 1]), t_y[n])
            ve.do(lambda e, y0=y0, y1=y1, n=n: e.scalar_tensor_tensor(y0, y1, gate[:, 1, n:n + 1], y0, ALU.mult, ALU.add), t)
            ve.after(lambda e, y0=y0: e.tensor_tensor(y0, y0, gates[:, 1, :], ALU.mult))
            t_m2[n] = ve.after(lambda e, y0=y0, n=n: e.tensor_tensor(X[:, n, :], X[:, n, :], y0, ALU.add))
        for n in range(2):
            row_norm(n, X[:, n, :], MX[:, n, :], t_m2[n])
            t_m2[n] = ve.after(lambda e, n=n: e.scalar_tensor_tensor(X[:, n, :], X[:, n, :], rr[:, n:n + 1], v_fin,
                                                                ALU.mult, ALU.mult), t_w5)
        for n in range(2):
            t = row_norm(n, X[:, n, :], MX[:, n, :], t_m2[n])
            t_hm[n] = ac.do(lambda e, n=n: e.activation(MX[:, n, :], X[:, n, :], ACT.Copy, scale=rr[:, n:n + 1]), t)
            t_m2[n] = po.do(lambda e, n=n: e.tensor_tensor(X[:, n, :], X[:, n, :], v_pb, ALU.add), t_hm[n], t_pbs)

        t_d = []
        for c in range(8):
            g = c // 2
            b, ps, fr = bank()
            cc = slice(c * 128, (c + 1) * 128)
            pe.do(lambda e, ps=ps, cc=cc, g=g: e.matmul(ps[:, 0:128], MX[:, 0, cc], band[:, g, 0:128],
                                     start=True, stop=True), t_hm[0], fr, t_band, inc=False)
            pe.do(lambda e, ps=ps, cc=cc, g=g: e.matmul(ps[:, 128:256], MX[:, 0, cc], band[:, g, 128:256],
                                     start=True, stop=False), inc=False)
            t = pe.do(lambda e, ps=ps, cc=cc, g=g: e.matmul(ps[:, 128:256], MX[:, 1, cc], band[:, g, 256:384],
                                         start=False, stop=True), t_hm[1])
            s = fcol[:, 176 + c:177 + c]
            if c % 2:
                free[b] = ac.do(lambda e, ps=ps, s=s, c=c: e.activation(hT[:, c, :], ps[:, 0:256], ACT.Copy, scale=s), t)
            else:
                free[b] = ve.do(lambda e, s=s, ps=ps, c=c: e.tensor_scalar(hT[:, c, :], ps[:, 0:256], s, None, ALU.mult), t)
            t_d.append(free[b])
        consumed(t)
        t_x3 = [None] * 2
        for n in range(2):
            for gg in range(2):
                b, ps, fr = bank()
                for g in (2 * gg, 2 * gg + 1):
                    o = 256 * (g % 2)
                    for c in range(2):
                        t = pe.do(lambda e, ps=ps, c=c, o=o, g=g, n=n: e.matmul(
                            ps[:, o:o + 256], hT[:, 2 * g + c, n * 128:(n + 1) * 128], w_pool[:, 2 * g + c, :],
                            start=(c == 0), stop=(c == 1)), fr, t_wp, t_d[2 * g], t_d[2 * g + 1])
                gs = slice(512 * gg, 512 * gg + 512)
                tmp = YP[:, 0, n, gs]
                free[b] = ve.do(lambda e, tmp=tmp, ps=ps, gs=gs: e.tensor_tensor(tmp, ps[:, :], v_psc[:, gs], ALU.mult), t, t_w5)
                t_x3[n] = ve.after(lambda e, tmp=tmp, n=n, gs=gs: e.tensor_tensor(X[:, n, gs], X[:, n, gs], tmp, ALU.add), t_m2[n])
        consumed(t)
        t_pool = t

        t_n3 = [None] * 2
        for n in range(2):
            row_norm(n, X[:, n, :], MX[:, n, :], t_x3[n], t_pool)
            t_n3[n] = ve.after(lambda e, n=n: e.tensor_scalar(MX[:, n, :], X[:, n, :], rr[:, n:n + 1], None, ALU.mult))
        t_hT = []
        for n in range(2):
            t_hT += turn_rows(hT, MX[:, n, :], n, fcol[:, 184:192], None, t_n3[n], t_pool)
        t_act = [None] * 22
        t_gt = [None] * 4
        for u in range(11):
            w, t_w = unit(w_f[:, :, 512 * u:512 * u + 512], 4096, 512)
            for q in range(4):
                m = 4 * u + q
                b, ps, fr = bank()
                for k in range(8):
                    t = pe.do(lambda e, ps=ps, w=w, k=k, q=q: e.matmul(
                        ps[:, 0:256], w[:, k, q * 128:(q + 1) * 128], hT[:, k, :],
                        start=(k == 0), stop=(k == 7)), t_w, fr, *t_hT, inc=(k == 7))
                y = ACTB[:, m, :] if m < 22 else gt[m % 4]
                tap = [fcol[:, 44 * r + m:44 * r + m + 1] for r in range(4)]
                t = ve.do(lambda e, y=y, ps=ps, tap=tap: e.tensor_scalar(y, ps[:, 0:256], tap[2], tap[3], ALU.mult, ALU.add),
                          t, t_fcol, t_gt[m % 4] if m >= 22 else None)
                for r in (1, 0):
                    o = 2 - r
                    t = ve.after(lambda e, y=y, ps=ps, tap=tap, r=r, o=o: e.scalar_tensor_tensor(
                        y[:, o:256], ps[:, 0:256 - o], tap[r], y[:, o:256], ALU.mult, ALU.add))
                free[b] = t
                if m >= 22:
                    t = ac.do(lambda e, y=y: e.activation(y, y, ACT.Silu), t)
                    t_act[m - 22] = t_gt[m % 4] = po.do(lambda e, y=y, m=m: e.tensor_tensor(
                        ACTB[:, m - 22, :], ACTB[:, m - 22, :], y, ALU.mult), t)
            consumed((pe.sem, pe.n))
        w_o = I["ffn_w_out_2"][0].rearrange("(c p) n -> p c n", p=128)
        acc = [bank() for _ in range(4)]
        for u in range(6):
            nk = min(4, 22 - 4 * u)
            w, t_w = unit(w_o[:, 4 * u:4 * u + nk, :], 1024 * nk, 1024)
            for k in range(nk):
                kk = 4 * u + k
                for a, (b, ps, fr) in enumerate(acc):
                    n, j = a // 2, a % 2
                    t = pe.do(lambda e, ps=ps, w=w, kk=kk, k=k, n=n, j=j: e.matmul(
                        ps[:, :], ACTB[:, kk, n * 128:(n + 1) * 128], w[:, k, 512 * j:512 * j + 512],
                        start=(kk == 0), stop=(kk == 21)), t_w, fr, t_act[kk])
            consumed(t)
        f_o = flag("f_o")
        o_r = out.rearrange("b (n p) d -> p (b n) d", p=128)
        for a, (b, ps, fr) in enumerate(acc):
            n, j = a // 2, a % 2
            js = slice(512 * j, 512 * j + 512)
            tt = ve.after(lambda e, ps=ps, n=n, js=js: e.tensor_tensor(X[:, n, js], X[:, n, js], ps[:, :], ALU.add), t)
            t_o = ac.dma(lambda e, n=n, js=js: e.dma_start(o_r[:, n, js], X[:, n, js]), f_o, tt)
        ac.wait(t_o)

        block = ctx.enter_context(nc.Block())

        def run(eng, lane, more):
            cut = split[id(lane)]
            whole = lane.ops
            seen = {}
            lane.ops = whole[:cut]
            lane.play(eng, seen)
            eng.wait_ge(t_flag[0], t_flag[1])
            val = eng.value_load(flag_i[0:1, 0:1], min_val=0, max_val=1)
            with eng.If(val > 0):
                more.play(eng, dict(seen))
            lane.ops = whole[cut:]
            lane.play(eng, seen)

        @block.sync
        def _(eng):
            run(eng, sp, o_sp)

        @block.tensor
        def _(eng):
            run(eng, pe, o_pe)

        @block.vector
        def _(eng):
            run(eng, ve, o_ve)

        @block.scalar
        def _(eng):
            run(eng, ac, o_ac)

        @block.gpsimd
        def _(eng):
            run(eng, po, o_po)


_INS = ['x', 'c', 'positions', 'w_ada', 'b_ada', 'norm1_w', 'w_in', 'conv_w', 'a_log', 'dt_bias', 'dn_norm_w',
        'w_out', 'norm2_w', 'w_group', 'b_group', 'w_expert', 'b_expert', 'w1', 'w3', 'w2', 'final_norm_w',
        'norm_mix_g_2', 'norm_ffn_g_2', 'pool_w_2', 'pool_b_2', 'pool_scale_2', 'ffn_w_in_2', 'ffn_conv_w_2',
        'ffn_conv_b_2', 'ffn_w_out_2']


def kernel(**inputs):
    import numpy as _np
    import concourse.bacc as _bacc
    from concourse import mybir as _mybir
    from concourse.bass_utils import run_bass_kernel_spmd as _run

    nc = _bacc.Bacc("TRN2", target_bir_lowering=False, num_devices=1)
    given = {k: _np.ascontiguousarray(inputs[k]) for k in _INS}
    given["consts"] = _np.concatenate(list(constants().values()), axis=1)
    given["late"] = late_constants()
    arrays, aps = {}, {}
    for name, a in given.items():
        arrays[f"in_{name}_dram"] = a
        aps[name] = nc.dram_tensor(f"in_{name}_dram", a.shape, _mybir.dt.from_np(a.dtype), kind="ExternalInput").ap()
    o = nc.dram_tensor("out_0_dram", (1, 256, 1024), F32, kind="ExternalOutput").ap()
    program(nc, aps, o)
    r = _run(nc, [arrays], core_ids=[0])
    return r.results[0]["out_0_dram"]
```

```python
from contextlib import ExitStack

import numpy as np

import concourse.bass as bass
from concourse import mybir

ALU = mybir.AluOpType
ACT = mybir.ActivationFunctionType
AX = mybir.AxisListType.X
F32 = mybir.dt.float32
F32R = mybir.dt.float32r
I32 = mybir.dt.int32
U32 = mybir.dt.uint32

R = 4
SLOTS = 64
NBLK = 256 // SLOTS
NE = 32
SPARE = 9999.0
WINDOWS = (2, 4, 8, 16)


def tokens(deps):
    out = []
    for d in deps:
        if d is not None:
            out += list(d) if isinstance(d[0], tuple) else [d]
    return out


class Lane:

    def __init__(self, sem):
        self.sem, self.n, self.ops = sem, 0, []

    def do(self, fn, *deps, inc=True):
        if inc:
            self.n += 1
        self.ops.append((fn, tokens(deps), (self.sem, 1) if inc else None))
        return (self.sem, self.n)

    def after(self, fn, *deps):
        return self.do(fn, (self.sem, self.n), *deps)

    def dma(self, fn, flag, *deps):
        flag[1] += 16
        self.ops.append((fn, tokens(deps), (flag[0], 16)))
        return (flag[0], flag[1])

    def wait(self, *deps):
        self.ops.append((None, tokens(deps), None))

    def play(self, eng, seen=None):
        seen = {} if seen is None else seen
        for fn, deps, up in self.ops:
            for sem, val in deps:
                if val > seen.get(sem.name, 0):
                    eng.wait_ge(sem, val)
                    seen[sem.name] = val
            if fn is not None:
                ins = fn(eng)
                if up is not None:
                    ins.then_inc(up[0], up[1])


def constants():
    p = np.arange(128)
    out = {}
    out["ident"] = np.eye(128)
    out["sel"] = np.repeat((p[:, None] % 32 == 0) * 1.0, 128, axis=1)
    out["nhalf"] = np.full((128, 1), -0.5)
    out["eps"] = np.full((128, 1), 1e-6)
    out["incl"] = (p[:, None] <= p[None, :]) * 1.0
    out["strict"] = (p[:, None] < p[None, :]) * 1.0
    out["ones"] = np.ones((128, 128))
    masks = []
    for level in range(7):
        b = 1 << level
        same = (p[:, None] // (2 * b)) == (p[None, :] // (2 * b))
        masks.append(same & ((p[:, None] // b) % 2 == 0) & ((p[None, :] // b) % 2 == 1))
    out["masks"] = np.concatenate(masks, axis=1) * 1.0
    i = np.arange(256)
    rel = (i[None, :] - p[:, None]).astype(np.float64)
    dec = []
    for h in range(4):
        lg = np.log1p(-(2.0 ** (-5.0 - h)))
        dec.append(np.where(rel >= 0, np.exp(lg * np.maximum(rel, 0)), 0.0) * 128.0 ** -0.5)
    out["decay"] = np.concatenate(dec, axis=1)
    freq = np.float32(10000.0) ** (-np.arange(0, 128, 2, dtype=np.float32) / np.float32(128))
    out["freq"] = np.tile(freq[None], (128, 1))
    out["rev4"] = np.tile(np.arange(4, 0, -1)[None], (128, 1))
    out["rev8"] = np.tile(np.arange(8, 0, -1)[None], (128, 1))
    out["places"] = np.tile((np.arange(128) % SLOTS)[None], (128, 1))
    out["ids"] = np.stack([p, p + 128, p + 256, p + 384], axis=1) - SPARE
    out["half"] = (p[:, None] >= SLOTS) * 1.0 + 2 * SPARE
    return {k: np.ascontiguousarray(v, np.float32) for k, v in out.items()}


def late_constants():
    s = np.arange(128)[:, None]
    t = np.arange(256)[None, :]
    parts = []
    for w in WINDOWS:
        count = np.minimum(t + 1, w)
        band = np.where((t - s >= 0) & (t - s < w), 1.0 / count, 0.0) - (t == s)
        u = t[:, 128:]
        own = np.where((u - (s + 128) >= 0) & (u - (s + 128) < w), 1.0 / w, 0.0) - (u == s + 128)
        parts += [band, own]
    return np.ascontiguousarray(np.concatenate(parts, axis=1), np.float32)


def layout():
    at, out = 0, {}
    for k, v in constants().items():
        out[k] = (at, v.shape[1])
        at += v.shape[1]
    return out, at


def program(nc, I, out):
    where, n_const = layout()
    ctx = ExitStack()
    with ctx:
        def sb(name, shape, dt=F32):
            return ctx.enter_context(nc.sbuf_tensor(name, shape, dt))

        def sem(name):
            return ctx.enter_context(nc.semaphore(name))

        C = sb("consts", [128, 258])
        vrow = sb("vrow", [128, 1024])
        ring = sb("ring", [128, R, 4096])
        X = sb("X", [128, 2, 1024])
        gates = sb("gates", [128, 2, 1024])
        MX = sb("MX", [128, 2, 1024])
        S = sb("S", [128, 3250])
        posi = sb("posi", [128, 2], I32)
        idx = sb("idx", [128, 2, 128], U32)
        flag_i = sb("flag_i", [128, 1], I32)

        room_a = ctx.enter_context(ExitStack())

        def sa(name, shape):
            return room_a.enter_context(nc.sbuf_tensor(name, shape, F32))

        arena = sa("arena", [128, 3, 4096])
        proj = sa("proj", [128, 5, 2, 512])
        RQ = sa("RQ", [128, 8, 256])
        hT = sa("hT", [128, 8, 256])
        CB = sa("consts2", [128, n_const - 258])
        part_ = sa("part", [128, 2, 512])
        stacks = sa("stacks", [128, 3, 128])
        AB = sa("AB", [128, 8, 8])
        WR = sa("WR", [128, 8, 36])
        g2x = hT[:, 0:2, :].rearrange("p a b -> p (a b)")
        pool_ = arena[:, :, :].rearrange("p a b -> p (a b)")
        D9 = [pool_[:, 1024 * i:1024 * i + 1024].rearrange("p (n h i) -> p n h i", n=2, h=4) for i in range(9)]
        D, LT, XM, XT = D9[0:5], D9[5:7], D9[7], D9[8]
        qkv = pool_[:, 9216:12288].rearrange("p (m t) -> p m t", m=12)
        PS = [ctx.enter_context(nc.psum_tensor(f"ps{i}", [128, 512], F32)) for i in range(8)]

        def cst(name):
            a, n = where[name]
            return C[:, a:a + n] if a < 258 else CB[:, a - 258:a - 258 + n]

        ident, incl, strict, ones = cst("ident"), cst("incl"), cst("strict"), cst("ones")
        eps = cst("eps")

        s_at = [0]

        def small(n):
            a = s_at[0]
            s_at[0] += n

            assert s_at[0] <= 3250
            return S[:, a:a + n]

        pe, ve, ac, po, sp = (Lane(sem(n)) for n in ("pe_n", "ve_n", "ac_n", "po_n", "sp_n"))

        def flag(name):
            return [sem(name), 0]

        def both(a, b):
            return (a, b)

        free = [None] * 8
        turn = [0]

        kept = set()

        def bank():
            while turn[0] % 8 in kept:
                turn[0] += 1
            b = turn[0] % 8
            turn[0] += 1
            return b, PS[b], free[b]

        slots = [ring[:, i, :] for i in range(R)] + [arena[:, i, :] for i in range(3)]
        slot_flag = [flag(f"slot{i}") for i in range(R + 3)]
        half_flag = [flag(f"half{i}") for i in range(R + 3)]
        last_read, first_read = [None] * (R + 3), [None] * (R + 3)
        rota = list(range(R))
        held = []
        at_slot = [0]

        def unit(src, cols, inner, *deps):
            s = rota[at_slot[0] % len(rota)]
            at_slot[0] += 1
            held.append(s)
            dst = slots[s][:, 0:cols].rearrange("p (a b) -> p a b", b=inner)
            return dst, sp.dma(lambda e: e.dma_start(dst, src), slot_flag[s], last_read[s], *deps)

        def halves(*srcs):
            ss_, views, toks = [], [], []
            for src in srcs:
                s = rota[at_slot[0] % len(rota)]
                at_slot[0] += 1
                held.append(s)
                ss_.append(s)
                views.append(slots[s].rearrange("p (a b) -> p a b", b=src.shape[2]))
            for s, src, v in zip(ss_, srcs, views):
                a = src.shape[1] // 2
                toks.append([sp.dma(lambda e, v=v, src=src, a=a: e.dma_start(v[:, 0:a, :], src[:, 0:a, :]), half_flag[s],
                                    first_read[s])])
            for s, src, v, tk in zip(ss_, srcs, views, toks):
                a = src.shape[1] // 2
                tk.append(sp.dma(lambda e, v=v, src=src, a=a: e.dma_start(v[:, a:, :], src[:, a:, :]), slot_flag[s], last_read[s]))
            return list(zip(views, toks))

        def consumed(t, first=None):
            s = held.pop(0)
            last_read[s], first_read[s] = t, first or t

        f_e, f_st, f_c, f_x, f_v = flag("f_e"), flag("f_st"), flag("f_c"), flag("f_x"), flag("f_v")

        def load(flag_, dst, src, *deps):
            return ac.dma(lambda e: e.dma_start(dst, src), flag_, *deps)

        t_e = load(f_e, C[:, :], I["consts"][:, 0:258])
        load(f_st, stacks[48:56, 0, :], I["c"].rearrange("l (m p) -> (l m) p", p=128))
        load(f_st, stacks[0:48, 0, :], I["conv_w"].rearrange("l k (m p) -> (l k m) p", p=128))
        load(f_st, stacks[56:104, 0, :], I["b_ada"].rearrange("l (m p) -> (l m) p", p=128))
        load(f_st, stacks[104:112, 0, :], I["norm1_w"].rearrange("l (m p) -> (l m) p", p=128))
        t_st = load(f_st, stacks[112:120, 0, :], I["norm2_w"].rearrange("l (m p) -> (l m) p", p=128))
        t_xl = load(f_x, X[:, :, :], I["x"].rearrange("b (n p) d -> p (b n) d", p=128))
        dnw, alog, dtb, rb = small(128), small(4), small(4), small(36)
        by_row = small(24).rearrange("p (a c) -> p a c", a=3)

        half = cst("nhalf")

        def rsqrt(dst, src, scale, eps_val, tmp, *deps):
            m, y, t = tmp
            k = half.to_broadcast([128, src.shape[1]])
            po.after(lambda e: e.tensor_scalar(m, src, scale, eps_val, ALU.mult, ALU.add), *deps)
            t1 = po.after(lambda e: e.tensor_tensor(y, m, k, ALU.pow), t_e)
            ve.after(lambda e: e.tensor_tensor(t, y, y, ALU.mult), t1)
            ve.after(lambda e: e.tensor_tensor(t, t, m, ALU.mult))
            ve.after(lambda e: e.tensor_scalar(t, t, -0.5, 1.5, ALU.mult, ALU.add))
            return ve.after(lambda e: e.tensor_tensor(dst, y, t, ALU.mult))

        ss, rr = small(16), small(16)
        tms = [[small(8) for _ in range(3)] for _ in range(2)]

        def row_norm(n, src, junk, *deps):
            t = ac.after(lambda e: e.activation(junk, src, ACT.Square, accum_out=ss[:, n:n + 1]), *deps)
            return rsqrt(rr[:, n:n + 1], ss[:, n:n + 1], 1.0 / 1024, 1e-6, [q[:, 0:1] for q in tms[n]], t)

        def turned(src, n, *deps):
            out = []
            for g in range(2):
                b, ps, fr = bank()
                kept.add(b)
                for c in range(4):
                    t = pe.do(lambda e, ps=ps, c=c, g=g: e.transpose(
                        ps[:, c * 128:(c + 1) * 128], src[:, (4 * g + c) * 128:(4 * g + c + 1) * 128], ident),
                        fr, *deps, inc=(c == 3))
                out.append((b, ps, t))
            return out

        def turn_rows(dst, src, n, scale, shift, *deps, banks=None):
            toks = []
            for g, (b, ps, t) in enumerate(banks or turned(src, n, *deps)):
                kept.discard(b)
                wait = deps if banks else ()
                d = dst[:, 4 * g:4 * g + 4, n * 128:(n + 1) * 128]
                q = ps[:, :].rearrange("p (c t) -> p c t", c=4)
                if scale is None:
                    t = ac.do(lambda e, d=d, q=q: e.copy(d, q), t)
                    free[b] = t
                    toks.append(t)
                    continue
                for c in range(4):
                    m = 4 * g + c
                    if shift is None and g == 0:
                        u = ac.do(lambda e, d=d, q=q, c=c, m=m: e.activation(d[:, c, :], q[:, c, :], ACT.Copy, scale=scale[:, m:m + 1]), t,
                                  *wait)
                    elif shift is None:
                        u = ve.do(lambda e, d=d, q=q, c=c, m=m: e.tensor_scalar(d[:, c, :], q[:, c, :], scale[:, m:m + 1], None,
                                                            ALU.mult), t, *wait)
                    elif g == 0:
                        u = ac.do(lambda e, d=d, q=q, c=c, m=m: e.activation(d[:, c, :], q[:, c, :], ACT.Identity,
                                                         scale=scale[:, m:m + 1], bias=shift[:, m:m + 1]), t, *wait)
                    else:
                        u = ve.do(lambda e, d=d, q=q, c=c, m=m: e.tensor_scalar(d[:, c, :], q[:, c, :], scale[:, m:m + 1],
                                                            shift[:, m:m + 1], ALU.mult, ALU.add), t, *wait)
                    toks.append(u)
                free[b] = toks[-1]
            return toks

        def tokens_by(acts, w, t_w, col, width, ps, fr, deps, chunks=8):
            for k in range(chunks):
                a = acts(k)
                t = pe.do(lambda e, k=k, a=a: e.matmul(ps[:, 0:width], a, w[:, k, col:col + width],
                                                  start=(k == 0), stop=(k == chunks - 1)),
                          t_w, fr, *deps, inc=(k == chunks - 1))
            return t

        cols = small(120)
        t = pe.do(lambda e: e.transpose(PS[0][:, 0:120], stacks[0:120, 0, :], ident[0:120, 0:120]), t_e, t_st)
        t = free[0] = ve.do(lambda e: e.tensor_copy(cols, PS[0][:, 0:120]), t)
        turn[0] = 1
        ccol = small(8)
        t = ac.do(lambda e: e.activation(ccol, cols[:, 48:56], ACT.Silu), t)
        crep = small(256).rearrange("p (a b) -> p a b", a=8)
        t_crep = ve.after(lambda e: e.tensor_copy(crep, ccol.unsqueeze(2).to_broadcast([128, 8, 32])), t)

        for n in range(2):
            row_norm(n, X[:, n, :], MX[:, n, :], t_xl)
            t_h = ve.after(lambda e, n=n: e.tensor_scalar(MX[:, n, :], X[:, n, :], rr[:, n:n + 1], None, ALU.mult))

        w_ada = I["w_ada"][0, :, :].rearrange("(c p) n -> p c n", p=128)
        w_in = I["w_in"][0, :, :].rearrange("(c p) n -> p c n", p=128)
        part = [part_[:, n, :] for n in range(2)]
        modc = small(32).rearrange("p (a c) -> p a c", a=4)
        modr = small(16).rearrange("p (a c) -> p a c", a=2)
        sel = cst("sel")
        t_part, t_sum, t_mod = [None, None], [None, None], [None] * 12

        def ada(j):
            w, t_w = unit(w_ada[:, :, 512 * j:512 * j + 512], 4096, 512, t_st if j == 1 else None)
            b, ps, fr = bank()
            for k in range(2):
                for q in range(4):
                    t = pe.do(lambda e, k=k, q=q: e.matmul(ps[32 * q:32 * q + 32, :], crep[:, 4 * k + q, :],
                                                 w[:, 4 * k + q, :], start=(k == 0), stop=(k == 1)),
                              t_w, fr, t_crep, inc=(k == 1 and q == 3))
            consumed(t)
            pt = part[j % 2]
            free[b] = t_p_ = ac.do(lambda e: e.copy(pt, ps[:, :]), t, t_sum[j % 2])

            def total():
                seg = j // 2
                b, ps, fr = bank()
                if seg in (2, 5):
                    g = gates[:, seg // 3, 512 * (j % 2):512 * (j % 2) + 512]
                    t = t_sum[j % 2] = pe.do(lambda e, ps=ps: e.matmul(ps[:, :], sel, pt, start=True, stop=True), t_p_, fr)
                    free[b] = t_mod[j] = ve.do(lambda e, ps=ps: e.tensor_tensor(g, ps[:, :], g, ALU.add), t, t_v)
                    return
                o = 4 * (j % 2)
                for c in range(4):
                    t = pe.do(lambda e, ps=ps, c=c: e.matmul(ps[:, c:c + 1], pt[:, 128 * c:128 * c + 128], sel[:, 0:1],
                                                 start=True, stop=True), t_p_, fr)
                t_sum[j % 2] = t
                s4 = (0, 1, None, 2, 3, None)[seg]
                free[b] = t_mod[j] = ve.do(lambda e, ps=ps: e.tensor_tensor(
                    modc[:, s4, o:o + 4], ps[:, 0:4], cols[:, 56 + 8 * seg + o:60 + 8 * seg + o], ALU.add), t)
                if seg >= 3:
                    b, ps, fr = bank()
                    r0 = 64 * (j % 2)
                    view = pt.rearrange("k (p c) -> k c p", c=8)
                    for c in range(8):
                        t = pe.do(lambda e, ps=ps, c=c: e.matmul(ps[r0:r0 + 64, c:c + 1], view[:, c, :], sel[:, 0:1],
                                                     start=True, stop=True), fr)
                    t_sum[j % 2] = t
                    free[b] = t_mod[j] = ve.do(lambda e, ps=ps: e.tensor_tensor(
                        modr[r0:r0 + 64, seg - 3, :], ps[r0:r0 + 64, 0:8], by_row[r0:r0 + 64, seg - 3, :],
                        ALU.add), t, t_v)
            return total

        for j in range(4):
            tot = ada(j)
            if j:
                prev()
            prev = tot
            if j == 1:
                x_turned = [turned(MX[:, n, :], n, t_h) for n in range(2)]
        prev()
        t_a1 = ve.after(lambda e: e.scalar_tensor_tensor(modc[:, 1, :], modc[:, 1, :], 1.0, cols[:, 104:112],
                                                         ALU.add, ALU.mult))
        t_hT = []
        for n in range(2):
            t_hT += turn_rows(hT, MX[:, n, :], n, modc[:, 1, :], modc[:, 0, :], t_h, t_a1,
                              banks=x_turned[n])

        def mid(ap, n=2):
            return ap.unsqueeze(1).to_broadcast([128, n, ap.shape[1]])

        def v4(ps):
            return ps[:, :].rearrange("p (h i) -> p h i", h=4)

        def four(lhs, rhs, *deps):
            b, ps, fr = bank()
            for h in range(4):
                a, m = lhs(h), rhs(h)
                t = pe.do(lambda e, a=a, m=m, h=h: e.matmul(ps[:, h * 128:(h + 1) * 128], a, m,
                                             start=True, stop=True), fr, *deps, inc=(h == 3))
            return b, ps, t

        def four_turned(src, *deps):
            b, ps, fr = bank()
            for h in range(4):
                a = src(h)
                t = pe.do(lambda e, a=a, h=h: e.transpose(ps[:, h * 128:(h + 1) * 128], a, ident), fr, *deps, inc=(h == 3))
            return b, ps, t

        def heads_bc(ap):
            return ap.unsqueeze(2).to_broadcast([128, 4, 128])

        def load_sp(flag_, dst, src):
            return sp.dma(lambda e: e.dma_start(dst, src), flag_)

        first_block = unit(w_in[:, :, 2048:2560], 4096, 512)
        t_c = load_sp(f_c, CB[:, :], I["consts"][:, 258:n_const])
        load_sp(f_v, AB[:, :, :], I["w_in"][0, :, 4096:4104].rearrange("(c p) n -> p c n", p=128))
        load_sp(f_v, dnw, I["dn_norm_w"][0, :].partition_broadcast(128))
        load_sp(f_v, alog, I["a_log"][0, :].partition_broadcast(128))
        load_sp(f_v, dtb, I["dt_bias"][0, :].partition_broadcast(128))
        sp.dma(lambda e: e.dma_start(posi[:, :], I["positions"].rearrange("b (n p) -> p (b n)", p=128),
                                     allow_slow_non_contiguous=True), f_v)
        load_sp(f_v, gates[:, 0, :], I["b_ada"][0, 2048:3072].partition_broadcast(128))
        load_sp(f_v, gates[:, 1, :], I["b_ada"][0, 5120:6144].partition_broadcast(128))
        load_sp(f_v, by_row[:, 0, :], I["b_ada"][0, 3072:4096].rearrange("(p c) -> p c", c=8))
        load_sp(f_v, by_row[:, 1, :], I["b_ada"][0, 4096:5120].rearrange("(p c) -> p c", c=8))
        load_sp(f_v, by_row[:, 2, :], I["norm2_w"][0, :].rearrange("(p c) -> p c", c=8))
        load_sp(f_v, WR[:, :, 0:4], I["w_group"][0].rearrange("(c p) n -> p c n", p=128))
        load_sp(f_v, WR[:, :, 4:36], I["w_expert"][0].rearrange("(c p) n -> p c n", p=128))
        load_sp(f_v, rb[:, 0:4], I["b_group"][0, :].partition_broadcast(128))
        load_sp(f_v, rb[:, 4:36], I["b_expert"][0, :].partition_broadcast(128))
        cw2 = I["ffn_conv_w_2"].rearrange("l k (m p) -> (l k m) p", p=128)
        load_sp(f_v, stacks[0:96, 1, :], cw2[0:96, :])
        load_sp(f_v, stacks[0:36, 2, :], cw2[96:132, :])
        load_sp(f_v, stacks[36:80, 2, :], I["ffn_conv_b_2"].rearrange("l (m p) -> (l m) p", p=128))
        load_sp(f_v, stacks[80:88, 2, :], I["norm_mix_g_2"].rearrange("l (m p) -> (l m) p", p=128))
        t_v = load_sp(f_v, stacks[88:96, 2, :], I["norm_ffn_g_2"].rearrange("l (m p) -> (l m) p", p=128))

        t_qkv = []

        def delta_project(seg):
            w, t_w = unit(w_in[:, :, 2048 + 512 * seg:2560 + 512 * seg], 4096, 512) if seg else first_block
            for m in range(4):
                b, ps, fr = bank()
                for k in range(8):
                    t = pe.do(lambda e, ps=ps, k=k, m=m: e.matmul(
                        ps[:, 0:256], w[:, k, m * 128:(m + 1) * 128], hT[:, k, :],
                        start=(k == 0), stop=(k == 7)), t_w, fr, *t_hT, inc=(k == 7))
                y = qkv[:, 4 * seg + m, :]
                tap = [cols[:, 12 * q + 4 * seg + m:12 * q + 4 * seg + m + 1] for q in range(4)]
                t = ve.do(lambda e, y=y, ps=ps, tap=tap: e.tensor_scalar(y, ps[:, 0:256], tap[3], None, ALU.mult), t)
                for q in (2, 1, 0):
                    o = 3 - q
                    t = ve.after(lambda e, y=y, ps=ps, tap=tap, q=q, o=o: e.scalar_tensor_tensor(
                        y[:, o:256], ps[:, 0:256 - o], tap[q], y[:, o:256], ALU.mult, ALU.add))
                free[b] = t
                t_qkv.append(ac.do(lambda e, y=y: e.activation(y, y, ACT.Silu), t))
            consumed((pe.sem, pe.n))

        delta_project(0)
        delta_project(1)

        SQ = MX[:, :, :].rearrange("p n (a t) -> p (n a) t", t=256)
        t_sq = ac.do(lambda e: e.activation(SQ, qkv[:, 0:8, :], ACT.Square), *t_qkv[0:8], *t_hT)
        b, ps_ab, fr = bank()
        for n in range(2):
            for k in range(8):
                t = pe.do(lambda e, k=k, n=n: e.matmul(
                    ps_ab[:, 8 * n:8 * n + 8], hT[:, k, n * 128:(n + 1) * 128], AB[:, k, :],
                    start=(k == 0), stop=(k == 7)), t_v, fr, inc=(k == 7))
        ab = small(16).rearrange("p (n h) -> p n h", n=2)
        free[b] = t = ve.do(lambda e: e.tensor_copy(ab, ps_ab[:, 0:16].rearrange("p (n h) -> p n h", n=2)), t)

        def s8():
            return small(8).rearrange("p (n h) -> p n h", n=2)

        z, az, gl, beta, ea, GC, EG, BE = (s8() for _ in range(8))
        eal = small(4)
        t = ve.after(lambda e: e.tensor_tensor(z, ab[:, :, 0:4], mid(dtb), ALU.add), t_v)
        ac.do(lambda e: e.activation(eal, alog, ACT.Exp), t_v)
        ac.do(lambda e: e.activation(ea, ab[:, :, 4:8], ACT.Exp, scale=-1.0), t)
        t = ac.do(lambda e: e.activation(az, z, ACT.Abs), t)
        t = ac.after(lambda e: e.activation(az, az, ACT.Exp, scale=-1.0))
        t = ve.after(lambda e: e.tensor_scalar(az, az, 1.0, None, ALU.add), t)
        t = ac.do(lambda e: e.activation(az, az, ACT.Ln), t)
        ve.after(lambda e: e.tensor_scalar(z, z, 0.0, None, ALU.max))
        ve.after(lambda e: e.tensor_tensor(z, z, az, ALU.add), t)
        ve.after(lambda e: e.scalar_tensor_tensor(gl, z, -1.0, mid(eal), ALU.mult, ALU.mult))
        ve.after(lambda e: e.tensor_scalar(ea, ea, 1.0, None, ALU.add))
        t_g = ve.after(lambda e: e.reciprocal(beta, ea))
        heads = "p (n h i) -> p n h i"
        GR = RQ[:, 0:4, :].rearrange("p a b -> p (a b)").rearrange(heads, n=2, h=4)
        BR = RQ[:, 4:8, :].rearrange("p a b -> p (a b)").rearrange(heads, n=2, h=4)
        for n in range(2):
            po.do(lambda e, n=n: e.tensor_copy(GR[:, n], heads_bc(gl[:, n, :])), t_g)
            t_gr = po.do(lambda e, n=n: e.tensor_copy(BR[:, n], heads_bc(beta[:, n, :])), t_g)

        def norm_sums(m):
            b, ps, fr = bank()
            t = pe.do(lambda e: e.matmul(ps[:, :], ones, SQ[:, 2 * m:2 * m + 2, :], start=True, stop=True), t_sq, fr)
            v2 = SQ[:, 2 * m:2 * m + 2, :]
            free[b] = ac.do(lambda e: e.activation(
                v2, ps[:, :].rearrange("p (a t) -> p a t", a=2), ACT.Ln, bias=eps), t)

        for m in (2, 3, 0, 1):
            norm_sums(m)
            if m in (3, 1):
                h4 = slice(0, 4) if m == 1 else slice(4, 8)
                t = ac.after(lambda e, h4=h4: e.activation(SQ[:, h4, :], SQ[:, h4, :], ACT.Exp, scale=-0.5))
                c0 = 128.0 ** -0.5 if m == 1 else 1.0
                t_qk = ve.do(lambda e, c0=c0, h4=h4: e.scalar_tensor_tensor(qkv[:, h4, :], qkv[:, h4, :], c0, SQ[:, h4, :],
                                                              ALU.mult, ALU.mult), t)
                if m == 3:
                    t_kn = t_qk

        delta_project(2)

        DEC, BT, ATT, AT, PM = D
        b, ps, fr = bank()
        for n in range(2):
            t = pe.do(lambda e, ps=ps, n=n: e.matmul(ps[:, 4 * n:4 * n + 4], incl, gl[:, n, :], start=True, stop=True), t_gr, fr)
        free[b] = t = ve.do(lambda e, ps=ps: e.tensor_copy(GC, ps[:, 0:8].rearrange("p (n h) -> p n h", n=2)), t)
        t = ac.do(lambda e: e.activation(EG, GC, ACT.Exp), t)
        t_be = ve.after(lambda e: e.tensor_tensor(BE, EG, beta, ALU.mult), t)
        t_dec, t_bt = [], []
        for n in range(2):
            b, ps, t = four(lambda h, n=n: GR[:, n, h, :], lambda h: incl, t_gr)
            for h in range(4):
                t = ve.do(lambda e, ps=ps, n=n, h=h: e.tensor_scalar(
                    DEC[:, n, h, :], ps[:, h * 128:(h + 1) * 128], GC[:, n, h:h + 1], 0.0,
                    ALU.subtract, ALU.min), t, t_be)
            free[b] = t
            t = ac.do(lambda e, n=n: e.activation(DEC[:, n], DEC[:, n], ACT.Exp), t)
            t_dec.append(po.do(lambda e, n=n: e.tensor_tensor(DEC[:, n], DEC[:, n], mid(incl, 4), ALU.mult), t))
        t_seg = [[None, None] for _ in range(5)]
        t_rot = {}
        R_ = {}

        def project(seg, col, func):
            def half(n):
                if n == 0:
                    R_["w"] = unit(w_in[:, :, col:col + 512], 4096, 512)
                w, t_w = R_["w"]
                b, ps, fr = bank()
                t = tokens_by(lambda k: hT[:, k, n * 128:(n + 1) * 128], w, t_w, 0, 512, ps, fr, t_hT)
                free[b] = t_seg[seg][n] = ac.do(lambda e: e.activation(proj[:, seg, n, :], ps[:, :], func), t)
                if n == 1:
                    consumed(t)
                if seg < 2:
                    rotate(seg, n)
                if seg == 4:
                    pv = proj[:, 4, n, :].rearrange("p (h d) -> p h d", h=4)
                    t_seg[4][n] = po.do(lambda e: e.tensor_tensor(pv, pv, mid(dnw, 4), ALU.mult), t_seg[4][n], t_v)
            return [lambda: half(0), lambda: half(1)]

        ang, kk_, cs, sn = (small(128).rearrange("p (n f) -> p n f", n=2) for _ in range(4))
        posf = small(2)
        po.do(lambda e: e.tensor_copy(posf, posi[:, :]), t_v)
        for n in range(2):
            po.after(lambda e, n=n: e.tensor_scalar(ang[:, n, :], cst("freq"), posf[:, n:n + 1], None, ALU.mult), t_c)
        MAGIC = 12582912.0
        C1, C2 = 6.28125, 0.0019350051879882812
        C3 = float(2 * np.pi - C1 - C2)
        po.after(lambda e: e.tensor_scalar(kk_, ang, float(1 / (2 * np.pi)), None, ALU.mult))
        po.after(lambda e: e.tensor_scalar(kk_, kk_, MAGIC, None, ALU.add))
        po.after(lambda e: e.tensor_scalar(kk_, kk_, -MAGIC, None, ALU.add))
        for cc in (C1, C2, C3):
            po.after(lambda e, cc=cc: e.tensor_scalar(cs, kk_, -cc, None, ALU.mult))
            po.after(lambda e: e.tensor_tensor(ang, ang, cs, ALU.add))
        PI = 3.1415925
        t = po.after(lambda e: e.tensor_scalar(ang, ang, PI, -PI, ALU.min, ALU.max))
        t = ac.do(lambda e: e.activation(cs, ang, ACT.Abs), t)
        t = po.after(lambda e: e.tensor_scalar(cs, cs, -1.0, float(np.pi / 2), ALU.mult, ALU.add), t)
        ac.do(lambda e: e.activation(sn, ang, ACT.Sin), t)
        t_sc = ac.do(lambda e: e.activation(cs, cs, ACT.Sin), t)
        room = small(1024)
        rt = [room[:, 256 * i:256 * i + 256].rearrange("p (h f) -> p h f", h=4) for i in range(4)]

        def rotate(seg, n):
            pv = proj[:, seg, n, :].rearrange("p (h a f) -> p h a f", h=4, a=2)
            x1, x2 = pv[:, :, 0, :], pv[:, :, 1, :]
            cb, sb_ = mid(cs[:, n, :], 4), mid(sn[:, n, :], 4)
            for q, (xa, tr) in enumerate(((x1, cb), (x2, sb_), (x2, cb), (x1, sb_))):
                t = po.do(lambda e, xa=xa, tr=tr, q=q: e.tensor_tensor(rt[q], xa, tr, ALU.mult), t_sc, t_seg[seg][n],
                          t_rot.get("last"))
            po.do(lambda e: e.tensor_tensor(x1, rt[0], rt[1], ALU.subtract), t)
            t_rot[seg, n] = t_rot["last"] = po.do(lambda e: e.tensor_tensor(x2, rt[2], rt[3], ALU.add), t)

        t_rq = []

        def turn_rotated(seg):
            for n in range(2):
                b, ps, t = four_turned(lambda h, n=n: proj[:, seg, n, h * 128:(h + 1) * 128], t_rot[seg, n])
                free[b] = ac.do(lambda e, ps=ps, n=n: e.copy(
                    RQ[:, 4 * seg:4 * seg + 4, n * 128:(n + 1) * 128], v4(ps)), t, t_br_used)
                t_rq.append(free[b])
            R_["turned"] = (pe.sem, pe.n)

        WT = proj[:, 0:2, :, :].rearrange("p a n c -> p (a n c)")[:, 0:1536].rearrange("p (h c) -> p h c", h=4)
        dec_r = cst("decay").rearrange("p (h i) -> p h i", h=4)

        def scores(pair):
            for h in pair:
                b, ps, fr = bank()
                pe.do(lambda e, ps=ps, h=h: e.matmul(ps[:, 0:256], RQ[:, 4 + h, 0:128], RQ[:, h, :],
                                         start=True, stop=True), fr, *t_rq, inc=False)
                t = pe.do(lambda e, ps=ps, h=h: e.matmul(ps[:, 256:384], RQ[:, 4 + h, 128:256], RQ[:, h, 128:256],
                                             start=True, stop=True))
                ve.do(lambda e, ps=ps, h=h: e.tensor_tensor(WT[:, h, 0:256], ps[:, 0:256], dec_r[:, h, :], ALU.mult),
                      t, R_["turned"])
                free[b] = R_["wt"] = ve.do(lambda e, ps=ps, h=h: e.tensor_tensor(WT[:, h, 256:384], ps[:, 256:384],
                                                                     dec_r[:, h, 0:128], ALU.mult))

        def head_norm(o, n, dst, gate_seg, weight, junk, on, *deps):
            s4, r4 = ss[:, 4 * n + 4:4 * n + 8], rr[:, 4 * n + 4:4 * n + 8]
            t = ac.do(lambda e: e.activation(junk, o, ACT.Square), *deps)
            t = ve.do(lambda e: e.tensor_reduce(s4, junk, AX, ALU.add), t)
            t = rsqrt(r4, s4, 1.0 / 128, 1e-6, [q[:, 4:8] for q in tms[n]], t)
            t = ve.after(lambda e: e.tensor_tensor(o, o, heads_bc(r4), ALU.mult))
            if weight is not None:
                t = on.do(lambda e: e.tensor_tensor(o, o, mid(weight, 4), ALU.mult), t)
            return on.do(lambda e: e.tensor_tensor(
                dst, o, proj[:, gate_seg, n, :].rearrange("p (h d) -> p h d", h=4), ALU.mult),
                t, t_seg[gate_seg][n])

        OR = [room[:, 512 * n:512 * n + 512].rearrange("p (h d) -> p h d", h=4) for n in range(2)]
        t_ret = [None, None]

        def retained(n):
            b, ps, fr = bank()
            for h in range(4):
                hs = slice(h * 128, (h + 1) * 128)
                if n == 0:
                    t = pe.do(lambda e, hs=hs, h=h: e.matmul(ps[:, hs], WT[:, h, 0:128], proj[:, 2, 0, hs],
                                                 start=True, stop=True),
                              fr, R_["wt"], *t_seg[2], inc=(h == 3))
                else:
                    pe.do(lambda e, hs=hs, h=h: e.matmul(ps[:, hs], WT[:, h, 128:256], proj[:, 2, 0, hs],
                                             start=True, stop=False), fr, inc=False)
                    t = pe.do(lambda e, hs=hs, h=h: e.matmul(ps[:, hs], WT[:, h, 256:384], proj[:, 2, 1, hs],
                                                 start=False, stop=True), inc=(h == 3))
            free[b] = t = ac.do(lambda e: e.copy(OR[n], v4(ps)), t, t_rot["last"])
            t_ret[n] = head_norm(OR[n], n, MX[:, n, 0:512].rearrange("p (h d) -> p h d", h=4), 3, None,
                                 MX[:, n, 0:512].rearrange("p (h d) -> p h d", h=4), po, t, t_qk)

        def ada_pair(j):
            def first():
                R_["tot"] = ada(j)

            def second():
                R_["tot"]()
            return [first, second]

        for f in project(2, 1024, ACT.Copy):
            f()
        for n in range(2):
            b, ps, t = four(lambda h, n=n: BR[:, n, h, :], lambda h: ident, t_gr)
            free[b] = ve.do(lambda e, ps=ps, n=n: e.tensor_tensor(BT[:, n], v4(ps), DEC[:, n], ALU.mult), t, t_dec[n])
            t_bt.append(free[b])
        t_br_used = (pe.sem, pe.n)
        t_at, t_att = [], []
        for n in range(2):
            tl = slice(n * 128, (n + 1) * 128)
            b, ps, t = four(lambda h, tl=tl: qkv[:, 4 + h, tl], lambda h, tl=tl: qkv[:, 4 + h, tl], t_kn)
            free[b] = ve.do(lambda e, ps=ps, n=n: e.tensor_tensor(AT[:, n], v4(ps), BT[:, n], ALU.mult), t, t_bt[n])
            t_at.append(free[b])

        KT = small(512).rearrange("p (h d) -> p h d", h=4)
        VBT = qkv[:, 8:12, :].rearrange("p a b -> p (a b)").rearrange(heads, n=2, h=4)
        t_keep = {}

        def by_token():
            b, ps, t = four_turned(lambda h: qkv[:, 4 + h, 0:128], t_kn)
            free[b] = t_keep["kt"] = ac.do(lambda e, ps=ps: e.copy(KT, v4(ps)), t)
            vb_ps = [four_turned(lambda h, n=n: qkv[:, 8 + h, n * 128:(n + 1) * 128], *t_qkv[8:12]) for n in range(2)]
            for n, (b, ps, _) in enumerate(vb_ps):
                t = vb_ps[1][2]
                free[b] = t_keep["vbt"] = ve.do(lambda e, ps=ps, n=n: e.tensor_tensor(
                    VBT[:, n], v4(ps), heads_bc(beta[:, n, :]), ALU.mult), t)

        def queries(n):
            tl = slice(n * 128, (n + 1) * 128)
            b, ps, t = four(lambda h: qkv[:, 4 + h, tl], lambda h: qkv[:, h, tl], t_qk)
            free[b] = ve.do(lambda e: e.tensor_tensor(ATT[:, n], v4(ps), DEC[:, n], ALU.mult), t, t_dec[n])
            t_att.append(free[b])

        more = [by_token, lambda: queries(0), lambda: queries(1)]
        A = {j: ada_pair(j) for j in range(4, 12)}
        more += project(0, 0, ACT.Copy) + project(1, 512, ACT.Copy) + A[4] + A[5]
        more += [lambda: turn_rotated(0), lambda: turn_rotated(1)] + A[6]
        more += [lambda: scores((0, 1)), lambda: scores((2, 3))] + project(3, 1536, ACT.Silu) + A[7]
        more += [lambda: retained(0), lambda: retained(1)] + A[8] + project(4, 3584, ACT.Silu)
        more += A[9] + A[10] + A[11]

        def fill(k):
            for _ in range(k):
                if more:
                    more.pop(0)()

        masks = cst("masks").rearrange("p (l i) -> p l i", l=7)
        t_x, t_xt = [None] * 2, [None] * 2
        t_p = [[None] * 2, [None] * 2]

        def masked(level):
            to = LT[level % 2]
            return [po.do(lambda e, n=n: e.tensor_tensor(
                to[:, n], AT[:, n], mid(masks[:, level, :], 4), ALU.mult), t_at[n], t_p[level % 2][n])
                for n in range(2)]

        t_next = masked(0)
        for level in range(7):
            L2, t_l = LT[level % 2], t_next
            if level == 0:
                idb = mid(ident, 4)
                for n in range(2):
                    b, ps, tq = four(lambda h, L2=L2, n=n: L2[:, n, h, :], lambda h: ident, t_l[n])
                    t_p[0][n] = tq
                    ve.do(lambda e, idb=idb, L2=L2, n=n: e.tensor_tensor(XT[:, n], idb, L2[:, n], ALU.subtract), t_l[n])
                    free[b] = t_x[n] = t_xt[n] = ve.do(lambda e, idb=idb, ps=ps, n=n: e.tensor_tensor(
                        XM[:, n], idb, v4(ps), ALU.subtract), tq)
                    t_p[0][n] = both(tq, t_x[n])
                t_next = masked(1)
                fill(2)
                continue
            prod = []
            for n in range(2):
                b, ps, tq = four(lambda h, L2=L2, n=n: L2[:, n, h, :], lambda h, n=n: XM[:, n, h, :], t_l[n], t_x[n])
                t_p[level % 2][n] = tq
                free[b] = ac.do(lambda e, ps=ps, n=n: e.copy(PM[:, n], v4(ps)), tq, t_xt[n])
                prod.append(free[b])
            if level < 6:
                t_next = masked(level + 1)
            fill(1)
            for n in range(2):
                b2, ps2, tr = four(lambda h, n=n: PM[:, n, h, :], lambda h, n=n: XT[:, n, h, :], prod[n], t_xt[n])
                if level < 6:
                    b1, ps1, tr = four(lambda h, n=n: XT[:, n, h, :], lambda h, n=n: PM[:, n, h, :])
                    free[b1] = t_x[n] = ve.do(lambda e, ps1=ps1, n=n: e.tensor_tensor(
                        XM[:, n], XM[:, n], v4(ps1), ALU.subtract), tr)
                free[b2] = t_xt[n] = ve.do(lambda e, ps2=ps2, n=n: e.tensor_tensor(
                    XT[:, n], XT[:, n], v4(ps2), ALU.subtract), tr)
            fill(2)

        U0, UK = PM[:, 0], PM[:, 1]
        ST, VN = LT[0][:, 0], LT[0][:, 1]
        O0, O1 = OR
        b, ps, t = four(lambda h: XT[:, 0, h, :], lambda h: VBT[:, 0, h, :], t_xt[0], t_xt[1], t_keep["vbt"])
        ve.do(lambda e, ps=ps: e.tensor_copy(U0, v4(ps)), t)
        free[b] = t_uk = ve.do(lambda e, ps=ps: e.tensor_tensor(
            UK, v4(ps), DEC[:, 0, :, 127:128].to_broadcast([128, 4, 128]), ALU.mult), t)
        fill(2)
        b, ps, t = four(lambda h: KT[:, h, :], lambda h: UK[:, h, :], t_uk, t_keep["kt"])
        free[b] = t_stt = ve.do(lambda e, ps=ps: e.tensor_copy(ST, v4(ps)), t)
        b0, ps0, t0 = four(lambda h: ATT[:, 0, h, :], lambda h: U0[:, h, :], t_uk, t_att[0])
        kept.add(b0)
        fill(2)
        b, ps, t = four(lambda h: qkv[:, 4 + h, 128:256], lambda h: ST[:, h, :], t_stt)
        ve.do(lambda e, ps=ps: e.tensor_tensor(VN, v4(ps), heads_bc(BE[:, 1, :]), ALU.mult), t)
        free[b] = t_vn = ve.after(lambda e: e.tensor_tensor(VN, VBT[:, 1], VN, ALU.subtract))
        bq, psq, tq = four(lambda h: qkv[:, h, 128:256], lambda h: ST[:, h, :], t_stt)
        kept.add(bq)
        fill(2)
        b, ps, t = four(lambda h: XT[:, 1, h, :], lambda h: VN[:, h, :], t_vn, t_xt[1])
        U1 = UK
        free[b] = t_u1 = ve.do(lambda e, ps=ps: e.tensor_copy(U1, v4(ps)), t)
        fill(2)
        b1, ps1, t1 = four(lambda h: ATT[:, 1, h, :], lambda h: U1[:, h, :], t_u1, t_att[1])
        kept.add(b1)
        fill(len(more) - 4)
        jn = [XM[:, n] for n in range(2)]
        free[b0] = t0 = ac.do(lambda e: e.copy(O0, v4(ps0)), t0, *t_ret)
        t_mx = [None, None]
        free[bq] = ve.do(lambda e: e.tensor_tensor(O1, v4(psq), heads_bc(EG[:, 1, :]), ALU.mult), tq, *t_ret)
        free[b1] = t1 = ve.after(lambda e, ps1=ps1: e.tensor_tensor(O1, O1, v4(ps1), ALU.add), t1)
        for n, (o, t) in enumerate(((O0, t0), (O1, t1))):
            t_mx[n] = head_norm(o, n, MX[:, n, 512:1024].rearrange("p (h d) -> p h d", h=4), 4, None, jn[n], ve, t)
        kept.clear()
        fill(len(more))

        xs = nc.dram_tensor("rows_scratch", (512, 1024), F32, kind="Internal").ap()
        ys = nc.dram_tensor("pair_scratch", (1024, 512), F32, kind="Internal").ap()
        f_xs = flag("f_xs")
        ve.after(lambda e: e.scalar_tensor_tensor(modr[:, 1, :], modr[:, 1, :], 1.0, by_row[:, 2, :],
                                                  ALU.add, ALU.mult))
        t_a2 = ve.after(lambda e: e.scalar_tensor_tensor(modc[:, 3, :], modc[:, 3, :], 1.0, cols[:, 112:120],
                                                         ALU.add, ALU.mult))
        b, ps, fr = bank()
        for k in range(8):
            t = pe.do(lambda e, ps=ps, k=k: e.matmul(ps[:, 0:36], modc[:, 2, k:k + 1].to_broadcast([128, 128]), WR[:, k, 0:36],
                                         start=(k == 0), stop=(k == 7)), t_v, fr, t_mod[6], t_mod[7], inc=(k == 7))
        free[b] = t_rb = ve.do(lambda e, ps=ps: e.tensor_tensor(rb, rb, ps[:, 0:36], ALU.add), t, t_v)
        w_out = I["w_out"][0, :, :].rearrange("(c p) n -> p c n", p=128)
        w_o2 = [unit(w_out[:, :, 512 * j:512 * j + 512], 4096, 512) for j in range(2)]
        t_x1, t_h2, t_hT, t_hT2 = [None] * 2, [None] * 2, [None] * 2, []
        q0 = at_slot[0]
        done_all = tuple((l.sem, l.n) for l in (pe, ve, ac, po))
        for i in range(3):
            last_read[R + i] = first_read[R + i] = done_all
        rota[:] = [q0 % R, (q0 + 1) % R, R, R + 1, R + 2, (q0 + 2) % R, (q0 + 3) % R]
        at_slot[0] = 0
        t_hT[0] = turn_rows(hT, MX[:, 0, :], 0, None, None, t_mx[0], t_ret[0])
        for n in range(2):
            for j in range(2):
                if j > n:
                    t_hT[1] = turn_rows(hT, MX[:, 1, :], 1, None, None, t_mx[1], t_ret[1])
                w, t_w = w_o2[j]
                js = slice(512 * j, 512 * j + 512)
                b, ps, fr = bank()
                t = tokens_by(lambda k, n=n: hT[:, k, n * 128:(n + 1) * 128], w, t_w, 0, 512, ps, fr, t_hT[n])
                tmp = part_[:, j, :]
                free[b] = ve.after(lambda e, tmp=tmp, ps=ps, js=js: e.tensor_tensor(tmp, ps[:, :], gates[:, 0, js], ALU.mult), t, *t_sum)
                t_x1[n] = ve.after(lambda e, tmp=tmp, n=n, js=js: e.tensor_tensor(X[:, n, js], X[:, n, js], tmp, ALU.add))
                if n:
                    consumed(t)
            if n == 0:
                row_norm(n, X[:, n, :], MX[:, n, :], t_x1[n], *t_hT[n])
        for n in range(2):
            t_hT2 += turn_rows(hT, X[:, n, :], n, modc[:, 3, :], None, t_x1[n], t_a2, (pe.sem, pe.n))
        row_norm(1, X[:, 1, :], MX[:, 1, :], t_x1[1], *t_hT[1])
        t_rr = (ve.sem, ve.n)
        for n in range(2):
            t_h2[n] = ac.do(lambda e, n=n: e.activation(MX[:, n, :], X[:, n, :], ACT.Copy, scale=rr[:, n:n + 1]), t_rr)
            for k in range(2):
                t_xs = ac.dma(lambda e, n=n, k=k: e.dma_start(xs[256 * k + 128 * n:256 * k + 128 * n + 128, :], MX[:, n, :]),
                              f_xs, t_h2[n])
        fold = sel[:, 0:64]
        LE = KT.rearrange("p h d -> p (h d)")[:, 0:256]
        po.do(lambda e: e.memset(LE, 0.0), (pe.sem, pe.n))
        t_fold = po.do(lambda e: e.tensor_tensor(fold, ident[:, 0:64], ident[:, 64:128], ALU.add))
        v_ffn = gates[:, 1, :]
        v_fin, v_psc, v_pb = room, gates[:, 0, :], vrow[:, :]
        f_w = flag("f_w")
        load(f_w, v_fin, I["final_norm_w"].partition_broadcast(128), *t_mx, t_x1[1])
        load(f_w, v_psc, I["pool_scale_2"][0, :].partition_broadcast(128))
        t_w5 = load(f_w, v_pb, I["pool_b_2"][0, :].partition_broadcast(128))

        flat_p = proj[:, :, :, :].rearrange("p a b c -> p (a b c)")
        for i in range(2):
            t_zero = po.do(lambda e, i=i: e.memset(flat_p[:, 1024 * i:1024 * i + 1024], 0.0), *t_mx)

        W = part_[:, :, :].rearrange("p a b -> p (a b)")
        w_at = [0]

        def ws(*shape):
            n = int(np.prod(shape))
            a = w_at[0]
            w_at[0] += n
            v = W[:, a:a + n]
            if len(shape) == 2:
                return v.rearrange("p (a b) -> p a b", a=shape[0])
            if len(shape) == 3:
                return v.rearrange("p (a b c) -> p a b c", a=shape[0], b=shape[1])
            return v

        b, ps_l, fr = bank()
        for k in range(8):
            r0 = 64 * (k % 2)
            t = pe.do(lambda e, ps_l=ps_l, k=k, r0=r0: e.matmul(ps_l[r0:r0 + 36, 0:256], WR[:, k, :], hT[:, k, :],
                                         start=(k < 2), stop=(k > 5)), t_v, fr, *t_hT2, inc=(k > 5))
        L = ws(2, 36)
        for r0 in (0, 64):
            free[b] = t_le = ve.do(lambda e, ps_l=ps_l, r0=r0: e.tensor_copy(LE[r0:r0 + 36, :], ps_l[r0:r0 + 36, 0:256]), t, t_fold)
        b, ps_l, fr = bank()
        for n in range(2):
            t2 = pe.do(lambda e, ps_l=ps_l, n=n: e.matmul(ps_l[:, 64 * n:64 * n + 64], LE[:, 128 * n:128 * n + 128], fold,
                                          start=True, stop=True), t_le, fr)
        for n in range(2):
            free[b] = ve.after(lambda e, ps_l=ps_l, n=n: e.scalar_tensor_tensor(
                L[:, n, :], ps_l[:, 64 * n:64 * n + 36], rr[:, n:n + 1], rb, ALU.mult, ALU.add), t2, t_rb, t_rr)

        def bc(ap, *shape):
            while len(ap.shape) < len(shape) + 1:
                ap = ap.unsqueeze(len(ap.shape))
            return ap.to_broadcast([128, *shape])

        def first_max(v, k, rev):
            m, q, oh, sc, m2 = ws(2, 1), None, ws(2, k), ws(2, k), ws(2, 1)
            ve.after(lambda e: e.tensor_reduce(m[:, :, 0], v, AX, ALU.max))
            ve.after(lambda e: e.tensor_tensor(sc, v, bc(m, 2, k), ALU.is_ge))
            ve.after(lambda e: e.tensor_tensor(sc, sc, mid(rev), ALU.mult))
            ve.after(lambda e: e.tensor_reduce(m2[:, :, 0], sc, AX, ALU.max))
            ve.after(lambda e: e.tensor_tensor(oh, sc, bc(m2, 2, k), ALU.is_equal))
            return m, oh

        lg = L[:, :, 0:4]
        gm, ohg = first_max(lg, 4, cst("rev4"))
        pr = ws(2, 4, 8)
        es, es2 = ws(2, 8), ws(2, 8)
        ohg4 = ohg.unsqueeze(3).to_broadcast([128, 2, 4, 8])
        ve.after(lambda e: e.tensor_tensor(pr, L[:, :, 4:36].rearrange("p n (g e) -> p n g e", g=4), ohg4, ALU.mult))
        ve.after(lambda e: e.tensor_reduce(es, pr.rearrange("p n g e -> p n e g"), AX, ALU.add))
        m1, oh1 = first_max(es, 8, cst("rev8"))
        ve.after(lambda e: e.scalar_tensor_tensor(es2, oh1, -3.0e38, es, ALU.mult, ALU.add))
        m2, oh2 = first_max(es2, 8, cst("rev8"))
        M = [ws(2, 4, 8), ws(2, 4, 8)]
        for k, oh in enumerate((oh1, oh2)):
            ve.after(lambda e, k=k, oh=oh: e.tensor_tensor(M[k], oh.unsqueeze(2).to_broadcast([128, 2, 4, 8]),
                                                           ohg4, ALU.mult))
        SM = ws(2, 32)
        flat = [m.rearrange("p n g e -> p n (g e)") for m in M]
        t_sm = ve.after(lambda e: e.tensor_tensor(SM, flat[0], flat[1], ALU.add))
        b_r, ps_r, fr = bank()
        pe.do(lambda e: e.matmul(ps_r[:, 0:32], strict, SM[:, 0, :], start=True, stop=True), t_sm, fr, inc=False)
        pe.do(lambda e: e.matmul(ps_r[:, 32:64], ones, SM[:, 0, :], start=True, stop=False), inc=False)
        t = pe.do(lambda e: e.matmul(ps_r[:, 32:64], strict, SM[:, 1, :], start=False, stop=True))
        b_n, ps_n, fr = bank()
        pe.do(lambda e: e.matmul(ps_n[:, 0:32], ones, SM[:, 0, :], start=True, stop=False), fr, inc=False)
        t_n = pe.do(lambda e: e.matmul(ps_n[:, 0:32], ones, SM[:, 1, :], start=False, stop=True))
        slot, cnt = ws(2, 2), ws(1)
        rank = ps_r[:, 0:64].rearrange("p (n c) -> p n c", n=2)
        pps = [ws(2, 32), ws(2, 32)]
        for k in range(2):
            free[b_r] = ve.do(lambda e, k=k: e.tensor_tensor(pps[k], flat[k], rank, ALU.mult), t)
        for k in range(2):
            ve.after(lambda e, k=k: e.tensor_reduce(slot[:, k, :], pps[k], AX, ALU.add))
        Q = [KT[:, i, :] for i in range(4)]
        t_q = [None]

        def places(blk):
            b, ps_t, fr = bank()
            if blk:
                ve.after(lambda e: e.tensor_scalar(slot, slot, -float(SLOTS), None, ALU.add))
            for k in range(2):
                for n in range(2):
                    i = 2 * k + n
                    t = ve.do(lambda e, i=i, k=k, n=n: e.tensor_scalar(Q[i], cst("places"), slot[:, k, n:n + 1],
                                                        cst("ids")[:, i:i + 1], ALU.is_equal, ALU.mult),
                              (ve.sem, ve.n), t_q[0])
                    t = pe.do(lambda e, i=i, k=k, n=n: e.matmul(ps_t[:, 0:NE], Q[i], flat[k][:, n, :],
                                                 start=(i == 0), stop=(i == 3)), t, fr)
            t_q[0] = t
            to = [idx[:, j, :].rearrange("p (e b) -> p e b", b=NBLK)[:, :, blk] for j in range(2)]
            ve.do(lambda e: e.tensor_scalar(to[0], ps_t[:, 0:NE], SPARE, None, ALU.add), t)
            free[b] = ve.do(lambda e: e.tensor_scalar(to[1], ps_t[:, 0:NE], 2.0, cst("half"), ALU.mult, ALU.add), t)
            return free[b]

        t_idx = places(0)
        ve.after(lambda e: e.tensor_reduce(cnt, ps_n[:, 0:32], AX, ALU.max), t_n)
        t_flag = ve.after(lambda e: e.tensor_scalar(flag_i[:, :], cnt, SLOTS + 0.5, None, ALU.is_gt))
        free[b_n] = t_flag
        gate = small(4).rearrange("p (k n) -> p k n", k=2)
        eg, zs = ws(2, 4), ws(2, 1)
        e2, den = ws(2, 1), ws(2, 1)
        t = ve.after(lambda e: e.tensor_tensor(eg, lg, bc(gm, 2, 4), ALU.subtract))
        ac.do(lambda e: e.activation(eg, eg, ACT.Exp), t)
        t = ve.after(lambda e: e.tensor_tensor(e2, m2, m1, ALU.subtract))
        t = ac.do(lambda e: e.activation(e2, e2, ACT.Exp), t)
        ve.after(lambda e: e.tensor_reduce(zs[:, :, 0], eg, AX, ALU.add), t)
        ve.after(lambda e: e.reciprocal(zs, zs))
        ve.after(lambda e: e.tensor_scalar(den, e2, 1.0, None, ALU.add))
        ve.after(lambda e: e.reciprocal(den, den))
        ve.after(lambda e: e.tensor_tensor(gate[:, 0, :], zs[:, :, 0], den[:, :, 0], ALU.mult))
        ve.after(lambda e: e.tensor_tensor(gate[:, 1, :], gate[:, 0, :], e2[:, :, 0], ALU.mult))
        assert w_at[0] <= 1024

        XG = [flat_p[64 * (i // 2):64 * (i // 2) + SLOTS, 1024 * (i % 2):1024 * (i % 2) + 1024] for i in range(4)]
        XTe = [flat_p[:, 2048 + 512 * i:2560 + 512 * i].rearrange("p (c s) -> p c s", c=8) for i in range(2)]
        HD = [flat_p[0:SLOTS, 3072 + 512 * i:3584 + 512 * i] for i in range(2)]
        HTe = [flat_p[:, 4096 + 256 * i:4352 + 256 * i].rearrange("p (c s) -> p c s", c=4) for i in range(2)]
        SL = [RQ[0:SLOTS, 2 * i:2 * i + 2, :].rearrange("p a b -> p (a b)") for i in range(2)]
        YS = [MX[:, i // 2, 512 * (i % 2):512 * (i % 2) + 512] for i in range(4)]
        w1, w3, w2 = I["w1"][0], I["w3"][0], I["w2"][0]

        def experts(jobs, lanes, load, done, flags, banks_free, first, aside=None):
            p_, v_, a_, g_ = lanes
            f_g, f_s = flags
            g_tok, y_tok, x_tok, xt_tok, h_tok, hd_tok, ht_tok = {}, {}, {}, {}, {}, {}, {}
            bt = [0]

            def nb():
                b = bt[0] % 8
                bt[0] += 1
                return b, PS[b], banks_free[b]

            def gather(i):
                e_, blk = jobs[i]
                col = e_ * NBLK + blk
                g_tok[i] = g_.dma(lambda e: e.indirect_dma_start(
                    XG[i % 4], None, xs, bass.IndirectOffsetOnAxis(ap=idx[0:SLOTS, 0, col:col + 1], axis=0),
                    bounds_check=511, oob_is_err=False), f_g[i % 4], *first, x_tok.get(i - 4))

            def turn_x(i):
                b, ps, fr = nb()
                src = XG[i % 4].rearrange("s (p c) -> s c p", c=8)
                r0 = 64 * (i % 4 // 2)
                for c in range(8):
                    t = p_.do(lambda e, c=c: e.transpose(ps[:, c * SLOTS:(c + 1) * SLOTS], src[:, c, :],
                                                         ident[r0:r0 + SLOTS, r0:r0 + SLOTS]), fr, g_tok[i], inc=(c == 7))
                x_tok[i] = t
                banks_free[b] = t = v_.do(lambda e: e.tensor_tensor(
                    XTe[i % 2], ps[:, :].rearrange("p (c s) -> p c s", c=8),
                    modr[:, 1, :].unsqueeze(2).to_broadcast([128, 8, SLOTS]), ALU.mult), t, h_tok.get(i - 2))
                xt_tok[i] = v_.do(lambda e: e.tensor_tensor(
                    XTe[i % 2], XTe[i % 2], modr[:, 0, :].unsqueeze(2).to_broadcast([128, 8, SLOTS]), ALU.add), t)

            def up(i):
                (u1, t1), (u3, t3) = load(("w1", "w3"), jobs[i])
                b, ps, fr = nb()
                for k in range(8):
                    p_.do(lambda e, k=k: e.matmul(ps[0:SLOTS, :], XTe[i % 2][:, k, :], u1[:, k, :],
                                                  start=(k == 0), stop=(k == 7)), fr, xt_tok[i], t1[k // 4], inc=False)
                    t = p_.do(lambda e, k=k: e.matmul(ps[64:64 + SLOTS, :], XTe[i % 2][:, k, :], u3[:, k, :],
                                                      start=(k == 0), stop=(k == 7)), t3[k // 4], inc=(k % 4 == 3))
                    if k == 3:
                        first_h = t
                h_tok[i] = t
                done(t, first_h)
                done(t, first_h)
                t = a_.do(lambda e: e.activation(SL[i % 2], ps[0:SLOTS, :], ACT.Silu), t, hd_tok.get(i - 2))
                banks_free[b] = hd_tok[i] = v_.do(lambda e: e.tensor_tensor(
                    HD[i % 2], SL[i % 2], ps[64:64 + SLOTS, :], ALU.mult), t, ht_tok.get(("pe", i - 2)))

            def turn_h(i):
                b, ps, fr = nb()
                src = HD[i % 2].rearrange("s (p c) -> s c p", c=4)
                for c in range(4):
                    t = p_.do(lambda e, c=c: e.transpose(ps[:, c * SLOTS:(c + 1) * SLOTS], src[:, c, :],
                                                         ident[0:SLOTS, 0:SLOTS]), fr, hd_tok[i], inc=(c == 3))
                ht_tok["pe", i] = t
                banks_free[b] = ht_tok[i] = v_.do(lambda e: e.tensor_copy(
                    HTe[i % 2], ps[:, 0:4 * SLOTS].rearrange("p (c s) -> p c s", c=4)), t, y_tok.get(("pe", i - 2)))

            def down(i):
                e_, blk = jobs[i]
                col = e_ * NBLK + blk
                (u2, t2), = load(("w2",), jobs[i])
                b, ps, fr = nb()
                for k in range(4):
                    p_.do(lambda e, k=k: e.matmul(ps[0:SLOTS, :], HTe[i % 2][:, k, :], u2[:, k, 0:512],
                                                  start=(k == 0), stop=(k == 3)), fr, ht_tok[i], t2[k // 2], inc=False)
                    t = p_.do(lambda e, k=k: e.matmul(ps[64:64 + SLOTS, :], HTe[i % 2][:, k, :], u2[:, k, 512:1024],
                                                      start=(k == 0), stop=(k == 3)), inc=(k % 2 == 1))
                    if k == 1:
                        first_h = t
                y_tok["pe", i] = t
                done(t, first_h)
                banks_free[b] = t = v_.do(lambda e: e.tensor_tensor(YS[i % 4], ps[:, :], g2x[:, :], ALU.mult),
                                          t, y_tok.get(i - 4), *(first if i < 4 else ()))
                y_tok[i] = g_.dma(lambda e: e.indirect_dma_start(
                    ys, bass.IndirectOffsetOnAxis(ap=idx[:, 1, col:col + 1], axis=0), YS[i % 4], None,
                    bounds_check=1023, oob_is_err=False), f_s[i % 4], t)

            N = len(jobs)
            for i in range(4):
                gather(i)
            turn_x(0)
            up(0)
            turn_x(1)
            for i in range(N):
                if i + 1 < N:
                    up(i + 1)
                turn_h(i)
                if i + 2 < N:
                    turn_x(i + 2)
                if i + 4 < N:
                    gather(i + 4)
                down(i)
                if aside and i == 3:
                    aside()
            return [y_tok[i] for i in range(N - 4, N)]

        fcol = small(192)
        for i in range(2):
            t_g2 = ve.do(lambda e, i=i: e.tensor_copy(g2x[64 * i:64 * i + 64, :], gates[64 * i:64 * i + 64, 1, 512 * i:512 * i + 512]),
                  (ve.sem, ve.n), t_idx)

        t_aside = {}

        def aside():
            b, ps, fr = bank()
            pe.do(lambda e: e.transpose(ps[:, 0:96], stacks[0:96, 1, :], ident[0:96, 0:96]), fr, t_v, inc=False)
            t = pe.do(lambda e: e.transpose(ps[:, 96:192], stacks[0:96, 2, :], ident[0:96, 0:96]))
            free[b] = t_aside["fcol"] = ve.after(lambda e: e.tensor_copy(fcol, ps[:, 0:192]), t)
            t_aside["pbs"] = po.do(lambda e: e.tensor_tensor(v_pb, v_pb, v_psc, ALU.mult), t_w5)
            t_aside["ffn"] = load(flag("f_ffn"), v_ffn, I["norm_ffn_g_2"][0, :].partition_broadcast(128), t_g2)
            for blk in range(1, NBLK):
                t_aside["idx"] = places(blk)

        srcs = {"w1": (w1, 8), "w3": (w3, 8), "w2": (w2, 4)}

        def weights(kind, job):
            w, c = srcs[kind]
            return w[job[0]].rearrange("(p c) n -> p c n", c=c)

        def load_main(kinds, job):
            return halves(*[weights(kind, job) for kind in kinds])

        t_ys = experts([(e, 0) for e in range(NE)], (pe, ve, ac, po), load_main, consumed,
                       ([flag(f"g{i}") for i in range(4)], [flag(f"y{i}") for i in range(4)]), free, (t_idx, t_xs, t_zero), aside)
        t_idx_all, t_fcol, t_ffn, t_pbs = (t_aside[k] for k in ("idx", "fcol", "ffn", "pbs"))
        po.wait((f_xs[0], f_xs[1]), t_zero)
        split = {id(l): len(l.ops) for l in (pe, ve, ac, po, sp)}

        o_pe, o_ve, o_ac, o_po, o_sp = (Lane(sem(n)) for n in ("o_pe", "o_ve", "o_ac", "o_po", "o_sp"))
        last_used = (pe.sem, pe.n)
        o_flag = [flag(f"o{i}") for i in range(3)]
        o_used = [None] * 3
        order = {"w1": 0, "w3": 1, "w2": 2}
        pend = []

        def load_more(kinds, job):
            got = []
            for kind in kinds:
                s = order[kind]
                src = weights(kind, job)
                dst = ring[:, s, :].rearrange("p (a b) -> p a b", b=src.shape[2])
                t = o_sp.dma(lambda e, dst=dst, src=src: e.dma_start(dst, src), o_flag[s], last_used, o_used[s])
                pend.append(s)
                got.append((dst, (t, t)))
            return got

        def done_more(t, first):
            o_used[pend.pop(0)] = t

        o_free = list(free)
        jobs = [(e, blk) for e in range(NE) for blk in range(1, NBLK)]
        t_more = experts(jobs, (o_pe, o_ve, o_ac, o_po), load_more, done_more,
                         ([flag(f"og{i}") for i in range(4)], [flag(f"oy{i}") for i in range(4)]), o_free, (t_idx_all, *t_ys, last_used))
        o_po.wait(*t_more)
        for lane in (o_ve, o_ac, o_sp, o_pe):
            lane.wait((o_pe.sem, o_pe.n), (o_ve.sem, o_ve.n), (o_ac.sem, o_ac.n))
        for i in range(3):
            o_sp.wait((o_flag[i][0], o_flag[i][1]))

        po.wait(*t_ys)
        mark = small(1)
        t_join = po.do(lambda e: e.memset(mark, 0.0))
        YP = pool_[:, 0:4096].rearrange("p (q n c) -> p q n c", q=2, n=2)
        q0 = at_slot[0]
        rota[:] = [rota[(q0 + i) % (R + 3)] for i in range(R + 3)]
        rota[:] = [i for i in rota if i < R]
        at_slot[0] = 0
        after_ring = last_read[R:]
        w_f = I["ffn_w_in_2"][0].rearrange("(c p) (a n) -> p c a n", p=128, a=2)
        w_o = I["ffn_w_out_2"][0].rearrange("(c p) n -> p c n", p=128)
        ac.wait(*after_ring)
        room_a.close()
        AH, AL = (sb(k, [128, 22, 256], F32R) for k in ("act_h", "act_l"))
        WH, WL = (sb(k, [128, 2, 2048], F32R) for k in ("w_h", "w_l"))
        HH, HL = (sb(k, [128, 8, 256], F32R) for k in ("h_h", "h_l"))
        f_y = [flag("f_y0"), flag("f_y1")]
        t_y, t_m2, t_hm = [None] * 2, [None] * 2, [None] * 2
        for n in range(2):
            for q in range(2):
                r0 = 512 * q + 256 * n
                t_y[n] = ac.dma(lambda e, q=q, n=n, r0=r0: e.dma_start(
                    YP[:, q, n, :], ys[r0:r0 + 256, :].rearrange("(p h) c -> p (h c)", h=2)), f_y[n], t_join,
                    (pe.sem, pe.n), (ve.sem, ve.n))
        lateb, t_band = unit(I["late"].unsqueeze(1), 1536, 1536, t_y[1])
        band = lateb[:, 0, :].rearrange("p (g c) -> p g c", g=4)
        w_pool, t_wp = unit(I["pool_w_2"][0].rearrange("g (c p) d -> p (g c) d", p=128), 2048, 256, t_y[1])
        sv, sq_ = small(2), small(2)
        t_r = [None] * 2
        V = [YP[:, 0, n, :] for n in range(2)]

        t_sq2 = [None] * 2

        def add_first(n):
            y0 = YP[:, 0, n, :]
            ve.after(lambda e: e.scalar_tensor_tensor(X[:, n, :], y0, gate[:, 0, n:n + 1], X[:, n, :],
                                                      ALU.mult, ALU.add), t_y[n])

        def add_second(n):
            y1 = YP[:, 1, n, :]
            t = ve.after(lambda e: e.scalar_tensor_tensor(X[:, n, :], y1, gate[:, 1, n:n + 1], X[:, n, :],
                                                          ALU.mult, ALU.add))
            t2 = ve.after(lambda e: e.tensor_tensor(V[n], X[:, n, :], v_fin, ALU.mult), t_w5)
            t3 = ac.after(lambda e: e.activation(MX[:, n, :], X[:, n, :], ACT.Square, accum_out=ss[:, n:n + 1]), t)
            t_sq2[n] = ac.after(lambda e: e.activation(MX[:, n, :], V[n], ACT.Square, accum_out=sv[:, n:n + 1]), t2)
            return t3

        def norm_once(n, t):
            r1, q1, q2 = rr[:, n:n + 1], sq_[:, n:n + 1], sv[:, n:n + 1]
            rsqrt(r1, ss[:, n:n + 1], 1.0 / 1024, 1e-6, [q[:, 0:1] for q in tms[n]], t)
            ve.after(lambda e: e.tensor_tensor(q1, r1, r1, ALU.mult))
            return ve.after(lambda e: e.tensor_tensor(q2, q2, q1, ALU.mult), t_sq2[n])

        def norm_again(n, t):
            r1, q1, q2 = rr[:, n:n + 1], sq_[:, n:n + 1], sv[:, n:n + 1]
            rsqrt(q1, q2, 1.0 / 1024, 1e-6, [q[:, 4:5] for q in tms[n]], t)
            t = ve.after(lambda e: e.tensor_tensor(q1, q1, r1, ALU.mult))
            t_hm[n] = ac.do(lambda e: e.activation(MX[:, n, :], V[n], ACT.Copy, scale=q1), t)

        add_first(0)
        s0 = add_second(0)
        add_first(1)
        n0 = norm_once(0, s0)
        s1 = add_second(1)
        norm_again(0, n0)
        norm_again(1, norm_once(1, s1))
        for n in range(2):
            t_m2[n] = ve.after(lambda e, n=n: e.scalar_tensor_tensor(X[:, n, :], V[n], rr[:, n:n + 1], v_pb,
                                                                ALU.mult, ALU.add), t_pbs)

        t_w_used = [None] * 2
        raw = {}

        def part_of(h):
            if h < 22:
                if h % 2 == 0:
                    raw["w"] = unit_in(h // 2)
                w, t_w = raw["w"]
                return w[:, :, 128 * (h % 2):128 * (h % 2) + 128], t_w, h % 2 == 1
            k = h - 22
            if k % 2 == 0:
                nk = min(4, 22 - 2 * k)
                raw["w"] = unit(w_o[:, 2 * k:2 * k + nk, :], 1024 * nk, 1024)
                raw["s"] = held.pop()
            w, t_w = raw["w"]
            o = 2 * (k % 2)
            return w[:, o:o + 2, :], t_w, k % 2 == 1 or k == 10

        def unit_in(u):
            s = rota[at_slot[0] % len(rota)]
            at_slot[0] += 1
            raw["s"] = s
            dst = slots[s].rearrange("p (c a n) -> p c a n", c=8, a=2)
            for a in range(2):
                t = sp.dma(lambda e, a=a: e.dma_start(dst[:, :, a, :], w_f[:, :, a, 256 * u:256 * u + 256]),
                           slot_flag[s], last_read[s], t_y[1])
            return slots[s].rearrange("p (c n) -> p c n", c=16), t

        def high(h):
            src, t_w, last = part_of(h)
            dst = WH[:, h % 2, :].rearrange("p (c n) -> p c n", n=src.shape[2])
            t = ac.do(lambda e: e.copy(dst, src), t_w, t_y[1], t_w_used[h % 2])
            low = WL[:, h % 2, :].rearrange("p (c n) -> p c n", n=src.shape[2])
            return src, dst, low, t, last, raw["s"]

        t_cv = {}

        def lower(h, src, dst, low, t, last, slot, lane=ve):
            t_cv[h] = lane.do(lambda e: e.tensor_tensor(low, src, dst.bitcast(F32), ALU.subtract), t)
            if last:
                last_read[slot] = t_cv[h]

        lower(0, *high(0), lane=po)

        t_d = []
        banks = [bank() for _ in range(8)]
        for c, (b, ps, fr) in enumerate(banks):
            g = c // 2
            cc = slice(c * 128, (c + 1) * 128)
            pe.do(lambda e, ps=ps, cc=cc, g=g: e.matmul(ps[:, 0:128], MX[:, 0, cc], band[:, g, 0:128],
                                     start=True, stop=True), t_hm[0], fr, t_band, inc=False)
            pe.do(lambda e, ps=ps, cc=cc, g=g: e.matmul(ps[:, 128:256], MX[:, 0, cc], band[:, g, 128:256],
                                     start=True, stop=False), inc=False)
        for c, (b, ps, fr) in enumerate(banks):
            g = c // 2
            cc = slice(c * 128, (c + 1) * 128)
            t = pe.do(lambda e, ps=ps, cc=cc, g=g: e.matmul(ps[:, 128:256], MX[:, 1, cc], band[:, g, 256:384],
                                         start=False, stop=True), t_hm[1])
            s = fcol[:, 176 + c:177 + c]
            if c % 2:
                free[b] = ac.do(lambda e, ps=ps, s=s, c=c: e.activation(hT[:, c, :], ps[:, 0:256], ACT.Copy, scale=s), t)
            else:
                free[b] = ve.do(lambda e, s=s, ps=ps, c=c: e.tensor_scalar(hT[:, c, :], ps[:, 0:256], s, None, ALU.mult), t)
            t_d.append(free[b])
        consumed(t)
        second_high = high(1)
        t_x3, t_n3, t_band_used = [None] * 2, [None] * 2, (pe.sem, pe.n)

        def norm3(n):
            row_norm(n, X[:, n, :], MX[:, n, :], t_x3[n], t_band_used)
            t_n3[n] = ve.after(lambda e: e.scalar_tensor_tensor(MX[:, n, :], X[:, n, :], rr[:, n:n + 1], v_ffn,
                                                                ALU.mult, ALU.mult), t_ffn)

        for n in range(2):
            for gg in range(2):
                b, ps, fr = bank()
                for g in (2 * gg, 2 * gg + 1):
                    o = 256 * (g % 2)
                    for c in range(2):
                        t = pe.do(lambda e, ps=ps, c=c, o=o, g=g, n=n: e.matmul(
                            ps[:, o:o + 256], hT[:, 2 * g + c, n * 128:(n + 1) * 128], w_pool[:, 2 * g + c, :],
                            start=(c == 0), stop=(c == 1)), fr, t_wp, t_d[2 * g], t_d[2 * g + 1])
                gs = slice(512 * gg, 512 * gg + 512)
                tmp = YP[:, 1, n, gs]
                free[b] = ve.do(lambda e, tmp=tmp, ps=ps, gs=gs: e.tensor_tensor(tmp, ps[:, :], v_psc[:, gs], ALU.mult), t, t_w5)
                t_x3[n] = ve.after(lambda e, tmp=tmp, n=n, gs=gs: e.tensor_tensor(X[:, n, gs], X[:, n, gs], tmp, ALU.add), t_m2[n])
        norm3(0)
        norm3(1)
        consumed(t)
        t_pool = t

        t_hT = []
        for n in range(2):
            for g in range(2):
                b, ps, fr = bank()
                for c in range(4):
                    m = 4 * g + c
                    t = pe.do(lambda e, ps=ps, n=n, c=c, m=m: e.transpose(ps[:, c * 128:(c + 1) * 128],
                                                    MX[:, n, m * 128:(m + 1) * 128], ident),
                              fr, t_n3[n], inc=(c == 3))
                to = [H[:, 4 * g:4 * g + 4, n * 128:(n + 1) * 128] for H in (HH, HL)]
                q = ps[:, :].rearrange("p (c t) -> p c t", c=4)
                t = ac.do(lambda e, q=q, to=to: e.copy(to[0], q), t, t_y[1], t_pool)
                free[b] = ve.do(lambda e, q=q, to=to: e.tensor_tensor(to[1], q, to[0].bitcast(F32), ALU.subtract), t)
                t_hT.append(free[b])
        lower(1, *second_high)
        TH = MX[:, :, :].rearrange("p n (a t) -> p (n a) t", t=256)
        t_tmp, t_act, st = [None] * 8, [None] * 22, {}

        def convolve(h):
            for a in range(2):
                ps, b, y, t, tap = st[h, a]
                for r in (1, 0):
                    o = 2 - r
                    t = ve.after(lambda e, y=y, ps=ps, tap=tap, r=r, o=o: e.scalar_tensor_tensor(
                        y[:, o:256], ps[:, 0:256 - o], tap[r], y[:, o:256], ALU.mult, ALU.add), t)
                free[b] = st[h, a, "t"] = t

        def gated(h):
            y0, y1 = st[h, 0][2], st[h, 1][2]
            t = ac.do(lambda e: e.activation(y1, y1, ACT.Silu), st[h, 1, "t"])
            st[h, "p"] = po.do(lambda e: e.tensor_tensor(y0, y0, y1, ALU.mult), t, st[h, 0, "t"])

        def act_high(h):
            y0 = st[h, 0][2]
            st[h, "h"] = ac.do(lambda e: e.copy(AH[:, h, :], y0), st[h, "p"])

        def act_low(h):
            y0 = st[h, 0][2]
            t_act[h] = ve.do(lambda e: e.tensor_tensor(AL[:, h, :], y0, AH[:, h, :].bitcast(F32), ALU.subtract),
                             st[h, "h"])
            t_tmp[2 * (h % 4)] = t_tmp[2 * (h % 4) + 1] = t_act[h]

        def three(ps, pairs, deps):
            for i, ((ah, al), (bh, bl), st_, sp_) in enumerate(pairs):
                pe.do(lambda e, ah=ah, bh=bh, st_=st_: e.matmul(ps, ah, bh, start=st_, stop=False), *deps, inc=False)
                pe.do(lambda e, ah=ah, bl=bl: e.matmul(ps, ah, bl, start=False, stop=False), inc=False)
                t = pe.do(lambda e, al=al, bh=bh, sp_=sp_: e.matmul(ps, al, bh, start=False, stop=sp_), inc=(i == len(pairs) - 1))
            return t

        for h in range(22):
            wh = WH[:, h % 2, :].rearrange("p (c a n) -> p c a n", c=8, a=2)
            wl = WL[:, h % 2, :].rearrange("p (c a n) -> p c a n", c=8, a=2)
            done = []
            for a in range(2):
                b, ps, fr = bank()
                t = three(ps[:, 0:256], [((wh[:, k, a, :], wl[:, k, a, :]), (HH[:, k, :], HL[:, k, :]), k == 0, k == 7)
                                         for k in range(8)], (t_cv[h], fr, *t_hT))
                done.append((b, ps, t))
            t_w_used[h % 2] = t
            nxt = high(h + 2)
            for a, (b, ps, t) in enumerate(done):
                m = h + 22 * a
                y = TH[:, 2 * (h % 4) + a, :]
                tap = [fcol[:, 44 * r + m:44 * r + m + 1] for r in range(4)]
                t = ac.do(lambda e, y=y, ps=ps, tap=tap: e.activation(y, ps[:, 0:256], ACT.Identity, scale=tap[2], bias=tap[3]),
                          t, t_fcol, t_tmp[2 * (h % 4) + a])
                st[h, a] = (ps, b, y, t, tap)
            if h:
                convolve(h - 1)
                gated(h - 1)
            lower(h + 2, *nxt)
            if h > 1:
                act_high(h - 2)
                act_low(h - 2)
        convolve(21)
        acc = [bank() for _ in range(4)]
        t_acc = [None] * 4
        for h in range(22, 33):
            wh = WH[:, h % 2, :].rearrange("p (c n) -> p c n", c=2)
            wl = WL[:, h % 2, :].rearrange("p (c n) -> p c n", c=2)
            turns = [(k, a) for k in range(2) for a in range(4)]
            for k, a in turns if h < 32 else sorted(turns, key=lambda ka: ka[1]):
                kk = 2 * (h - 22) + k
                b, ps, fr = acc[a]
                n, j = a // 2, a % 2
                tl, js = slice(n * 128, (n + 1) * 128), slice(512 * j, 512 * j + 512)
                t = three(ps[:, :], [((AH[:, kk, tl], AL[:, kk, tl]), (wh[:, k, js], wl[:, k, js]),
                                      kk == 0, kk == 21)], (t_cv[h], fr, t_act[kk]))
                t_acc[a] = t
            t_w_used[h % 2] = t
            if h + 2 < 33:
                lower(h + 2, *high(h + 2))
            if h == 22:
                gated(21)
                for i in (20, 21):
                    act_high(i)
                    act_low(i)
        f_o = flag("f_o")
        o_r = out.rearrange("b (n p) d -> p (b n) d", p=128)
        for a, (b, ps, fr) in enumerate(acc):
            n, j = a // 2, a % 2
            js = slice(512 * j, 512 * j + 512)
            tt = ve.after(lambda e, ps=ps, n=n, js=js: e.tensor_tensor(X[:, n, js], X[:, n, js], ps[:, :], ALU.add), t_acc[a])
            t_o = ac.dma(lambda e, n=n, js=js: e.dma_start(o_r[:, n, js], X[:, n, js]), f_o, tt)
        ac.wait(t_o)

        block = ctx.enter_context(nc.Block())

        def run(eng, lane, more):
            cut = split[id(lane)]
            whole = lane.ops
            seen = {}
            lane.ops = whole[:cut]
            lane.play(eng, seen)
            eng.wait_ge(t_flag[0], t_flag[1])
            val = eng.value_load(flag_i[0:1, 0:1], min_val=0, max_val=1)
            with eng.If(val > 0):
                more.play(eng, dict(seen))
            lane.ops = whole[cut:]
            lane.play(eng, seen)

        @block.sync
        def _(eng):
            run(eng, sp, o_sp)

        @block.tensor
        def _(eng):
            run(eng, pe, o_pe)

        @block.vector
        def _(eng):
            run(eng, ve, o_ve)

        @block.scalar
        def _(eng):
            run(eng, ac, o_ac)

        @block.gpsimd
        def _(eng):
            run(eng, po, o_po)


_INS = ['x', 'c', 'positions', 'w_ada', 'b_ada', 'norm1_w', 'w_in', 'conv_w', 'a_log', 'dt_bias', 'dn_norm_w',
        'w_out', 'norm2_w', 'w_group', 'b_group', 'w_expert', 'b_expert', 'w1', 'w3', 'w2', 'final_norm_w',
        'norm_mix_g_2', 'norm_ffn_g_2', 'pool_w_2', 'pool_b_2', 'pool_scale_2', 'ffn_w_in_2', 'ffn_conv_w_2',
        'ffn_conv_b_2', 'ffn_w_out_2']


def kernel(**inputs):
    import numpy as _np
    import concourse.bacc as _bacc
    from concourse import mybir as _mybir
    from concourse.bass_utils import run_bass_kernel_spmd as _run

    nc = _bacc.Bacc("TRN2", target_bir_lowering=False, num_devices=1)
    given = {k: _np.ascontiguousarray(inputs[k]) for k in _INS}
    given["consts"] = _np.concatenate(list(constants().values()), axis=1)
    given["late"] = late_constants()
    arrays, aps = {}, {}
    for name, a in given.items():
        arrays[f"in_{name}_dram"] = a
        aps[name] = nc.dram_tensor(f"in_{name}_dram", a.shape, _mybir.dt.from_np(a.dtype), kind="ExternalInput").ap()
    o = nc.dram_tensor("out_0_dram", (1, 256, 1024), F32, kind="ExternalOutput").ap()
    program(nc, aps, o)
    r = _run(nc, [arrays], core_ids=[0])
    return r.results[0]["out_0_dram"]
```
